# Optimizing a Trainium2 kernel written in Bass

```python
import jax, jax.numpy as jnp
from jax import lax
import numpy as np
import jax
import jax.numpy as jnp

D_MODEL = 1024
BATCH = 1
SEQ = 512
DEPTH = 1

HEAD_DIM = 64
MIX_WIDTH = D_MODEL
NSA_WIDTH = MIX_WIDTH // 2
DSA_WIDTH = MIX_WIDTH - NSA_WIDTH
NSA_HEADS = NSA_WIDTH // HEAD_DIM
NSA_KV_HEADS = 2
NSA_KV_W = NSA_KV_HEADS * HEAD_DIM
DSA_HEADS = DSA_WIDTH // HEAD_DIM
DSA_KV_HEADS = 2
DSA_KV_W = DSA_KV_HEADS * HEAD_DIM
IDX_HEADS = 4
IDX_DIM = 64
CMP_BLOCK = 32
CMP_STRIDE = 16
CMP_HIDDEN = 256
SEL_BLOCK = 64
SEL_TOPN = 16
WINDOW = 512
DSA_TOPK_MAX = 256
ROPE_THETA = 10000.0
EPS = 1e-6
Q_BLOCK = 128
SEL_Q_BLOCK = 64
NEG = -1e30
FORCE = 1e6
ATTN_SCALE = HEAD_DIM ** -0.5

IN_WIDTHS = (NSA_WIDTH, NSA_KV_W, NSA_KV_W, NSA_KV_W, NSA_KV_W, NSA_KV_W, NSA_KV_W,
             3 * NSA_HEADS, NSA_WIDTH,
             DSA_WIDTH, DSA_KV_W, DSA_KV_W, IDX_HEADS * IDX_DIM, IDX_DIM, IDX_HEADS, DSA_WIDTH)
IN_COLS = sum(IN_WIDTHS)


def rms_norm(x, gain):
    xf = x.astype(jnp.float32)
    y = xf * lax.rsqrt(jnp.mean(xf * xf, axis=-1, keepdims=True) + EPS)
    return (y * gain.astype(jnp.float32)).astype(x.dtype)

def rope(x, pos):
    half = x.shape[-1] // 2
    inv_freq = ROPE_THETA ** (-jnp.arange(half, dtype=jnp.float32) / half)
    ang = pos[:, None] * inv_freq[None, :]
    cos = jnp.cos(ang)[:, None, :]
    sin = jnp.sin(ang)[:, None, :]
    xf = x.astype(jnp.float32)
    x1, x2 = xf[..., :half], xf[..., half:]
    return jnp.concatenate([x1 * cos - x2 * sin, x2 * cos + x1 * sin], axis=-1).astype(x.dtype)

def masked_softmax(s, mask):
    s = jnp.where(mask, s.astype(jnp.float32), NEG)
    p = jax.nn.softmax(s, axis=-1)
    return jnp.where(mask, p, 0.0)

def split_columns(proj, widths):
    offsets = np.cumsum(np.array(widths))[:-1]
    return jnp.split(proj, [int(o) for o in offsets], axis=-1)

def compress(k_raw, pe, w1, b1, w2):
    B, S, G, Dh = k_raw.shape
    n_cmp = (S - CMP_BLOCK) // CMP_STRIDE + 1
    idx = jnp.arange(n_cmp)[:, None] * CMP_STRIDE + jnp.arange(CMP_BLOCK)[None, :]
    blocks = k_raw[:, idx] + pe[None, None, :, None, :]
    flat = blocks.transpose(0, 1, 3, 2, 4).reshape(B, n_cmp, G, CMP_BLOCK * Dh)
    hid = jax.nn.silu(flat @ w1 + b1)
    return hid @ w2

def compressed_branch(q, kc, vc):
    S = q.shape[1]
    n_cmp = kc.shape[1]
    cmp_end = jnp.arange(n_cmp) * CMP_STRIDE + CMP_BLOCK - 1
    t = jnp.arange(S)
    s = jnp.einsum('bsgrd,bcgd->bgrsc', q, kc) * ATTN_SCALE
    p = masked_softmax(s, cmp_end[None, :] <= t[:, None])
    o = jnp.einsum('bgrsc,bcgd->bsgrd', p.astype(vc.dtype), vc)
    return o, p

def selection_indices(p_cmp):
    S, n_cmp = p_cmp.shape[-2], p_cmp.shape[-1]
    n_sel = S // SEL_BLOCK
    c_start = jnp.arange(n_cmp) * CMP_STRIDE
    j = jnp.arange(n_sel)
    j_start = j * SEL_BLOCK
    overlap = jnp.clip(jnp.minimum(c_start[:, None] + CMP_BLOCK, j_start[None, :] + SEL_BLOCK)
                       - jnp.maximum(c_start[:, None], j_start[None, :]), 0, None)
    overlap = overlap.astype(jnp.float32) / CMP_BLOCK
    imp = jnp.einsum('bgrsc,cj->bgsj', p_cmp, overlap)
    t = jnp.arange(S)
    cur = t // SEL_BLOCK
    forced = (j[None, :] == 0) | (j[None, :] == cur[:, None]) | (j[None, :] == cur[:, None] - 1)
    imp = jnp.where(forced, FORCE, imp)
    imp = jnp.where(j_start[None, :] <= t[:, None], imp, NEG)
    _, idx = lax.top_k(imp, min(SEL_TOPN, n_sel))
    return idx.transpose(0, 2, 1, 3)

def selected_branch(q, ks, vs, sel_idx):
    B, S, G, R, Dh = q.shape
    n_sel = S // SEL_BLOCK
    n = sel_idx.shape[-1]
    k_blocks = ks.reshape(B, n_sel, SEL_BLOCK, G, Dh).transpose(0, 3, 1, 2, 4)
    v_blocks = vs.reshape(B, n_sel, SEL_BLOCK, G, Dh).transpose(0, 3, 1, 2, 4)
    b_ix = jnp.arange(B)[:, None, None, None]
    g_ix = jnp.arange(G)[None, None, :, None]

    def one_block(i):
        t0 = i * SEL_Q_BLOCK
        q_b = lax.dynamic_slice_in_dim(q, t0, SEL_Q_BLOCK, axis=1)
        idx_b = lax.dynamic_slice_in_dim(sel_idx, t0, SEL_Q_BLOCK, axis=1)
        k_sel = k_blocks[b_ix, g_ix, idx_b].reshape(B, SEL_Q_BLOCK, G, n * SEL_BLOCK, Dh)
        v_sel = v_blocks[b_ix, g_ix, idx_b].reshape(B, SEL_Q_BLOCK, G, n * SEL_BLOCK, Dh)
        kpos = (idx_b[..., None] * SEL_BLOCK + jnp.arange(SEL_BLOCK)).reshape(B, SEL_Q_BLOCK, G, n * SEL_BLOCK)
        t = t0 + jnp.arange(SEL_Q_BLOCK)
        mask = (kpos <= t[None, :, None, None])[:, :, :, None, :]
        s = jnp.einsum('btgrd,btgkd->btgrk', q_b, k_sel) * ATTN_SCALE
        p = masked_softmax(s, mask)
        return jnp.einsum('btgrk,btgkd->btgrd', p.astype(v_sel.dtype), v_sel)

    out = lax.map(one_block, jnp.arange(S // SEL_Q_BLOCK))
    return out.transpose(1, 0, 2, 3, 4, 5).reshape(B, S, G, R, Dh)

def window_branch(q, kw, vw):
    B, S, G, R, Dh = q.shape
    pad = ((0, 0), (WINDOW, 0), (0, 0), (0, 0))
    kp = jnp.pad(kw, pad)
    vp = jnp.pad(vw, pad)
    span = Q_BLOCK + WINDOW

    def one_block(i):
        t0 = i * Q_BLOCK
        q_b = lax.dynamic_slice_in_dim(q, t0, Q_BLOCK, axis=1)
        k_b = lax.dynamic_slice_in_dim(kp, t0, span, axis=1)
        v_b = lax.dynamic_slice_in_dim(vp, t0, span, axis=1)
        kpos = t0 - WINDOW + jnp.arange(span)
        t = t0 + jnp.arange(Q_BLOCK)
        diff = t[:, None] - kpos[None, :]
        mask = (diff >= 0) & (diff < WINDOW) & (kpos[None, :] >= 0)
        s = jnp.einsum('btgrd,bkgd->bgrtk', q_b, k_b) * ATTN_SCALE
        p = masked_softmax(s, mask)
        return jnp.einsum('bgrtk,bkgd->btgrd', p.astype(v_b.dtype), v_b)

    out = lax.map(one_block, jnp.arange(S // Q_BLOCK))
    return out.transpose(1, 0, 2, 3, 4, 5).reshape(B, S, G, R, Dh)

def dsa_branch(q, k, v, qi, ki, wi):
    B, S, G, R, Dh = q.shape
    topk = min(DSA_TOPK_MAX, S // 4)
    b_ix = jnp.arange(B)[:, None, None]
    key_pos = jnp.arange(S)
    wi = wi * (IDX_HEADS ** -0.5)

    def one_block(i):
        t0 = i * Q_BLOCK
        q_b = lax.dynamic_slice_in_dim(q, t0, Q_BLOCK, axis=1)
        qi_b = lax.dynamic_slice_in_dim(qi, t0, Q_BLOCK, axis=1)
        wi_b = lax.dynamic_slice_in_dim(wi, t0, Q_BLOCK, axis=1)
        t = t0 + jnp.arange(Q_BLOCK)
        logits = jnp.einsum('bthd,bsd->bths', qi_b, ki) * (IDX_DIM ** -0.5)
        score = jnp.einsum('bths,bth->bts', jax.nn.relu(logits), wi_b).astype(jnp.float32)
        score = jnp.where(key_pos[None, None, :] <= t[None, :, None], score, NEG)
        _, idx = lax.top_k(score, topk)
        k_sel = k[b_ix, idx]
        v_sel = v[b_ix, idx]
        mask = (idx <= t[None, :, None])[:, :, None, None, :]
        s = jnp.einsum('btgrd,btkgd->btgrk', q_b, k_sel) * ATTN_SCALE
        p = masked_softmax(s, mask)
        return jnp.einsum('btgrk,btkgd->btgrd', p.astype(v_sel.dtype), v_sel)

    out = lax.map(one_block, jnp.arange(S // Q_BLOCK))
    return out.transpose(1, 0, 2, 3, 4, 5).reshape(B, S, G, R, Dh)

def hybrid_layer(x, norm_gain, w_in, nsa_q_gain, nsa_kc_gain, nsa_ks_gain, nsa_kw_gain,
                 cmp_pe_k, cmp_k_w1, cmp_k_b1, cmp_k_w2, cmp_pe_v, cmp_v_w1, cmp_v_b1, cmp_v_w2,
                 dsa_q_gain, dsa_k_gain, w_out):
    B, S, _ = x.shape
    pos = jnp.arange(S, dtype=jnp.float32)
    h = rms_norm(x, norm_gain)
    proj = jnp.einsum('bsd,dc->bsc', h, w_in)
    (q_n, kc, vc, ks, vs, kw, vw, gate_logits, z_n,
     q_d, k_d, v_d, qi, ki, wi, z_d) = split_columns(proj, IN_WIDTHS)

    def heads(a, n):
        return a.reshape(B, S, n, HEAD_DIM)

    G, R = NSA_KV_HEADS, NSA_HEADS // NSA_KV_HEADS
    qn = rope(rms_norm(heads(q_n, NSA_HEADS), nsa_q_gain), pos).reshape(B, S, G, R, HEAD_DIM)
    kc_cmp = compress(heads(kc, G), cmp_pe_k, cmp_k_w1, cmp_k_b1, cmp_k_w2)
    vc_cmp = compress(heads(vc, G), cmp_pe_v, cmp_v_w1, cmp_v_b1, cmp_v_w2)
    cmp_pos = (jnp.arange(kc_cmp.shape[1]) * CMP_STRIDE + CMP_BLOCK - 1).astype(jnp.float32)
    kc_cmp = rope(rms_norm(kc_cmp, nsa_kc_gain), cmp_pos)
    o_cmp, p_cmp = compressed_branch(qn, kc_cmp, vc_cmp)
    sel_idx = selection_indices(p_cmp)
    ks_r = rope(rms_norm(heads(ks, G), nsa_ks_gain), pos)
    o_sel = selected_branch(qn, ks_r, heads(vs, G), sel_idx)
    kw_r = rope(rms_norm(heads(kw, G), nsa_kw_gain), pos)
    o_win = window_branch(qn, kw_r, heads(vw, G))
    g = jax.nn.sigmoid(gate_logits.astype(jnp.float32)).reshape(B, S, G, R, 3).astype(o_cmp.dtype)
    o_nsa = g[..., 0:1] * o_cmp + g[..., 1:2] * o_sel + g[..., 2:3] * o_win
    o_nsa = o_nsa.reshape(B, S, NSA_WIDTH) * jax.nn.silu(z_n)

    Gd, Rd = DSA_KV_HEADS, DSA_HEADS // DSA_KV_HEADS
    qd = rope(rms_norm(heads(q_d, DSA_HEADS), dsa_q_gain), pos).reshape(B, S, Gd, Rd, HEAD_DIM)
    kd = rope(rms_norm(heads(k_d, Gd), dsa_k_gain), pos)
    qi_r = rope(qi.reshape(B, S, IDX_HEADS, IDX_DIM), pos)
    ki_r = rope(ki.reshape(B, S, 1, IDX_DIM), pos).reshape(B, S, IDX_DIM)
    o_dsa = dsa_branch(qd, kd, heads(v_d, Gd), qi_r, ki_r, wi)
    o_dsa = o_dsa.reshape(B, S, DSA_WIDTH) * jax.nn.silu(z_d)

    mixed = jnp.concatenate([o_nsa, o_dsa], axis=-1)
    return x + jnp.einsum('bsc,cd->bsd', mixed, w_out)

def first_inputs(seed: int = 0) -> dict:
    key = jax.random.key(seed)
    k = jax.random.split(key, 18)
    L = DEPTH
    Dh = HEAD_DIM

    def nrm(kk, shape, scale):
        return jax.random.normal(kk, shape, jnp.float32) * scale

    def gain(kk, n):
        return 1.0 + 0.01 * jax.random.normal(kk, (L, n), jnp.float32)

    return {
        "x": nrm(k[0], (BATCH, SEQ, D_MODEL), 1.0),
        "norm_gain": gain(k[1], D_MODEL),
        "w_in": nrm(k[2], (L, D_MODEL, IN_COLS), D_MODEL ** -0.5),
        "nsa_q_gain": gain(k[3], Dh),
        "nsa_kc_gain": gain(k[4], Dh),
        "nsa_ks_gain": gain(k[5], Dh),
        "nsa_kw_gain": gain(k[6], Dh),
        "cmp_pe_k": nrm(k[7], (L, CMP_BLOCK, Dh), 0.1),
        "cmp_k_w1": nrm(k[8], (L, CMP_BLOCK * Dh, CMP_HIDDEN), (CMP_BLOCK * Dh) ** -0.5),
        "cmp_k_b1": nrm(k[9], (L, CMP_HIDDEN), 0.01),
        "cmp_k_w2": nrm(k[10], (L, CMP_HIDDEN, Dh), CMP_HIDDEN ** -0.5),
        "cmp_pe_v": nrm(k[11], (L, CMP_BLOCK, Dh), 0.1),
        "cmp_v_w1": nrm(k[12], (L, CMP_BLOCK * Dh, CMP_HIDDEN), (CMP_BLOCK * Dh) ** -0.5),
        "cmp_v_b1": nrm(k[13], (L, CMP_HIDDEN), 0.01),
        "cmp_v_w2": nrm(k[14], (L, CMP_HIDDEN, Dh), CMP_HIDDEN ** -0.5),
        "dsa_q_gain": gain(k[15], Dh),
        "dsa_k_gain": gain(k[16], Dh),
        "w_out": nrm(k[17], (L, MIX_WIDTH, D_MODEL), MIX_WIDTH ** -0.5),
    }

def first_block(x, norm_gain, w_in, nsa_q_gain, nsa_kc_gain, nsa_ks_gain, nsa_kw_gain,
              cmp_pe_k, cmp_k_w1, cmp_k_b1, cmp_k_w2, cmp_pe_v, cmp_v_w1, cmp_v_b1, cmp_v_w2,
              dsa_q_gain, dsa_k_gain, w_out):
    for l in range(DEPTH):
        x = hybrid_layer(x, norm_gain[l], w_in[l], nsa_q_gain[l], nsa_kc_gain[l], nsa_ks_gain[l],
                         nsa_kw_gain[l], cmp_pe_k[l], cmp_k_w1[l], cmp_k_b1[l], cmp_k_w2[l],
                         cmp_pe_v[l], cmp_v_w1[l], cmp_v_b1[l], cmp_v_w2[l],
                         dsa_q_gain[l], dsa_k_gain[l], w_out[l])
    return x


DEPTH_2 = 2

CTX_LEN = 256
GRID_W = 64
N_MOD = 9

GROUP_W = 256
MIX_W = 4 * GROUP_W

FNET_HEADS = 4
FNET_HD = GROUP_W // FNET_HEADS

MLA_HEADS = 4
QK_NOPE = 64
QK_ROPE = 32
AXIS_ROPE = QK_ROPE // 2
V_HD = 64
Q_RANK = 192
KV_RANK = 128
ROPE_BASE = 10000.0

SGU_HEADS = 4
SGU_HD = GROUP_W // SGU_HEADS
SGU_CHUNK = 128

POOL_WINDOWS = (2, 4, 8, 16)
POOL_GROUPS = len(POOL_WINDOWS)
POOL_HD = GROUP_W // POOL_GROUPS

D_FF = 2816

OFF_F = 0
OFF_Q = OFF_F + GROUP_W
OFF_KV = OFF_Q + Q_RANK
OFF_KR = OFF_KV + KV_RANK
OFF_G = OFF_KR + QK_ROPE
OFF_P = OFF_G + 2 * GROUP_W
IN_W = OFF_P + GROUP_W


def rms_norm_2(x, g):
    xf = x.astype(jnp.float32)
    y = xf * lax.rsqrt(jnp.mean(xf * xf, axis=-1, keepdims=True) + EPS)
    return (y * g.astype(jnp.float32)).astype(x.dtype)

def modulate(x, shift, scale):
    return x * (1 + scale) + shift

def swiglu(x, w13, w2):
    a, b = jnp.split(x @ w13, 2, axis=-1)
    return (jax.nn.silu(a) * b) @ w2

def ffn_half_step(h, g, shift, scale, gate, w13, w2):
    return h + 0.5 * gate * swiglu(modulate(rms_norm_2(h, g), shift, scale), w13, w2)

def axial_rope_tables(n_tokens):
    rows = n_tokens // GRID_W
    row = jnp.repeat(jnp.arange(rows, dtype=jnp.float32), GRID_W)
    col = (jnp.arange(n_tokens) % GRID_W).astype(jnp.float32)
    inv = jnp.power(ROPE_BASE, -jnp.arange(0, AXIS_ROPE, 2, dtype=jnp.float32) / AXIS_ROPE)
    ang = jnp.stack([row[:, None] * inv, col[:, None] * inv], axis=1)
    return jnp.cos(ang), jnp.sin(ang)

def apply_axial_rope(x, cos, sin):
    xs = x.reshape(x.shape[:-1] + (2, 2, AXIS_ROPE // 2)).astype(jnp.float32)
    x1, x2 = xs[..., 0, :], xs[..., 1, :]
    c = cos[None, :, None]
    s = sin[None, :, None]
    out = jnp.stack([x1 * c - x2 * s, x1 * s + x2 * c], axis=-2)
    return out.reshape(x.shape).astype(x.dtype)

def fourier_mixer(z, w_f):
    B, L, _ = z.shape
    zh = z.reshape(B, L, FNET_HEADS, FNET_HD).astype(jnp.float32)
    f = jnp.fft.fft2(zh, axes=(1, 3), norm="ortho").real.astype(z.dtype)
    return jnp.einsum('blhc,hcd->blhd', f, w_f).reshape(B, L, GROUP_W)

def mla_query(cq, g_q, w_uq, rope):
    B, L, _ = cq.shape
    q = (rms_norm_2(cq, g_q) @ w_uq).reshape(B, L, MLA_HEADS, QK_NOPE + QK_ROPE)
    if rope is not None:
        q = jnp.concatenate([q[..., :QK_NOPE], apply_axial_rope(q[..., QK_NOPE:], *rope)], axis=-1)
    return q

def mla_keys_values(ckv, kr, g_kv, w_ukv, rope):
    B, L, _ = ckv.shape
    kv = (rms_norm_2(ckv, g_kv) @ w_ukv).reshape(B, L, MLA_HEADS, QK_NOPE + V_HD)
    k_rope = kr[:, :, None, :]
    if rope is not None:
        k_rope = apply_axial_rope(k_rope, *rope)
    k = jnp.concatenate([kv[..., :QK_NOPE], jnp.broadcast_to(k_rope, (B, L, MLA_HEADS, QK_ROPE))], axis=-1)
    return k, kv[..., QK_NOPE:]

def attend(q, k, v):
    s = jnp.einsum('bqhd,bkhd->bhqk', q, k).astype(jnp.float32) * (QK_NOPE + QK_ROPE) ** -0.5
    p = jax.nn.softmax(s, axis=-1).astype(v.dtype)
    return jnp.einsum('bhqk,bkhd->bqhd', p, v)

def blocked_attention(q, k, v):
    B, L, H, dk = q.shape
    qb = q.reshape(B, L // Q_BLOCK, Q_BLOCK, H, dk).transpose(1, 0, 2, 3, 4)
    ob = lax.map(lambda qi: attend(qi, k, v), qb)
    return ob.transpose(1, 0, 2, 3, 4).reshape(B, L, H, v.shape[-1])

def spatial_gating_mixer(z, g_v, w_s, b_s):
    B, L, _ = z.shape
    z = jax.nn.gelu(z)
    u, v = jnp.split(z, 2, axis=-1)
    v = rms_norm_2(v.reshape(B, L, SGU_HEADS, SGU_HD), g_v)
    v = v.reshape(B, L // SGU_CHUNK, SGU_CHUNK, SGU_HEADS, SGU_HD)
    v = jnp.einsum('hpq,bnqhc->bnphc', w_s, v) + b_s.T[None, None, :, :, None]
    return u * v.reshape(B, L, GROUP_W)

def pooling_mixer(z, w_p, s_p):
    B, L, _ = z.shape
    zf = z.reshape(B, L, POOL_GROUPS, POOL_HD).astype(jnp.float32)
    cs = jnp.concatenate([jnp.zeros((B, 1, POOL_GROUPS, POOL_HD), jnp.float32), jnp.cumsum(zf, axis=1)], axis=1)
    t = jnp.arange(L)[:, None]
    w = jnp.array(POOL_WINDOWS, dtype=jnp.int32)[None, :]
    lo = jnp.clip(t - w // 2, 0, L)
    hi = jnp.clip(t - w // 2 + w, 0, L)
    gi = jnp.arange(POOL_GROUPS)[None, :]
    win_sum = cs[:, hi, gi] - cs[:, lo, gi]
    pooled = win_sum / (hi - lo).astype(jnp.float32)[None, :, :, None] - zf
    y = jnp.einsum('blgc,gcd->blgd', pooled.astype(z.dtype), w_p).reshape(B, L, GROUP_W)
    return y * s_p

def mix_heads(z, k, v, rope, w_fnet, g_q, w_uq, g_sgu, w_sgu, b_sgu, w_pool, s_pool):
    B, L, _ = z.shape
    q = mla_query(z[..., OFF_Q:OFF_KV], g_q, w_uq, rope)
    att = blocked_attention(q, k, v).reshape(B, L, GROUP_W)
    return jnp.concatenate([
        fourier_mixer(z[..., OFF_F:OFF_Q], w_fnet),
        att,
        spatial_gating_mixer(z[..., OFF_G:OFF_P], g_sgu, w_sgu, b_sgu),
        pooling_mixer(z[..., OFF_P:], w_pool, s_pool),
    ], axis=-1)

def second_inputs(seed: int = 0) -> dict:
    key = jax.random.key(seed)
    ks = iter(jax.random.split(key, 32))
    f32 = jnp.float32

    def nrm(shape, scale):
        return jax.random.normal(next(ks), shape, f32) * scale

    def gain(shape):
        return 1.0 + 0.1 * jax.random.normal(next(ks), shape, f32)

    n = DEPTH_2
    return {
        "x": nrm((BATCH, SEQ, D_MODEL), 1.0),
        "c": nrm((BATCH, D_MODEL), 1.0),
        "ctx": nrm((BATCH, CTX_LEN, D_MODEL), 1.0),
        "c_ctx": nrm((D_MODEL,), 1.0),
        "w_ada": nrm((n, D_MODEL, N_MOD * D_MODEL), 0.5 * D_MODEL ** -0.5),
        "b_ada": nrm((n, N_MOD * D_MODEL), 0.02),
        "g_ffn1": gain((n, D_MODEL)),
        "w13_ffn1": nrm((n, D_MODEL, 2 * D_FF), D_MODEL ** -0.5),
        "w2_ffn1": nrm((n, D_FF, D_MODEL), D_FF ** -0.5),
        "g_mix": gain((n, D_MODEL)),
        "w_in": nrm((n, D_MODEL, IN_W), D_MODEL ** -0.5),
        "w_fnet": nrm((n, FNET_HEADS, FNET_HD, FNET_HD), FNET_HD ** -0.5),
        "g_q": gain((n, Q_RANK)),
        "w_uq": nrm((n, Q_RANK, MLA_HEADS * (QK_NOPE + QK_ROPE)), Q_RANK ** -0.5),
        "g_kv": gain((n, KV_RANK)),
        "w_ukv": nrm((n, KV_RANK, MLA_HEADS * (QK_NOPE + V_HD)), KV_RANK ** -0.5),
        "g_sgu": gain((n, SGU_HEADS, SGU_HD)),
        "w_sgu": nrm((n, SGU_HEADS, SGU_CHUNK, SGU_CHUNK), SGU_CHUNK ** -0.5),
        "b_sgu": gain((n, SGU_HEADS, SGU_CHUNK)),
        "w_pool": nrm((n, POOL_GROUPS, POOL_HD, POOL_HD), POOL_HD ** -0.5),
        "s_pool": gain((n, GROUP_W)),
        "w_out": nrm((n, MIX_W, D_MODEL), MIX_W ** -0.5),
        "g_ffn2": gain((n, D_MODEL)),
        "w13_ffn2": nrm((n, D_MODEL, 2 * D_FF), D_MODEL ** -0.5),
        "w2_ffn2": nrm((n, D_FF, D_MODEL), D_FF ** -0.5),
        "g_final": gain((D_MODEL,)),
    }

def second_block(x, c, ctx, c_ctx, w_ada, b_ada, g_ffn1, w13_ffn1, w2_ffn1, g_mix, w_in, w_fnet,
              g_q, w_uq, g_kv, w_ukv, g_sgu, w_sgu, b_sgu, w_pool, s_pool, w_out,
              g_ffn2, w13_ffn2, w2_ffn2, g_final):
    B, L, _ = x.shape
    rope = axial_rope_tables(L)
    silu_c = jax.nn.silu(c)
    silu_cc = jax.nn.silu(c_ctx)[None]
    h, hc = x, ctx
    for i in range(DEPTH_2):
        last = i == DEPTH_2 - 1
        m = jnp.split((silu_c @ w_ada[i] + b_ada[i])[:, None, :], N_MOD, axis=-1)
        mc = jnp.split((silu_cc @ w_ada[i] + b_ada[i])[:, None, :], N_MOD, axis=-1)

        h = ffn_half_step(h, g_ffn1[i], m[0], m[1], m[2], w13_ffn1[i], w2_ffn1[i])
        hc = ffn_half_step(hc, g_ffn1[i], mc[0], mc[1], mc[2], w13_ffn1[i], w2_ffn1[i])

        n_lat = modulate(rms_norm_2(h, g_mix[i]), m[3], m[4])
        n_ctx = modulate(rms_norm_2(hc, g_mix[i]), mc[3], mc[4])
        z = n_lat @ w_in[i]
        zc = n_ctx @ (w_in[i][:, OFF_KV:OFF_G] if last else w_in[i])
        zc_kv = zc if last else zc[..., OFF_KV:OFF_G]
        kc, vc = mla_keys_values(zc_kv[..., :KV_RANK], zc_kv[..., KV_RANK:], g_kv[i], w_ukv[i], None)
        k, v = mla_keys_values(z[..., OFF_KV:OFF_KR], z[..., OFF_KR:OFF_G], g_kv[i], w_ukv[i], rope)
        mix_p = (w_fnet[i], g_q[i], w_uq[i], g_sgu[i], w_sgu[i], b_sgu[i], w_pool[i], s_pool[i])
        y = mix_heads(z, jnp.concatenate([k, kc], axis=1), jnp.concatenate([v, vc], axis=1), rope, *mix_p) @ w_out[i]
        h = h + m[5] * y

        h = ffn_half_step(h, g_ffn2[i], m[6], m[7], m[8], w13_ffn2[i], w2_ffn2[i])

        if not last:
            yc = mix_heads(zc, kc, vc, None, *mix_p) @ w_out[i]
            hc = hc + mc[5] * yc
            hc = ffn_half_step(hc, g_ffn2[i], mc[6], mc[7], mc[8], w13_ffn2[i], w2_ffn2[i])
    return rms_norm_2(h, g_final)


def setup_inputs(seed=0):
    out = dict(first_inputs(seed))
    for name, value in second_inputs(seed + 1).items():
        if name != "x":
            out[name + "_2"] = value
    return out


def reference(
    x, norm_gain, w_in, nsa_q_gain, nsa_kc_gain, nsa_ks_gain, nsa_kw_gain, cmp_pe_k, cmp_k_w1,
    cmp_k_b1, cmp_k_w2, cmp_pe_v, cmp_v_w1, cmp_v_b1, cmp_v_w2, dsa_q_gain, dsa_k_gain, w_out,
    c_2, ctx_2, c_ctx_2, w_ada_2, b_ada_2, g_ffn1_2, w13_ffn1_2, w2_ffn1_2, g_mix_2, w_in_2,
    w_fnet_2, g_q_2, w_uq_2, g_kv_2, w_ukv_2, g_sgu_2, w_sgu_2, b_sgu_2, w_pool_2, s_pool_2,
    w_out_2, g_ffn2_2, w13_ffn2_2, w2_ffn2_2, g_final_2,
):
    x = first_block(
        x, norm_gain, w_in, nsa_q_gain, nsa_kc_gain, nsa_ks_gain, nsa_kw_gain, cmp_pe_k,
        cmp_k_w1, cmp_k_b1, cmp_k_w2, cmp_pe_v, cmp_v_w1, cmp_v_b1, cmp_v_w2, dsa_q_gain,
        dsa_k_gain, w_out,
    )
    return second_block(
        x, c_2, ctx_2, c_ctx_2, w_ada_2, b_ada_2, g_ffn1_2, w13_ffn1_2, w2_ffn1_2, g_mix_2,
        w_in_2, w_fnet_2, g_q_2, w_uq_2, g_kv_2, w_ukv_2, g_sgu_2, w_sgu_2, b_sgu_2, w_pool_2,
        s_pool_2, w_out_2, g_ffn2_2, w13_ffn2_2, w2_ffn2_2, g_final_2,
    )


_drawn_inputs = setup_inputs


def setup_inputs(seed=0):
    import zlib

    import numpy as np

    out = dict(_drawn_inputs(seed))
    spreads = {}
    factors = {'norm_gain': 8.0,
     'nsa_q_gain': 8.0,
     'nsa_kc_gain': 30.849,
     'nsa_ks_gain': 8.0,
     'nsa_kw_gain': 8.0,
     'cmp_pe_k': 8.0,
     'cmp_k_b1': 29.246,
     'cmp_pe_v': 11.666,
     'cmp_v_b1': 64.0,
     'dsa_q_gain': 8.0,
     'dsa_k_gain': 8.0,
     'ctx_2': 200.0,
     'c_ctx_2': 66.968,
     'g_q_2': 200.0,
     'w_uq_2': 23.048,
     'g_kv_2': 200.0,
     'g_sgu_2': 200.0,
     'b_sgu_2': 200.0,
     's_pool_2': 175.488,
     'g_ffn2_2': 115.296,
     'b_ada_2': 5.333,
     'g_ffn1_2': 8.0,
     'w13_ffn1_2': 5.049,
     'w2_ffn1_2': 5.227,
     'g_mix_2': 19.602,
     'w_fnet_2': 64.0,
     'w_sgu_2': 3.789,
     'w_pool_2': 3.756,
     'w_ukv_2': 8.0}
    for name, (base, spread) in spreads.items():
        noise = np.random.default_rng([zlib.crc32(name.encode()), seed]).standard_normal(out[name].shape)
        drawn = base * np.exp(spread * noise) if base else spread * noise
        out[name] = jnp.asarray(drawn.astype(out[name].dtype))
    for name, factor in factors.items():
        out[name] = (out[name] * factor).astype(out[name].dtype)
    return out
```

```python
from contextlib import ExitStack, contextmanager
from itertools import count

import concourse.bass as bass
from concourse import mybir

P = 128
SERIAL = count()
F32 = mybir.dt.float32
F32R = mybir.dt.float32r
ALU = mybir.AluOpType
ACT = mybir.ActivationFunctionType
AX_X = mybir.AxisListType.X

D = 1024
KT = D // P
SEQ = 512
QT = SEQ // P
HD = 64
HEADS = 8
GROUPS = 2
PER_GROUP = HEADS // GROUPS
IDX_HEADS = 4
CMP_BLOCK, CMP_STRIDE, CMP_HIDDEN = 32, 16, 256
N_CMP = (SEQ - CMP_BLOCK) // CMP_STRIDE + 1
CMP_PAD = 32
TOPK = min(256, SEQ // 4)
WIDTHS = dict(q_n=512, kc=128, vc=128, ks=128, vs=128, kw=128, vw=128, gate=3 * HEADS, z_n=512,
              q_d=512, k_d=128, v_d=128, qi=IDX_HEADS * HD, ki=HD, wi=IDX_HEADS, z_d=512)
OFF, _at = {}, 0
for _name, _w in WIDTHS.items():
    OFF[_name] = _at
    _at += _w
IN_COLS = _at
ROTATED = [("q_n", 8), ("q_d", 8), ("ks", 2), ("kw", 2), ("k_d", 2), ("qi", 4), ("ki", 1)]
HEAD_AT, _at = {}, 0
for _name, _n in ROTATED:
    HEAD_AT[_name] = _at
    _at += _n
N_ROT = _at
N_NORMED = HEAD_AT["qi"]
SCALE = HD ** -0.5
EPS = 1e-6
NEG = -1e30
TAKEN = -3e38
TAKEN_LIMIT = -2e38

CTX = 256
TOK = SEQ + CTX
TT = TOK // P
N_MOD = 9
LAYERS = 2
FF = 2816
FT = FF // P
GW = 256
MH = 4
QK_NOPE, QK_ROPE, V_HD = 64, 32, 64
QKW = QK_NOPE + QK_ROPE
Q_RANK, KV_RANK = 192, 128
OFF_F = 0
OFF_Q = OFF_F + GW
OFF_KV = OFF_Q + Q_RANK
OFF_KR = OFF_KV + KV_RANK
OFF_G = OFF_KR + QK_ROPE
OFF_P = OFF_G + 2 * GW
IN_W = OFF_P + GW
SPANS = [(0, SEQ), (SEQ, TOK)]
ADA_STEPS = N_MOD * D // 256
ADA_N = 128

RING_W = 2048


class Tally:

    def __init__(self, sem, n=0):
        self.sem, self.n = sem, n


class Chain:

    def __init__(self, tally):
        self.t = tally
        self.eng = None

    def on(self, eng):
        self.eng = eng
        return self

    def mark(self, ins):
        ins.then_inc(self.t.sem, 1)
        self.t.n += 1
        return self.t.n

    def wait(self, n):
        self.eng.wait_ge(self.t.sem, n)

    def link(self, ins):
        self.wait(self.mark(ins))


class Core:

    def __init__(self, nc, ctx):
        self.nc, self.ctx = nc, ctx
        self.sems = {}

    def sb(self, name, shape, dt=F32):
        return self.ctx.enter_context(self.nc.sbuf_tensor(name, shape, dt))

    def tally(self, name):
        if name not in self.sems:
            self.sems[name] = Tally(self.ctx.enter_context(self.nc.semaphore(name)))
        return self.sems[name]


@contextmanager
def scope(nc):
    with ExitStack() as st:
        yield lambda name, shape, dt=F32: st.enter_context(nc.sbuf_tensor(f"{name}_{next(SERIAL)}", shape, dt))



class Ring:

    def __init__(self, c, sb):
        self.nc = c.nc
        self.raw = sb("w_raw", [P, 2, RING_W])
        self.hi = sb("w_hi", [P, 2, RING_W], F32R)
        self.lo = sb("w_lo", [P, 2, RING_W], F32R)
        self.loaded = [c.tally("w_loaded0").sem, c.tally("w_loaded1").sem]
        self.rounded = c.tally("w_rounded").sem
        self.split = c.tally("w_split").sem
        self.used = c.tally("w_used").sem
        self.drained = c.tally("psum_drained").sem
        self.c = c
        self.ahead = False

    def load_ahead(self, sp, s, after):
        for i in range(2):
            self.load(sp, s + i, (s + i) // 2, (s + i) % 2, after(s + i, i))

    def load(self, sp, s, half, slot, parts):
        sp.wait_ge(self.split, s + 1)
        for dst, src in parts:
            sp.dma_start(dst, src).then_inc(self.loaded[slot], 16)

    def round(self, act, s, half, slot, n):
        act.wait_ge(self.loaded[slot], half * 32 + 32)
        act.wait_ge(self.used, s + 1)
        self.nc.scalar.activation(self.hi[:, slot, 0:n], self.raw[:, slot, 0:n], ACT.Copy).then_inc(self.rounded, 1)

    def rest(self, dve, s, half, slot, n):
        dve.wait_ge(self.rounded, s + 1)
        self.nc.vector.tensor_tensor(self.lo[:, slot, 0:n], self.raw[:, slot, 0:n],
                                     self.hi[:, slot, 0:n].bitcast(F32), ALU.subtract).then_inc(self.split, 1)

    def view(self, slot, pattern, n=RING_W, **kw):
        return tuple(t[:, slot, 0:n].rearrange(pattern, **kw) for t in (self.raw, self.hi, self.lo))


def products(nc, out, pairs, width):
    n = len(pairs)
    for i, ((whi, wlo), (xhi, xlo)) in enumerate(pairs):
        nc.tensor.matmul(out, whi, xhi, start=(i == 0), stop=False)
        nc.tensor.matmul(out, whi, xlo, start=False, stop=False)
        last = nc.tensor.matmul(out, wlo, xhi, start=False, stop=(i == n - 1))
    return last



def start(c, dram):
    nc = c.nc
    c.hT = c.sb("hT", [P, KT, TOK])
    c.ident = c.sb("ident", [P, P])
    c.ones = c.sb("ones", [P, P])
    c.ones1 = c.sb("ones1", [P, P])
    c.eps = c.sb("eps", [P, 1])
    c.mod = c.sb("mod", [P, LAYERS, 2, N_MOD * KT])
    c.PS = c.ctx.enter_context(nc.psum_tensor("PS", [P, 8, 512], F32))
    c.dve = Chain(c.tally("dve_step"))
    c.act = Chain(c.tally("act_step"))
    c.step = 0
    names = ["w_split", "w_used", "psum_drained"]
    const_in = c.tally("const_in")
    with nc.Block() as block:
        @block.sync
        def _(sp):
            sp.dma_start(c.ident[:], dram["identity"]).then_inc(const_in.sem, 16)
            sp.wait_ge(const_in.sem, 16)

        @block.vector
        def _(dve):
            nc.vector.memset(c.ones[:], 1.0 / D).then_inc(c.tally(names[0]).sem, 2)
            nc.vector.memset(c.ones1[:], 1.0).then_inc(c.tally(names[1]).sem, 2)
            nc.vector.memset(c.eps[:], EPS).then_inc(c.tally(names[2]).sem, 2)


def load_rows(c, src, n_tok, at, tag):
    nc = c.nc
    nt = n_tok // P
    rows_in, turned, moved = [c.tally(f"rows_in{i}") for i in range(2)], c.tally("rows_turned"), c.tally("rows_moved")
    t0, m0 = turned.n, moved.n
    r0 = [r.n for r in rows_in]
    with scope(nc) as sb:
        rows = sb("rows_" + tag, [P, 2, D])
        with nc.Block() as block:
            @block.sync
            def _(sp):
                for t in range(nt):
                    if t >= 2:
                        sp.wait_ge(turned.sem, t0 + 2 * (t - 1))
                    sp.dma_start(rows[:, t % 2, :], src[t * P:(t + 1) * P, :]).then_inc(rows_in[t % 2].sem, 16)

            @block.tensor
            def _(pe):
                for t in range(nt):
                    pe.wait_ge(rows_in[t % 2].sem, r0[t % 2] + 16 * (t // 2 + 1))
                    for half in range(2):
                        n = 2 * t + half
                        if n >= 2:
                            pe.wait_ge(moved.sem, m0 + n - 1)
                        for j in range(4):
                            last = nc.tensor.transpose(c.PS[:, n % 2, j * P:(j + 1) * P],
                                                       rows[:, t % 2, (4 * half + j) * P:(4 * half + j + 1) * P], c.ident[:])
                        last.then_inc(turned.sem, 1)

            @block.vector
            def _(dve):
                for n in range(2 * nt):
                    t, half = n // 2, n % 2
                    dve.wait_ge(turned.sem, t0 + n + 1)
                    nc.vector.tensor_copy(c.hT[:, 4 * half:4 * half + 4, at + t * P:at + (t + 1) * P],
                                          c.PS[:, n % 2, :].rearrange("p (j t) -> p j t", j=4)).then_inc(moved.sem, 1)
    turned.n += 2 * nt
    moved.n += 2 * nt
    for t in range(nt):
        rows_in[t % 2].n += 16


def norm(c, sb, spans, gains, shifts, tag):
    nc = c.nc
    n = spans[-1][1]
    hi, lo = sb(f"x_hi_{tag}", [P, KT, n], F32R), sb(f"x_lo_{tag}", [P, KT, n], F32R)
    squared, summed, rooted = c.tally("n_squared"), c.tally("n_summed"), c.tally("n_rooted")
    scaled, shifted, free = c.tally("n_scaled"), c.tally("n_shifted"), c.tally("n_free")
    q0, s0, r0, a0, h0, f0 = (t.n for t in (squared, summed, rooted, scaled, shifted, free))
    with scope(nc) as tmp:
        sq = tmp("sq_" + tag, [P, 2, n])
        inv = tmp("inv_" + tag, [P, n])
        normed = tmp("normed_" + tag, [P, 2, n])
        xf = tmp("xf_" + tag, [P, 2, n])
        with nc.Block() as block:
            @block.scalar
            def _(act):
                for k in range(KT):
                    if k >= 2:
                        act.wait_ge(summed.sem, s0 + k - 1)
                    nc.scalar.activation(sq[:, k % 2, :], c.hT[:, k, 0:n], ACT.Square).then_inc(squared.sem, 1)
                act.wait_ge(summed.sem, s0 + KT)
                for a, b in spans:
                    last = nc.scalar.activation(inv[:, a:b], c.PS[:, a // 512, 0:b - a], ACT.Sqrt, bias=c.eps[:])
                    last.then_inc(rooted.sem, 1)
                for k in range(KT):
                    act.wait_ge(scaled.sem, a0 + k + 1)
                    if k >= 2:
                        act.wait_ge(free.sem, f0 + k - 1)
                    for (a, b), g, s in zip(spans, gains, shifts):
                        bias = 0.0 if s is None else s[:, k:k + 1]
                        nc.scalar.activation(xf[:, k % 2, a:b], normed[:, k % 2, a:b], ACT.Identity,
                                             bias=bias, scale=g[:, k:k + 1]).then_inc(shifted.sem, 1)

            @block.tensor
            def _(pe):
                for k in range(KT):
                    pe.wait_ge(squared.sem, q0 + k + 1)
                    for a, b in spans:
                        last = nc.tensor.matmul(c.PS[:, a // 512, 0:b - a], c.ones[:], sq[:, k % 2, a:b],
                                                start=(k == 0), stop=(k == KT - 1))
                    last.then_inc(summed.sem, 1)

            @block.vector
            def _(dve):
                ch = c.dve.on(dve)
                dve.wait_ge(rooted.sem, r0 + len(spans))
                ch.link(nc.vector.reciprocal(inv[:], inv[:]))

                def split(k):
                    dve.wait_ge(shifted.sem, h0 + (k + 1) * len(spans))
                    ch.link(nc.vector.tensor_copy(hi[:, k, :], xf[:, k % 2, :]))
                    nc.vector.tensor_tensor(lo[:, k, :], xf[:, k % 2, :], hi[:, k, :].bitcast(F32),
                                            ALU.subtract).then_inc(free.sem, 1)

                for k in range(KT):
                    if k >= 2:
                        dve.wait_ge(shifted.sem, h0 + (k - 1) * len(spans))
                    nc.vector.tensor_tensor(normed[:, k % 2, :], c.hT[:, k, 0:n], inv[:], ALU.mult).then_inc(scaled.sem, 1)
                    if k >= 1:
                        split(k - 1)
                split(KT - 1)
    squared.n += KT
    summed.n += KT
    rooted.n += len(spans)
    scaled.n += KT
    shifted.n += KT * len(spans)
    free.n += KT
    return hi, lo


def rows_step(ring, w, col0, n_cols):
    def parts(s, i):
        a = 256 * (i % -(-n_cols // 256))
        m = min(256, n_cols - a)
        raw = ring.view(s % 2, "p (k n) -> p k n", k=KT)[0]
        src = w.rearrange("(k p) n -> p k n", p=P)
        return [(raw[:, k:k + 4, 0:m], src[:, k:k + 4, col0 + a:col0 + a + m]) for k in (0, 4)]
    return parts


def cols_step(ring, w, tiles):
    steps = [tiles[i:i + 2] for i in range(0, len(tiles), 2)]

    def parts(s, i):
        raw = ring.raw[:, s % 2, :].rearrange("p (j k n) -> p j k n", j=2, k=KT)
        out = []
        for j in range(2):
            half = slice(None) if len(steps[i]) == 2 else slice(4 * j, 4 * j + 4)
            t = steps[i][j % len(steps[i])]
            src = (t[2] if len(t) > 2 else w).rearrange("(k p) n -> p k n", p=P)
            out.append((raw[:, j % len(steps[i]), half, 0:t[1]], src[:, half, t[0]:t[0] + t[1]]))
        return out
    return parts


def project_rows(c, ring, x, w, col0, n_cols, tiles, out, after=None, beside=None):
    nc = c.nc
    hi, lo = x
    parts = rows_step(ring, w, col0, n_cols)
    done = 2 if ring.ahead else 0
    chunks = [(a, min(256, n_cols - a)) for a in range(0, n_cols, 256)]
    steps = []
    for t0 in range(0, len(tiles), 4):
        for a, m in chunks:
            steps.append((tiles[t0:t0 + 4], t0, a, m))
    s0 = c.step

    def bank(s, j):
        return c.PS[:, 4 * (s % 2) + j // 2, (j % 2) * 256:(j % 2) * 256 + 256]

    with nc.Block() as block:
        @block.sync
        def _(sp):
            for i in range(done, len(steps)):
                ring.load(sp, s0 + i, (s0 + i) // 2, (s0 + i) % 2, parts(s0 + i, i))
            if after:
                ring.load_ahead(sp, s0 + len(steps), after)

        @block.scalar
        def _(act):
            for i in range(done // 2, len(steps)):
                s = s0 + i
                m = steps[i][3]
                act.wait_ge(ring.loaded[s % 2], (s // 2) * 32 + 32)
                act.wait_ge(ring.used, s + 1)
                raw, hi_, lo_ = ring.view(s % 2, "p (k n) -> p k n", k=KT)
                nc.scalar.activation(hi_[:, :, 0:m], raw[:, :, 0:m], ACT.Copy).then_inc(ring.rounded, 1)
            if after:
                s = s0 + len(steps)
                ring.round(act, s, s // 2, s % 2, RING_W)

        @block.vector
        def _(dve):
            ch = c.dve.on(dve)

            def evac(i):
                ts, t0, a, m = steps[i]
                s = s0 + i
                dve.wait_ge(ring.used, s + 3)
                for j in range(len(ts)):
                    last = nc.vector.tensor_copy(out[:, t0 + j, a:a + m], bank(s, j)[:, 0:m])
                last.then_inc(ring.drained, 1)

            for i in range(len(steps)):
                s = s0 + i
                m = steps[i][3]
                raw, hi_, lo_ = ring.view(s % 2, "p (k n) -> p k n", k=KT)
                if i >= done // 2:
                    dve.wait_ge(ring.rounded, s + 1)
                    nc.vector.tensor_tensor(lo_[:, :, 0:m], raw[:, :, 0:m], hi_[:, :, 0:m].bitcast(F32),
                                            ALU.subtract).then_inc(ring.split, 1)
                if beside:
                    beside(ch, i)
                if i >= 1:
                    evac(i - 1)
            if after:
                s = s0 + len(steps)
                ring.rest(dve, s, s // 2, s % 2, RING_W)
            evac(len(steps) - 1)

        @block.tensor
        def _(pe):
            for i, (ts, t0, a, m) in enumerate(steps):
                s = s0 + i
                _, whi, wlo = ring.view(s % 2, "p (k n) -> p k n", k=KT)
                pe.wait_ge(ring.split, s + 3)
                pe.wait_ge(ring.drained, s + 1)
                for j, t in enumerate(ts):
                    tok = slice(t * P, (t + 1) * P)
                    last = products(nc, bank(s, j)[:, 0:m],
                                    [((hi[:, k, tok], lo[:, k, tok]), (whi[:, k, 0:m], wlo[:, k, 0:m]))
                                     for k in range(KT)], m)
                last.then_inc(ring.used, 1)
    c.step += len(steps)
    ring.ahead = after is not None


def rotate(c, P1, QKT, dram):
    nc = c.nc
    names = ["gain_rows", "cos", "sin"]
    tab_in = c.tally("tables_in")
    sq_done, rooted, raw_copied = c.tally("r_squared"), c.tally("r_rooted"), c.tally("r_raw_copied")
    summed, normed, crossed, rotated = c.tally("r_summed"), c.tally("r_normed"), c.tally("r_crossed"), c.tally("r_rotated")
    turned, moved = c.tally("r_turned"), c.tally("r_moved")
    all_t = [tab_in, sq_done, rooted, raw_copied, summed, normed, crossed, rotated, turned, moved]
    b = {t: t.n for t in all_t}
    n_bank = (N_ROT + 3) // 4
    segs = [(OFF[name], HEAD_AT[name], n) for name, n in ROTATED if name not in ("qi", "ki")]
    with scope(nc) as sb:
        gain = sb("rot_gain", [P, N_NORMED, HD])
        cos, sin = sb("rot_cos", [P, QT, HD]), sb("rot_sin", [P, QT, HD])
        sq = sb("rot_sq", [P, N_NORMED, HD])
        X = sb("rot_x", [P, 2, N_ROT, HD])
        A, B = sb("rot_a", [P, N_ROT, HD]), sb("rot_b", [P, N_ROT, HD])
        R = sb("rot_r", [P, 2, N_ROT, HD])
        ss, rt, inv = (sb("rot_" + x, [P, N_NORMED]) for x in ("ss", "rt", "inv"))
        with nc.Block() as block:
            @block.sync
            def _(sp):
                sp.dma_start(gain[:], dram["gain_rows"]).then_inc(tab_in.sem, 16)
                sp.dma_start(cos[:], dram["cos"]).then_inc(tab_in.sem, 16)
                sp.dma_start(sin[:], dram["sin"]).then_inc(tab_in.sem, 16)

            @block.scalar
            def _(act):
                def evac(n):
                    t, j = n // n_bank, n % n_bank
                    m = min(4, N_ROT - 4 * j)
                    act.wait_ge(turned.sem, b[turned] + n + 1)
                    nc.scalar.activation(QKT[:, 4 * j:4 * j + m, t * P:(t + 1) * P],
                                         c.PS[0:HD, n % 4, 0:m * P].rearrange("p (h t) -> p h t", h=m),
                                         ACT.Copy).then_inc(moved.sem, 1)

                def first(t):
                    if t >= 1:
                        act.wait_ge(summed.sem, b[summed] + t)
                    for col, h, n in segs:
                        last = nc.scalar.activation(sq[:, h:h + n, :],
                                                    P1[:, t, col:col + n * HD].rearrange("p (h d) -> p h d", h=n), ACT.Square)
                    last.then_inc(sq_done.sem, 1)
                    if t >= 2:
                        act.wait_ge(rotated.sem, b[rotated] + t - 1)
                    nc.scalar.activation(X[:, t % 2, N_NORMED:N_ROT, :],
                                         P1[:, t, OFF["qi"]:OFF["qi"] + 5 * HD].rearrange("p (h d) -> p h d", h=5),
                                         ACT.Copy).then_inc(raw_copied.sem, 1)
                    act.wait_ge(summed.sem, b[summed] + t + 1)
                    nc.scalar.activation(rt[:], ss[:], ACT.Sqrt, bias=c.eps[:], scale=1.0 / HD).then_inc(rooted.sem, 1)

                first(0)
                for t in range(QT):
                    if t + 1 < QT:
                        first(t + 1)
                    for j in range(n_bank):
                        evac(t * n_bank + j)

            @block.gpsimd
            def _(pool):
                pool.wait_ge(tab_in.sem, b[tab_in] + 48)
                for t in range(QT):
                    pool.wait_ge(normed.sem, b[normed] + t + 1)
                    pool.wait_ge(raw_copied.sem, b[raw_copied] + t + 1)
                    if t >= 1:
                        pool.wait_ge(rotated.sem, b[rotated] + t)
                    x = X[:, t % 2].rearrange("p h (a d) -> p h a d", a=2)
                    s = sin[:, t, :].rearrange("p (a d) -> p a d", a=2)
                    bb = B[:].rearrange("p h (a d) -> p h a d", a=2)
                    for a in range(2):
                        last = nc.gpsimd.tensor_tensor(bb[:, :, a, :], x[:, :, 1 - a, :],
                                                       s[:, None, a, :].to_broadcast([P, N_ROT, HD // 2]), ALU.mult)
                    last.then_inc(crossed.sem, 1)

            @block.vector
            def _(dve):
                ch = c.dve.on(dve)
                dve.wait_ge(tab_in.sem, b[tab_in] + 48)
                for t in range(QT):
                    dve.wait_ge(sq_done.sem, b[sq_done] + t + 1)
                    if t >= 1:
                        dve.wait_ge(rooted.sem, b[rooted] + t)
                    nc.vector.reduce_sum(ss[:], sq[:], AX_X).then_inc(summed.sem, 1)
                    dve.wait_ge(rooted.sem, b[rooted] + t + 1)
                    ch.link(nc.vector.reciprocal(inv[:], rt[:]))
                    if t >= 2:
                        dve.wait_ge(rotated.sem, b[rotated] + t - 1)
                    for col, h, n in segs:
                        last = nc.vector.tensor_tensor(X[:, t % 2, h:h + n, :],
                                                       P1[:, t, col:col + n * HD].rearrange("p (h d) -> p h d", h=n),
                                                       inv[:, h:h + n, None].to_broadcast([P, n, HD]), ALU.mult)
                    ch.link(last)
                    nc.vector.tensor_tensor(X[:, t % 2, 0:N_NORMED, :], X[:, t % 2, 0:N_NORMED, :], gain[:],
                                            ALU.mult).then_inc(normed.sem, 1)
                    dve.wait_ge(normed.sem, b[normed] + t + 1)
                    dve.wait_ge(raw_copied.sem, b[raw_copied] + t + 1)
                    ch.link(nc.vector.tensor_tensor(A[:], X[:, t % 2], cos[:, t, None, :].to_broadcast([P, N_ROT, HD]), ALU.mult))
                    dve.wait_ge(crossed.sem, b[crossed] + t + 1)
                    if t >= 2:
                        dve.wait_ge(turned.sem, b[turned] + (t - 1) * n_bank)
                    nc.vector.tensor_tensor(R[:, t % 2], A[:], B[:], ALU.add).then_inc(rotated.sem, 1)
                    dve.wait_ge(rotated.sem, b[rotated] + t + 1)

            @block.tensor
            def _(pe):
                for t in range(QT):
                    pe.wait_ge(rotated.sem, b[rotated] + t + 1)
                    for j in range(n_bank):
                        n = t * n_bank + j
                        if n >= 4:
                            pe.wait_ge(moved.sem, b[moved] + n - 3)
                        for h in range(4 * j, min(4 * j + 4, N_ROT)):
                            last = nc.tensor.transpose(c.PS[0:HD, n % 4, (h % 4) * P:(h % 4 + 1) * P], R[:, t % 2, h, :], c.ident[:])
                        last.then_inc(turned.sem, 1)
    for t, d in ((tab_in, 48), (sq_done, QT), (rooted, QT), (raw_copied, QT), (summed, QT), (normed, QT), (crossed, QT),
                 (rotated, QT), (turned, QT * n_bank), (moved, QT * n_bank)):
        t.n += d


def compress(c, P1, kcmpT, vbd, dram):
    nc = c.nc
    w_in, small_in = c.tally("cmp_w_in"), c.tally("cmp_small_in")
    turned, moved, shifted, added = c.tally("cmp_turned"), c.tally("cmp_moved"), c.tally("cmp_shifted"), c.tally("cmp_added")
    hid_done, silu_done, rep_done, out_done = c.tally("cmp_hid"), c.tally("cmp_silu"), c.tally("cmp_repeated"), c.tally("cmp_out")
    rooted, summed, normed, kturned, kmoved = (c.tally("cmp_" + x) for x in ("rooted", "summed", "normed", "kturned", "kmoved"))
    all_t = [w_in, small_in, turned, moved, shifted, added, hid_done, silu_done, rep_done, out_done, rooted, summed, normed,
             kturned, kmoved]
    NJ = CMP_BLOCK // 2
    HT = CMP_HIDDEN // P
    with scope(nc) as sb:
        w1 = sb("cmp_w1", [P, 2, NJ, CMP_HIDDEN])
        w2 = sb("cmp_w2", [P, 2, HT, HD])
        b1 = sb("cmp_b1", [P, 2, HT])
        pe_t = sb("cmp_pe", [P, 2, NJ])
        gain = sb("cmp_gain", [CMP_PAD, HD])
        cos, sin = sb("cmp_cos", [CMP_PAD, HD]), sb("cmp_sin", [CMP_PAD, HD])
        T = sb("cmp_t", [P, 2, SEQ])
        S = sb("cmp_s", [P, 2, GROUPS, SEQ])
        G = sb("cmp_g", [P, 2, NJ, GROUPS, CMP_PAD])
        hid = sb("cmp_hid_sb", [P, 2, HT, GROUPS, CMP_PAD])
        rep = sb("cmp_rep", [P, HT, GROUPS, PER_GROUP, CMP_PAD])
        kraw, sq, A, B, R = (sb("cmp_" + x, [CMP_PAD, GROUPS, HD]) for x in ("kraw", "sq", "a", "b", "r"))
        ss, rt, inv = (sb("cmp_" + x, [CMP_PAD, GROUPS]) for x in ("ss", "rt", "inv"))
        with nc.Block() as block:
            @block.sync
            def _(sp):
                for i, x in enumerate("kv"):
                    sp.dma_start(w1[:, i], dram[f"cmp_{x}_w1"].rearrange("(j p) n -> p j n", p=P)).then_inc(w_in.sem, 16)
                    sp.dma_start(w2[:, i], dram[f"cmp_{x}_w2"].rearrange("(j p) n -> p j n", p=P)).then_inc(w_in.sem, 16)
                    sp.dma_start(b1[:, i], dram[f"cmp_{x}_b1"]).then_inc(small_in.sem, 16)
                    sp.dma_start(pe_t[:, i], dram[f"cmp_pe_{x}"]).then_inc(small_in.sem, 16)
                sp.dma_start(gain[:], dram["kc_gain"]).then_inc(small_in.sem, 16)
                sp.dma_start(cos[:], dram["cmp_cos"]).then_inc(small_in.sem, 16)
                sp.dma_start(sin[:], dram["cmp_sin"]).then_inc(small_in.sem, 16)
                sp.wait_ge(moved.sem, 2)
                for i in range(2):
                    for g in range(GROUPS):
                        for par in range(2):
                            sp.dma_start(S[par * HD:(par + 1) * HD, i, g, 0:SEQ - par],
                                         T[g * HD:(g + 1) * HD, i, par:SEQ]).then_inc(shifted.sem, 16)

            @block.tensor
            def _(pe):
                for i, x in enumerate(("kc", "vc")):
                    for t in range(QT):
                        last = nc.tensor.transpose(c.PS[:, i, t * P:(t + 1) * P], P1[:, t, OFF[x]:OFF[x] + P], c.ident[:])
                    last.then_inc(turned.sem, 1)
                pe.wait_ge(added.sem, 5)
                pe.wait_ge(w_in.sem, 64)
                for i in range(2):
                    for ht in range(HT):
                        for j in range(NJ):
                            last = nc.tensor.matmul(c.PS[:, 2 + i, ht * 64:ht * 64 + 64], w1[:, i, j, ht * P:(ht + 1) * P],
                                                    G[:, i, j].rearrange("p g c -> p (g c)"), start=(j == 0), stop=(j == NJ - 1))
                    last.then_inc(hid_done.sem, 1)
                pe.wait_ge(silu_done.sem, 4)
                for g in range(GROUPS):
                    for ht in range(HT):
                        last = nc.tensor.matmul(c.PS[0:CMP_PAD, 4, g * HD:(g + 1) * HD], hid[:, 0, ht, g, :], w2[:, 0, ht, :],
                                                start=(ht == 0), stop=(ht == HT - 1))
                last.then_inc(out_done.sem, 1)
                pe.wait_ge(rep_done.sem, 1)
                for g in range(GROUPS):
                    for ht in range(HT):
                        last = nc.tensor.matmul(c.PS[:, 5, g * HD:(g + 1) * HD], rep[:, ht, g].rearrange("p r c -> p (r c)"),
                                                w2[:, 1, ht, :], start=(ht == 0), stop=(ht == HT - 1))
                last.then_inc(out_done.sem, 1)
                pe.wait_ge(normed.sem, 1)
                for g in range(GROUPS):
                    last = nc.tensor.transpose(c.PS[0:HD, 6, g * CMP_PAD:(g + 1) * CMP_PAD], R[:, g, :], c.ident[0:CMP_PAD, 0:CMP_PAD])
                last.then_inc(kturned.sem, 1)

            @block.scalar
            def _(act):
                ch = c.act.on(act)
                act.wait_ge(small_in.sem, 16 * 7)
                for i in range(2):
                    act.wait_ge(hid_done.sem, i + 1)
                    for ht in range(HT):
                        nc.scalar.activation(hid[:, i, ht].rearrange("p g c -> p (g c)"), c.PS[:, 2 + i, ht * 64:ht * 64 + 64],
                                             ACT.Silu, bias=b1[:, i, ht:ht + 1]).then_inc(silu_done.sem, 1)
                act.wait_ge(out_done.sem, 1)
                ch.link(nc.scalar.activation(sq[:].rearrange("p g d -> p (g d)"), c.PS[0:CMP_PAD, 4, 0:GROUPS * HD], ACT.Square))
                nc.scalar.activation(kraw[:].rearrange("p g d -> p (g d)"), c.PS[0:CMP_PAD, 4, 0:GROUPS * HD],
                                     ACT.Copy).then_inc(silu_done.sem, 1)
                act.wait_ge(summed.sem, 1)
                nc.scalar.activation(rt[:], ss[:], ACT.Sqrt, bias=c.eps[0:CMP_PAD], scale=1.0 / HD).then_inc(rooted.sem, 1)

            @block.vector
            def _(dve):
                ch = c.dve.on(dve)
                nc.vector.memset(G[:], 0.0).then_inc(added.sem, 1)
                ch.link(nc.vector.memset(vbd[:], 0.0))
                for i in range(2):
                    dve.wait_ge(turned.sem, i + 1)
                    nc.vector.tensor_copy(T[:, i, :], c.PS[:, i, :]).then_inc(moved.sem, 1)
                dve.wait_ge(added.sem, 1)
                dve.wait_ge(small_in.sem, 16 * 7)
                dve.wait_ge(shifted.sem, 16 * 8)
                for i in range(2):
                    for g in range(GROUPS):
                        for part in range(2):
                            src = S[:, i, g, part * CMP_STRIDE:part * CMP_STRIDE + N_CMP * CMP_STRIDE].rearrange(
                                "p (c j two) -> p j c two", c=N_CMP, two=2)[:, :, :, 0]
                            js = slice(part * 8, part * 8 + 8)
                            last = nc.vector.tensor_tensor(G[:, i, js, g, 0:N_CMP], src,
                                                           pe_t[:, i, js, None].to_broadcast([P, 8, N_CMP]), ALU.add)
                        last.then_inc(added.sem, 1)
                dve.wait_ge(silu_done.sem, 4)
                for ht in range(HT):
                    last = nc.vector.tensor_copy(rep[:, ht], hid[:, 1, ht, :, None, :].to_broadcast([P, GROUPS, PER_GROUP, CMP_PAD]))
                last.then_inc(rep_done.sem, 1)
                dve.wait_ge(silu_done.sem, 5)
                nc.vector.reduce_sum(ss[:], sq[:], AX_X).then_inc(summed.sem, 1)
                dve.wait_ge(rooted.sem, 1)
                ch.link(nc.vector.reciprocal(inv[:], rt[:]))
                ch.link(nc.vector.tensor_tensor(kraw[:], kraw[:], inv[:, :, None].to_broadcast([CMP_PAD, GROUPS, HD]), ALU.mult))
                ch.link(nc.vector.tensor_tensor(kraw[:], kraw[:], gain[:, None, :].to_broadcast([CMP_PAD, GROUPS, HD]), ALU.mult))
                nc.vector.tensor_tensor(A[:], kraw[:], cos[:, None, :].to_broadcast([CMP_PAD, GROUPS, HD]), ALU.mult)
                for a in range(2):
                    lo, hi = a * 32, a * 32 + 32
                    last = nc.vector.tensor_tensor(B[:, :, lo:hi], kraw[:, :, 32 - lo:64 - lo],
                                                   sin[:, None, lo:hi].to_broadcast([CMP_PAD, GROUPS, 32]), ALU.mult)
                ch.link(last)
                nc.vector.tensor_tensor(R[:], A[:], B[:], ALU.add).then_inc(normed.sem, 1)
                dve.wait_ge(out_done.sem, 2)
                for g in range(GROUPS):
                    for h in range(PER_GROUP):
                        rows = slice(h * CMP_PAD, (h + 1) * CMP_PAD)
                        nc.vector.tensor_copy(vbd[rows, g, h * HD:(h + 1) * HD], c.PS[rows, 5, g * HD:(g + 1) * HD])
                dve.wait_ge(kturned.sem, 1)
                ch.link(nc.vector.tensor_copy(kcmpT[:].rearrange("p g c -> p (g c)"), c.PS[0:HD, 6, 0:GROUPS * CMP_PAD]))


def gate_and_compressed(c, P1, QKT, kcmpT, vbd, gates, dram):
    nc = c.nc
    mask_in, sig, scored, masked, expd, weighed = (c.tally("cb_" + x) for x in ("mask_in", "sig", "scored", "masked", "expd", "weighed"))
    turned, moved, summed, out = (c.tally("cb_" + x) for x in ("turned", "moved", "summed", "out"))
    with scope(nc) as sb:
        neg = sb("cb_neg", [P, QT, CMP_PAD])
        one = sb("cb_one", [P, QT, CMP_PAD])
        S = sb("cb_s", [P, HEADS, CMP_PAD])
        E = sb("cb_e", [P, HEADS, CMP_PAD])
        PT = sb("cb_pt", [P, GROUPS, P])
        mx, rs, co = (sb("cb_" + x, [P, HEADS]) for x in ("mx", "rs", "co"))
        with nc.Block() as block:
            @block.sync
            def _(sp):
                sp.dma_start(neg[:], dram["cmp_neg"]).then_inc(mask_in.sem, 16)
                sp.dma_start(one[:], dram["cmp_one"]).then_inc(mask_in.sem, 16)

            @block.tensor
            def _(pe):
                for t in range(QT):
                    if t >= 1:
                        pe.wait_ge(masked.sem, t)
                    for h in range(HEADS):
                        last = nc.tensor.matmul(c.PS[:, 0, h * CMP_PAD:(h + 1) * CMP_PAD],
                                                QKT[:, HEAD_AT["q_n"] + h, t * P:(t + 1) * P], kcmpT[:, h // PER_GROUP, :],
                                                start=True, stop=True)
                    last.then_inc(scored.sem, 1)
                    pe.wait_ge(weighed.sem, t + 1)
                    if t >= 1:
                        pe.wait_ge(moved.sem, t)
                    for g in range(GROUPS):
                        last = nc.tensor.transpose(c.PS[:, 1, g * P:(g + 1) * P],
                                                   E[:, 4 * g:4 * g + 4, :].rearrange("p h c -> p (h c)"), c.ident[:])
                    last.then_inc(turned.sem, 1)
                    pe.wait_ge(moved.sem, t + 1)
                    if t >= 1:
                        pe.wait_ge(out.sem, 2 * t)
                    for g in range(GROUPS):
                        last = nc.tensor.matmul(c.PS[:, 2, g * 256:(g + 1) * 256], PT[:, g, :], vbd[:, g, :], start=True, stop=True)
                    last.then_inc(out.sem, 1)

            @block.scalar
            def _(act):
                nc.scalar.activation(gates[:], P1[:, :, OFF["gate"]:OFF["gate"] + 3 * HEADS], ACT.Sigmoid).then_inc(sig.sem, 1)
                for t in range(QT):
                    act.wait_ge(masked.sem, t + 1)
                    act.wait_ge(summed.sem, 2 * t + 1)
                    nc.scalar.activation(E[:], S[:], ACT.Exp, scale=SCALE).then_inc(expd.sem, 1)
                for i, z in enumerate(("z_n", "z_d")):
                    nc.scalar.activation(P1[:, :, OFF[z]:OFF[z] + 512], P1[:, :, OFF[z]:OFF[z] + 512], ACT.Silu)

            @block.vector
            def _(dve):
                ch = c.dve.on(dve)
                dve.wait_ge(mask_in.sem, 32)
                dve.wait_ge(sig.sem, 1)
                for t in range(QT):
                    dve.wait_ge(scored.sem, t + 1)
                    if t >= 1:
                        dve.wait_ge(expd.sem, t)
                    nc.vector.tensor_tensor(S[:], c.PS[:, 0, 0:HEADS * CMP_PAD].rearrange("p (h c) -> p h c", h=HEADS),
                                            neg[:, t, None, :].to_broadcast([P, HEADS, CMP_PAD]), ALU.add).then_inc(masked.sem, 1)
                    dve.wait_ge(masked.sem, t + 1)
                    ch.link(nc.vector.reduce_max(mx[:], S[:], AX_X))
                    nc.vector.tensor_tensor(S[:], S[:], mx[:, :, None].to_broadcast([P, HEADS, CMP_PAD]),
                                            ALU.subtract).then_inc(summed.sem, 1)
                    dve.wait_ge(expd.sem, t + 1)
                    ch.link(nc.vector.reduce_sum(rs[:], E[:], AX_X))
                    nc.vector.tensor_tensor(E[:], E[:], one[:, t, None, :].to_broadcast([P, HEADS, CMP_PAD]),
                                            ALU.mult).then_inc(weighed.sem, 1)
                    ch.link(nc.vector.reciprocal(co[:], rs[:]))
                    ch.link(nc.vector.tensor_tensor(co[:], co[:], gates[:, t].rearrange("p (h b) -> p h b", b=3)[:, :, 0], ALU.mult))
                    dve.wait_ge(turned.sem, t + 1)
                    nc.vector.tensor_copy(PT[:].rearrange("p g q -> p (g q)"), c.PS[:, 1, 0:2 * P]).then_inc(moved.sem, 1)
                    dve.wait_ge(out.sem, 2 * t + 1)
                    nc.vector.tensor_tensor(P1[:, t, OFF["q_n"]:OFF["q_n"] + 512].rearrange("p (h d) -> p h d", h=HEADS),
                                            c.PS[:, 2, :].rearrange("p (h d) -> p h d", h=HEADS),
                                            co[:, :, None].to_broadcast([P, HEADS, HD]), ALU.mult).then_inc(out.sem, 1)
                    dve.wait_ge(out.sem, 2 * t + 2)
                    nc.vector.tensor_copy(mx[:], co[:]).then_inc(summed.sem, 1)


def index_scores(c, P1, QKT, scores, tri, sc_at, dram):
    nc = c.nc
    tri_in, scored, relu, added = (c.tally("ix_" + x) for x in ("tri_in", "scored", "relu", "added"))
    items = [(t, h) for t in range(1, QT) for h in range(IDX_HEADS)]
    with scope(nc) as sb:
        R = sb("ix_r", [P, 2, SEQ])
        wi = sb("ix_w", [P, QT, IDX_HEADS])
        with nc.Block() as block:
            @block.sync
            def _(sp):
                sp.dma_start(tri[:], dram["tri"]).then_inc(tri_in.sem, 16)

            @block.tensor
            def _(pe):
                for n, (t, h) in enumerate(items):
                    if n >= 4:
                        pe.wait_ge(relu.sem, n - 3)
                    keys = (t + 1) * P
                    nc.tensor.matmul(c.PS[:, n % 4, 0:keys], QKT[:, HEAD_AT["qi"] + h, t * P:(t + 1) * P],
                                     QKT[:, HEAD_AT["ki"], 0:keys], start=True, stop=True).then_inc(scored.sem, 1)

            @block.scalar
            def _(act):
                for n, (t, h) in enumerate(items):
                    act.wait_ge(scored.sem, n + 1)
                    if n >= 2:
                        act.wait_ge(added.sem, n - 1)
                    keys = (t + 1) * P
                    nc.scalar.activation(R[:, n % 2, 0:keys], c.PS[:, n % 4, 0:keys], ACT.Relu, scale=HD ** -0.5).then_inc(relu.sem, 1)

            @block.vector
            def _(dve):
                ch = c.dve.on(dve)
                ch.link(nc.vector.tensor_scalar(wi[:], P1[:, :, OFF["wi"]:OFF["wi"] + IDX_HEADS], IDX_HEADS ** -0.5, None, ALU.mult))
                dve.wait_ge(tri_in.sem, 16)
                for n, (t, h) in enumerate(items):
                    keys = (t + 1) * P
                    dst = scores[:, sc_at[t]:sc_at[t] + keys]
                    prev = tri[:, SEQ - keys:SEQ] if h == 0 else dst
                    dve.wait_ge(relu.sem, n + 1)
                    if h > 0:
                        dve.wait_ge(added.sem, n)
                    nc.vector.scalar_tensor_tensor(dst, R[:, n % 2, 0:keys], wi[:, t, h:h + 1], prev, ALU.mult,
                                                   ALU.add).then_inc(added.sem, 1)


class Unit:

    def __init__(self, q, k, v, mask, group, at, scale, needs=0):
        self.q, self.k, self.v, self.mask, self.group, self.at, self.scale = q, k, v, mask, group, at, scale
        self.needs = needs
        self.keys = P * len(v)
        self.pieces = [(a, min(4, len(v) - a)) for a in range(0, len(v), 4)]


def attend(c, sb, tag, units, s_banks, pt_banks, out_banks, finish, between=None, chosen=None, extra=None):
    nc = c.nc
    names = ["scored", "masked", "expd", "turned", "weighed", "drained"]
    scored, masked, expd, turned, weighed, drained = (c.tally("at_" + x) for x in names)
    b = {t: t.n for t in (scored, masked, expd, turned, weighed, drained)}
    moved = [c.tally("at_moved_even"), c.tally("at_moved_odd")]
    bm = [t.n for t in moved]
    S = sb("at_s_" + tag, [P, 2, 768])
    E = sb("at_e_" + tag, [P, 2, 768])
    NPT = len(pt_banks)
    PT = sb("at_pt_" + tag, [P, NPT, 512])
    mx, rs = sb("at_mx_" + tag, [P, len(units)]), sb("at_rs_" + tag, [P, len(units)])
    first = [0]
    for u in units:
        first.append(first[-1] + len(u.pieces))
    pieces = [(i, a, n) for i, u in enumerate(units) for a, n in u.pieces]
    ends = {u.group: i for i, u in enumerate(units)}

    def s_ps(i, lo, hi):
        return c.PS[:].rearrange("p b n -> p (b n)")[:, s_banks[i % 2] * 512 + lo:s_banks[i % 2] * 512 + hi]

    with nc.Block() as block:
        @block.sync
        def _(sp):
            if extra:
                extra.load(sp)

        @block.tensor
        def _(pe):
            def score(i):
                u = units[i]
                if i >= 2:
                    pe.wait_ge(masked.sem, b[masked] + i - 1)
                for lo in range(0, u.keys, 512):
                    hi = min(u.keys, lo + 512)
                    last = nc.tensor.matmul(s_ps(i, lo, hi), u.q, u.k(lo, hi), start=True, stop=True)
                last.then_inc(scored.sem, 1)

            def turn(p):
                i, a, n = pieces[p]
                pe.wait_ge(expd.sem, b[expd] + i + 1)
                if p >= NPT:
                    pe.wait_ge(moved[(p - NPT) % 2].sem, bm[(p - NPT) % 2] + (p - NPT) // 2 + 1)
                for j in range(n):
                    last = nc.tensor.transpose(c.PS[:, pt_banks[p % NPT], j * P:(j + 1) * P], E[:, i % 2, (a + j) * P:(a + j + 1) * P],
                                               c.ident[:])
                last.then_inc(turned.sem, 1)

            def weigh(p):
                i, a, n = pieces[p]
                u = units[i]
                pe.wait_ge(moved[p % 2].sem, bm[p % 2] + p // 2 + 1)
                n_out = len(out_banks)
                if u.group >= n_out and (i == 0 or units[i - 1].group != u.group) and a == 0:
                    pe.wait_ge(drained.sem, b[drained] + u.group - n_out + 1)
                bank = out_banks[u.group % n_out]
                width = u.v[a].shape[1]
                for j in range(n):
                    last = nc.tensor.matmul(c.PS[:, bank, u.at:u.at + width], PT[:, p % NPT, j * P:(j + 1) * P], u.v[a + j],
                                            start=(a + j == 0), stop=(a + j == len(u.v) - 1))
                last.then_inc(weighed.sem, 1)

            score(0)
            for i in range(len(units)):
                if i + 1 < len(units):
                    score(i + 1)
                for p in range(first[i], first[i + 1]):
                    turn(p)
                    if p >= 2:
                        weigh(p - 2)
                if extra:
                    extra.work(pe, i)
            weigh(len(pieces) - 2)
            weigh(len(pieces) - 1)
            if extra:
                extra.end(pe, len(units))

        @block.scalar
        def _(act):
            def exp(i):
                u = units[i]
                act.wait_ge(masked.sem, b[masked] + i + 1)
                if i >= 2:
                    act.wait_ge(turned.sem, b[turned] + first[i - 1])
                nc.scalar.activation(E[:, i % 2, 0:u.keys], S[:, i % 2, 0:u.keys], ACT.Exp, bias=mx[:, i:i + 1], scale=-1.0,
                                     accum_out=rs[:, i:i + 1]).then_inc(expd.sem, 1)

            def move(p):
                i, a, n = pieces[p]
                act.wait_ge(turned.sem, b[turned] + p + 1)
                if p >= NPT:
                    act.wait_ge(weighed.sem, b[weighed] + p - NPT + 1)
                nc.scalar.activation(PT[:, p % NPT, 0:n * P], c.PS[:, pt_banks[p % NPT], 0:n * P], ACT.Copy
                                     ).then_inc(moved[p % 2].sem, 1)

            exp(0)
            for i in range(len(units)):
                if i + 1 < len(units):
                    exp(i + 1)
                for p in range(first[i], first[i + 1]):
                    if p % 2 == 0:
                        move(p)

        @block.vector
        def _(dve):
            ch = c.dve.on(dve)

            def mask(i):
                u = units[i]
                dve.wait_ge(scored.sem, b[scored] + i + 1)
                if i >= 2:
                    dve.wait_ge(expd.sem, b[expd] + i - 1)
                if u.mask is None:
                    nc.vector.tensor_scalar(S[:, i % 2, 0:u.keys], s_ps(i, 0, u.keys), -u.scale, None, ALU.mult, ALU.min,
                                            accum_out=mx[:, i:i + 1]).then_inc(masked.sem, 1)
                else:
                    if u.needs:
                        ch.wait(chosen[u.needs])
                    nc.vector.tensor_tensor_reduce(S[:, i % 2, 0:u.keys], s_ps(i, 0, u.keys), u.mask, -u.scale, 3e38,
                                                   ALU.add, ALU.min, mx[:, i:i + 1]).then_inc(masked.sem, 1)

            def move(p):
                i, a, n = pieces[p]
                dve.wait_ge(turned.sem, b[turned] + p + 1)
                if p >= NPT:
                    dve.wait_ge(weighed.sem, b[weighed] + p - NPT + 1)
                nc.vector.tensor_copy(PT[:, p % NPT, 0:n * P], c.PS[:, pt_banks[p % NPT], 0:n * P]).then_inc(moved[p % 2].sem, 1)

            mask(0)
            for i in range(len(units)):
                if between and not (i + 1 < len(units) and units[i + 1].needs):
                    between(ch, i)
                if i + 1 < len(units):
                    mask(i + 1)
                if between and i + 1 < len(units) and units[i + 1].needs:
                    between(ch, i)
                for p in range(first[i], first[i + 1]):
                    if p % 2 == 1:
                        move(p)
                g = units[i - 1].group
                if i >= 1 and units[i - 1].group != units[i].group:
                    dve.wait_ge(weighed.sem, b[weighed] + first[ends[g] + 1])
                    finish(ch, g, rs, drained)
            g = units[-1].group
            dve.wait_ge(weighed.sem, b[weighed] + len(pieces))
            finish(ch, g, rs, drained)
    n_groups = units[-1].group + 1
    for t, d in ((scored, len(units)), (masked, len(units)), (expd, len(units)), (turned, len(pieces)),
                 (moved[0], (len(pieces) + 1) // 2), (moved[1], len(pieces) // 2), (weighed, len(pieces)), (drained, n_groups)):
        t.n += d


def project_cols(c, ring, x, w, tiles, spans, drain, after=None):
    nc = c.nc
    hi, lo = x
    parts = cols_step(ring, w, tiles)
    done = 2 if ring.ahead else 0
    steps = [tiles[i:i + 2] for i in range(0, len(tiles), 2)]
    s0 = c.step

    def ps(s, j, n, width):
        a, e = spans[n]
        return c.PS[0:width, 4 * (s % 2) + 2 * j + n, 0:e - a]

    def views(s, j):
        return tuple(t[:, s % 2, :].rearrange("p (j k n) -> p j k n", j=2, k=KT)[:, j] for t in (ring.raw, ring.hi, ring.lo))

    with nc.Block() as block:
        @block.sync
        def _(sp):
            for i in range(done, len(steps)):
                ring.load(sp, s0 + i, (s0 + i) // 2, (s0 + i) % 2, parts(s0 + i, i))
            if after:
                ring.load_ahead(sp, s0 + len(steps), after)

        @block.scalar
        def _(act):
            for i, step in list(enumerate(steps))[done // 2:]:
                s = s0 + i
                act.wait_ge(ring.loaded[s % 2], (s // 2) * 32 + 32)
                act.wait_ge(ring.used, s + 1)
                for j, (_, width, *_) in enumerate(step):
                    raw, whi, _ = views(s, j)
                    last = nc.scalar.activation(whi[:, :, 0:width], raw[:, :, 0:width], ACT.Copy)
                last.then_inc(ring.rounded, 1)
            if after:
                s = s0 + len(steps)
                ring.round(act, s, s // 2, s % 2, RING_W)

        @block.vector
        def _(dve):
            ch = c.dve.on(dve)

            def evac(i):
                dve.wait_ge(ring.used, s0 + i + 3)
                for j, tile in enumerate(steps[i]):
                    for n in range(len(spans)):
                        last = drain(dve, ch, 2 * i + j, n, ps(s0 + i, j, n, tile[1]))
                last.then_inc(ring.drained, 1)

            for i, step in enumerate(steps):
                s = s0 + i
                if i >= done // 2:
                    dve.wait_ge(ring.rounded, s + 1)
                    for j, (_, width, *_) in enumerate(step):
                        raw, whi, wlo = views(s, j)
                        last = nc.vector.tensor_tensor(wlo[:, :, 0:width], raw[:, :, 0:width], whi[:, :, 0:width].bitcast(F32),
                                                       ALU.subtract)
                    last.then_inc(ring.split, 1)
                if i >= 1:
                    evac(i - 1)
            if after:
                s = s0 + len(steps)
                ring.rest(dve, s, s // 2, s % 2, RING_W)
            evac(len(steps) - 1)

        @block.tensor
        def _(pe):
            for i, step in enumerate(steps):
                s = s0 + i
                pe.wait_ge(ring.split, s + 3)
                pe.wait_ge(ring.drained, s + 1)
                for j, (_, width, *_) in enumerate(step):
                    _, whi, wlo = views(s, j)
                    for k in range(KT):
                        for wt, xt, first, end in ((whi, hi, k == 0, False), (whi, lo, False, False), (wlo, hi, False, k == KT - 1)):
                            for n, (a, e) in enumerate(spans):
                                last = nc.tensor.matmul(ps(s, j, n, width), wt[:, k, 0:width], xt[:, k, a:e], start=first, stop=end)
                last.then_inc(ring.used, 1)
    c.step += len(steps)
    ring.ahead = after is not None


def attend_first(c, P1, QKT, scores, sc_at, tri, gates, sb, extra=None):
    nc = c.nc
    units, groups = [], []
    for t in range(QT):
        for kname, vname, gate in (("ks", "vs", 1), ("kw", "vw", 2)):
            for h in range(HEADS):
                g = h // PER_GROUP
                units.append(Unit(QKT[:, HEAD_AT["q_n"] + h, t * P:(t + 1) * P],
                                  lambda lo, hi, kh=HEAD_AT[kname] + g: QKT[:, kh, lo:hi],
                                  [P1[:, kt, OFF[vname] + g * HD:OFF[vname] + g * HD + (HD if h == HEADS - 1 else 2 * HD)] for kt in range(t + 1)],
                                  tri[:, SEQ - (t + 1) * P:SEQ], len(groups), h * HD, SCALE))
            groups.append((t, gate))
    n_before = len(units)
    for t in range(QT):
        mask = tri[:, SEQ - P:SEQ] if t == 0 else scores[:, sc_at[t]:sc_at[t] + (t + 1) * P]
        for h in range(HEADS):
            g = h // PER_GROUP
            units.append(Unit(QKT[:, HEAD_AT["q_d"] + h, t * P:(t + 1) * P],
                              lambda lo, hi, kh=HEAD_AT["k_d"] + g: QKT[:, kh, lo:hi],
                              [P1[:, kt, OFF["v_d"] + g * HD:OFF["v_d"] + g * HD + (HD if h == HEADS - 1 else 2 * HD)] for kt in range(t + 1)],
                              mask, len(groups), h * HD, SCALE, needs=t))
        groups.append((t, 0))
    top = sb("top", [P, 8])
    co = sb("co", [P, HEADS])
    tmp = sb("o_tmp", [P, HEADS, HD])
    chosen = {}
    rounds = [(t, r) for t in range(1, QT) for r in range(TOPK // 8)]

    def between(ch, i):
        if i >= len(rounds):
            return
        t, r = rounds[i]
        s = scores[:, sc_at[t]:sc_at[t] + (t + 1) * P]
        ch.link(nc.vector.max(top[:], s))
        ch.link(nc.vector.match_replace(s, top[:], s, TAKEN))
        if r == TOPK // 8 - 1:
            chosen[t] = ch.mark(nc.vector.tensor_scalar(s, s, TAKEN_LIMIT, NEG, ALU.is_ge, ALU.mult))

    def finish(ch, g, rs, drained):
        t, gate = groups[g]
        ps = c.PS[:, 6 + g % 2, :].rearrange("p (h d) -> p h d", h=HEADS)
        at, z_at = (OFF["q_n"], OFF["z_n"]) if gate else (OFF["q_d"], OFF["z_d"])
        dst = P1[:, t, at:at + 512].rearrange("p (h d) -> p h d", h=HEADS)
        z = P1[:, t, z_at:z_at + 512].rearrange("p (h d) -> p h d", h=HEADS)
        ch.link(nc.vector.reciprocal(co[:], rs[:, 8 * g:8 * g + 8]))
        if gate:
            ch.link(nc.vector.tensor_tensor(co[:], co[:], gates[:, t].rearrange("p (h b) -> p h b", b=3)[:, :, gate], ALU.mult))
        n = drained.n + g + 1
        nc.vector.tensor_tensor(tmp[:], ps, co[:, :, None].to_broadcast([P, HEADS, HD]), ALU.mult).then_inc(drained.sem, 1)
        ch.eng.wait_ge(drained.sem, n)
        if gate:
            ch.link(nc.vector.tensor_tensor(dst, dst, tmp[:], ALU.add))
            if gate == 2:
                ch.link(nc.vector.tensor_tensor(dst, dst, z, ALU.mult))
        else:
            ch.link(nc.vector.tensor_tensor(dst, tmp[:], z, ALU.mult))

    if len(rounds) > n_before:
        raise ValueError("the rounds of the top-k end before the indexed units")
    attend(c, sb, "1", units, [0, 1], [2, 4, 5], [6, 7], finish, between, chosen, extra)


def turn_rows(c, tiles, n_tok_tiles, out, tag):
    nc = c.nc
    turned, rounded, split = c.tally("tr_turned"), c.tally("tr_rounded"), c.tally("tr_split")
    b = {t: t.n for t in (turned, rounded, split)}
    items = [(j, a, min(a + 4, n_tok_tiles)) for j in range(len(tiles)) for a in range(0, n_tok_tiles, 4)]
    with nc.Block() as block:
        @block.tensor
        def _(pe):
            for n, (j, a, e) in enumerate(items):
                if n >= 4:
                    pe.wait_ge(split.sem, b[split] + n - 3)
                for t in range(a, e):
                    last = nc.tensor.transpose(c.PS[:, n % 4, (t - a) * P:(t - a + 1) * P], tiles[j](t), c.ident[:])
                last.then_inc(turned.sem, 1)

        @block.scalar
        def _(act):
            for n, (j, a, e) in enumerate(items):
                dst = out(j, a * P, e * P)
                if len(dst) == 2:
                    act.wait_ge(turned.sem, b[turned] + n + 1)
                    nc.scalar.activation(dst[0], c.PS[:, n % 4, 0:(e - a) * P], ACT.Copy).then_inc(rounded.sem, 1)

        @block.vector
        def _(dve):
            for n, (j, a, e) in enumerate(items):
                dst = out(j, a * P, e * P)
                if len(dst) == 2:
                    dve.wait_ge(rounded.sem, b[rounded] + n + 1)
                    nc.vector.tensor_tensor(dst[1], c.PS[:, n % 4, 0:(e - a) * P], dst[0].bitcast(F32),
                                            ALU.subtract).then_inc(split.sem, 1)
                else:
                    dve.wait_ge(turned.sem, b[turned] + n + 1)
                    nc.vector.tensor_copy(dst[0], c.PS[:, n % 4, 0:(e - a) * P]).then_inc(split.sem, 1)
    turned.n += len(items)
    split.n += len(items)
    if len(out(0, 0, P)) == 2:
        rounded.n += len(items)


class Adaptive:
    SLOTS = 4

    def __init__(self, c, sb, w_ada, s_c, bank):
        self.nc, self.c, self.s_c, self.bank = c.nc, c, s_c, bank
        self.w = w_ada.rearrange("l (k p) (s n) -> l s p k n", p=P, n=256)
        self.raw = sb("ada_w", [P, self.SLOTS, KT, 256])
        self.loaded = [c.tally(f"ada_loaded{i}").sem for i in range(self.SLOTS)]
        self.used = c.tally("ada_used").sem
        self.n = LAYERS * ADA_STEPS
        self.done = 0
        self.units = 1

    def load(self, sp):
        for n in range(self.n):
            if n >= self.SLOTS:
                sp.wait_ge(self.used, n - self.SLOTS + 1)
            sp.dma_start(self.raw[:, n % self.SLOTS], self.w[n // ADA_STEPS, n % ADA_STEPS]).then_inc(self.loaded[n % self.SLOTS], 16)

    def step(self, pe, n):
        pe.wait_ge(self.loaded[n % self.SLOTS], 16 * (n // self.SLOTS + 1))
        for j in range(2):
            at = 2 * (2 * n + j)
            for k in range(KT):
                last = self.nc.tensor.matmul(self.c.PS[:, self.bank, at:at + ADA_N], self.raw[:, n % self.SLOTS, k, j * P:(j + 1) * P],
                                             self.s_c[:, k, :], start=(k == 0), stop=(k == KT - 1))
        last.then_inc(self.used, 1)

    def work(self, pe, i):
        while self.done < self.n * (i + 1) // self.units:
            self.step(pe, self.done)
            self.done += 1

    def end(self, pe, n):
        while self.done < self.n:
            self.step(pe, self.done)
            self.done += 1


def silu_conditions(c, sb, s_c, dram):
    nc = c.nc
    c_in, cleared = c.tally("cond_in"), c.tally("cond_cleared")
    raw = sb("cond_raw", [P, KT, 2])
    with nc.Block() as block:
        @block.sync
        def _(sp):
            sp.dma_start(raw[:], dram["conditions"]).then_inc(c_in.sem, 16)

        @block.vector
        def _(dve):
            nc.vector.memset(s_c[:], 0.0).then_inc(cleared.sem, 1)

        @block.scalar
        def _(act):
            act.wait_ge(c_in.sem, 16)
            act.wait_ge(cleared.sem, 1)
            nc.scalar.activation(s_c[:, :, 0:2], raw[:], ACT.Silu)


def finish_adaptive(c, bank, dram):
    nc = c.nc
    small = c.tally("ada_small_in")
    with scope(nc) as sb:
        bias = sb("b_ada", [P, LAYERS, N_MOD * KT])
        gains = sb("layer_gains", [P, LAYERS, 3, KT])
        with nc.Block() as block:
            @block.sync
            def _(sp):
                sp.dma_start(bias[:], dram["b_ada"]).then_inc(small.sem, 16)
                sp.dma_start(gains[:], dram["layer_gains"]).then_inc(small.sem, 16)

            @block.vector
            def _(dve):
                ch = c.dve.on(dve)
                dve.wait_ge(small.sem, 32)
                for l in range(LAYERS):
                    for v in range(2):
                        src = c.PS[:, bank, l * 144:(l + 1) * 144].rearrange("p (n v) -> p v n", v=2)[:, v]
                        last = ch.mark(nc.vector.tensor_tensor(c.mod[:, l, v, :], src, bias[:, l], ALU.add))
                ch.wait(last)
                for l in range(LAYERS):
                    for v in range(2):
                        for i, m in enumerate((1, 4, 7)):
                            x = c.mod[:, l, v, m * KT:(m + 1) * KT]
                            ch.mark(nc.vector.scalar_tensor_tensor(x, x, 1.0, gains[:, l, i], ALU.add, ALU.mult))
                        for m in (2, 8):
                            x = c.mod[:, l, v, m * KT:(m + 1) * KT]
                            last = ch.mark(nc.vector.tensor_scalar(x, x, 0.5, None, ALU.mult))
                ch.wait(last)


def first_block(c, dram):
    nc = c.nc
    load_rows(c, dram["x"], SEQ, 0, "x")
    g_in = c.tally("gain_in")
    with scope(nc) as sb1:
        P1 = sb1("P1", [P, QT, IN_COLS])
        with scope(nc) as sb:
            gain = sb("norm_gain_cols", [P, KT])
            with nc.Block() as block:
                @block.sync
                def _(sp):
                    sp.dma_start(gain[:], dram["norm_gain"]).then_inc(g_in.sem, 16)
                    sp.wait_ge(g_in.sem, 16)
            ring = Ring(c, sb)
            x = norm(c, sb, [(0, SEQ)], [gain], [None], "b1")
            project_rows(c, ring, x, dram["w_in"], 0, IN_COLS, list(range(QT)), P1)
        with scope(nc) as sb2:
            QKT = sb2("QKT", [HD, N_ROT, SEQ])
            kcmpT = sb2("kcmpT", [HD, GROUPS, CMP_PAD])
            vbd = sb2("vbd", [P, GROUPS, PER_GROUP * HD])
            gates = sb2("gates", [P, QT, 3 * HEADS])
            tri = sb2("tri_mask", [P, SEQ])
            sc_at = {1: 0, 2: 2 * P, 3: 5 * P}
            scores = sb2("scores", [P, 9 * P])
            s_c = sb2("s_c", [P, KT, ADA_N])
            silu_conditions(c, sb2, s_c, dram)
            rotate(c, P1, QKT, dram)
            compress(c, P1, kcmpT, vbd, dram)
            gate_and_compressed(c, P1, QKT, kcmpT, vbd, gates, dram)
            index_scores(c, P1, QKT, scores, tri, sc_at, dram)
            with scope(nc) as sb:
                ada = Adaptive(c, sb, dram["w_ada"], s_c, 3)
                ada.units = 3 * HEADS * QT
                attend_first(c, P1, QKT, scores, sc_at, tri, gates, sb, ada)
            finish_adaptive(c, 3, dram)
        with scope(nc) as sb:
            hi, lo = sb("mixT_hi", [P, KT, SEQ], F32R), sb("mixT_lo", [P, KT, SEQ], F32R)
            cols = [OFF[n] + j * P for n in ("q_n", "q_d") for j in range(4)]
            turn_rows(c, [lambda t, a=a: P1[:, t, a:a + P] for a in cols], QT,
                      lambda j, a, e: (hi[:, j, a:e], lo[:, j, a:e]), "b1")
            ring = Ring(c, sb)

            def drain(dve, ch, d, n, ps):
                return nc.vector.tensor_tensor(c.hT[:, d, 0:SEQ], ps, c.hT[:, d, 0:SEQ], ALU.add)

            project_cols(c, ring, (hi, lo), dram["w_out"], [(d * P, P) for d in range(KT)], [(0, SEQ)], drain)



def ffn_step(ring, w13):
    src = w13.rearrange("(k p) (f n) -> p k f n", p=P, n=P)

    def parts(s, i):
        raw = ring.raw[:, s % 2].rearrange("p (w k n) -> p w k n", w=2, k=KT)
        return [(raw[:, w], src[:, :, w * FT + i, :]) for w in range(2)]
    return parts


def ffn(c, sb, ring, x, w13, w2, gates, spans, tag, after=None):
    nc = c.nc
    hi, lo = x
    n_tok = spans[-1][1]
    G = 8
    groups = [(f, min(G, FT - f)) for f in range(0, FT, G)]
    hid_hi, hid_lo = sb("hid_hi_" + tag, [P, G, n_tok], F32R), sb("hid_lo_" + tag, [P, G, n_tok], F32R)
    sa, hf = sb("silu_a_" + tag, [P, 2, n_tok]), sb("hid_f_" + tag, [P, 2, n_tok])
    silu_done, h_rounded, h_split = c.tally("f_silu"), c.tally("f_h_rounded"), c.tally("f_h_split")
    u0, hr0, hs0 = silu_done.n, h_rounded.n, h_split.n
    w13_v = w13.rearrange("(k p) (f n) -> p k f n", p=P, n=P)
    w2_v = w2.rearrange("(f p) (q n) -> p f q n", p=P, n=2 * P)
    s0 = c.step
    n_steps = FT + len(groups) * KT // 2
    flat = c.PS[:].rearrange("p b n -> p (b n)")
    raw_up = [ring.raw[:, q].rearrange("p (w k n) -> p w k n", w=2, k=KT) for q in range(2)]
    up = [[t[:, q].rearrange("p (w k n) -> p w k n", w=2, k=KT) for q in range(2)] for t in (ring.hi, ring.lo)]
    raw_dn = [ring.raw[:, q].rearrange("p (f n) -> p f n", f=G) for q in range(2)]
    dn = [[t[:, q].rearrange("p (f n) -> p f n", f=G) for q in range(2)] for t in (ring.hi, ring.lo)]

    def phases():
        s = s0
        for f, nf in groups:
            yield s, nf, f, nf, True
            s += nf
            yield s, KT // 2, f, nf, False
            s += KT // 2

    def two(s, i):
        return [(2 * i + (s + k), i + (s + k) // 2, (s + k) % 2, k) for k in range(2)]

    with nc.Block() as block:
        @block.sync
        def _(sp):
            for s1, n, f0, nf, is_up in phases():
                with sp.Fori(1 if s1 == s0 and ring.ahead else 0, n // 2) as i:
                    for s, half, q, k in two(s1, i):
                        sp.wait_ge(ring.split, s + 1)
                        if is_up:
                            for w in range(2):
                                sp.dma_start(raw_up[q][:, w], w13_v[:, :, 2 * i + (w * FT + f0 + k), :]).then_inc(ring.loaded[q], 16)
                        else:
                            for h in range(2):
                                fs = slice(h * nf // 2, (h + 1) * nf // 2)
                                sp.dma_start(raw_dn[q][:, fs], w2_v[:, f0 + h * nf // 2:f0 + (h + 1) * nf // 2, 2 * i + k, :]
                                             ).then_inc(ring.loaded[q], 16)
            if after:
                ring.load_ahead(sp, s0 + n_steps, after)

        @block.tensor
        def _(pe):
            for s1, n, f0, nf, is_up in phases():
                if not is_up:
                    pe.wait_ge(h_split.sem, hs0 + f0 + nf - 1)
                with pe.Fori(0, n // 2) as i:
                    for s, half, q, k in two(s1, i):
                        pe.wait_ge(ring.split, s + 3)
                        pe.wait_ge(ring.drained, s + 1)
                        for w in range(2):
                            n_k = KT if is_up else nf
                            for kk in range(n_k):
                                if not is_up and k == 0 and w == 0 and kk == nf - 1:
                                    pe.wait_ge(h_split.sem, hs0 + f0 + nf)
                                if is_up:
                                    whi, wlo = up[0][q][:, w, kk, :], up[1][q][:, w, kk, :]
                                    xhi, xlo = hi[:, kk], lo[:, kk]
                                else:
                                    whi, wlo = dn[0][q][:, kk, w * P:(w + 1) * P], dn[1][q][:, kk, w * P:(w + 1) * P]
                                    xhi, xlo = hid_hi[:, kk], hid_lo[:, kk]
                                for wt, xt, first, end in ((whi, xhi, kk == 0, False), (whi, xlo, False, False),
                                                           (wlo, xhi, False, kk == n_k - 1)):
                                    for m, (a, e) in enumerate(spans):
                                        last = nc.tensor.matmul(c.PS[:, 4 * q + 2 * w + m, 0:e - a], wt, xt[:, a:e],
                                                                start=first, stop=end)
                        last.then_inc(ring.used, 1)

        def res(q, w):
            return flat[:, (4 * q + 2 * w) * 512:(4 * q + 2 * w) * 512 + n_tok]

        def round_next(act, s, half, q):
            act.wait_ge(ring.loaded[q], half * 32 + 32)
            act.wait_ge(ring.used, s + 1)
            nc.scalar.activation(ring.hi[:, q, :], ring.raw[:, q, :], ACT.Copy).then_inc(ring.rounded, 1)

        @block.scalar
        def _(act):
            def body(s1, f0, is_up, i, more):
                for s, half, q, k in two(s1, i):
                    if k == 0 or more:
                        round_next(act, s + 1, i + (s1 + k + 1) // 2, 1 - q)
                    if is_up:
                        u = 2 * i + (f0 + k)
                        act.wait_ge(ring.used, s + 3)
                        act.wait_ge(ring.drained, s + 1)
                        nc.scalar.activation(sa[:, q, :], res(q, 0), ACT.Silu).then_inc(silu_done.sem, 1)
                        act.wait_ge(ring.drained, s + 3)
                        nc.scalar.activation(hid_hi[:, 2 * i + k, :], hf[:, q, :], ACT.Copy).then_inc(h_rounded.sem, 1)

            if not ring.ahead:
                round_next(act, s0, s0 // 2, s0 % 2)
            for s1, n, f0, nf, is_up in phases():
                if after or s1 + n < s0 + n_steps:
                    with act.Fori(0, n // 2) as i:
                        body(s1, f0, is_up, i, True)
                else:
                    for i in range(n // 2):
                        body(s1, f0, is_up, i, i < n // 2 - 1)

        @block.vector
        def _(dve):
            def rest_next(s, half, q):
                dve.wait_ge(ring.rounded, s + 1)
                nc.vector.tensor_tensor(ring.lo[:, q, :], ring.raw[:, q, :], ring.hi[:, q, :].bitcast(F32),
                                        ALU.subtract).then_inc(ring.split, 1)

            def body(s1, f0, is_up, i, more):
                for s, half, q, k in two(s1, i):
                    if k == 0 or more:
                        rest_next(s + 1, 0, 1 - q)
                    if is_up:
                        u = 2 * i + (f0 + k)
                        dve.wait_ge(silu_done.sem, u + (u0 + 1))
                        nc.vector.tensor_tensor(hf[:, q, :], res(q, 1), sa[:, q, :], ALU.mult).then_inc(ring.drained, 1)
                        dve.wait_ge(h_rounded.sem, u + (hr0 + 1))
                        nc.vector.tensor_tensor(hid_lo[:, 2 * i + k, :], hf[:, q, :], hid_hi[:, 2 * i + k, :].bitcast(F32),
                                                ALU.subtract).then_inc(h_split.sem, 1)
                    else:
                        dve.wait_ge(ring.used, s + 3)
                        for w in range(2):
                            for (a, e), gate in zip(spans, gates):
                                d = 4 * i + (2 * k + w)
                                last = nc.vector.scalar_tensor_tensor(c.hT[:, d, a:e], res(q, w)[:, a:e], gate[:, bass.ds(d, 1)],
                                                                      c.hT[:, d, a:e], ALU.mult, ALU.add)
                        last.then_inc(ring.drained, 1)

            if not ring.ahead:
                rest_next(s0, 0, s0 % 2)
            for s1, n, f0, nf, is_up in phases():
                if after or s1 + n < s0 + n_steps:
                    with dve.Fori(0, n // 2) as i:
                        body(s1, f0, is_up, i, True)
                else:
                    for i in range(n // 2):
                        body(s1, f0, is_up, i, i < n // 2 - 1)
    c.step += n_steps
    ring.ahead = after is not None
    for t in (silu_done, h_rounded, h_split):
        t.n += FT


PAD = 8
ZL = PAD + SEQ + 2 * PAD + CTX + PAD
Z_AT = [PAD, PAD + SEQ + 2 * PAD]


def load_all(c, name, pairs):
    t = c.tally(name)
    t.n += 16 * len(pairs)
    n = t.n

    def issue(sp):
        for dst, src in pairs:
            sp.dma_start(dst, src).then_inc(t.sem, 16)
        sp.wait_ge(t.sem, n)
    return issue


KR_AT = OFF_KR - QK_NOPE


def kv_tiles(dram, l):
    return [(OFF_KV, P), (KR_AT, QKW), (0, QKW, dram["w_kr_swapped"][l])]


REST_TILES = [(OFF_F, P), (OFF_F + P, P), (OFF_Q, 96), (OFF_Q + 96, 96), (OFF_P, P), (OFF_P + P, P)]
ALL_TILES = [(d * P, P) for d in range(KT)]


def mix_layer(c, ring, l, dram, after):
    nc = c.nc
    last = l == LAYERS - 1
    spans = SPANS[:1] if last else SPANS
    n_out = spans[-1][1]
    n_tt = n_out // P
    mod = lambda v, m: c.mod[:, l, v, m * KT:(m + 1) * KT]
    with scope(nc) as sbm:
        mixf = sbm("mixf", [P, KT, n_out])
        with scope(nc) as sbo:
            fT = sbo("fT", [P, 2, n_out])
            cqT = sbo("cqT", [96, 2, n_out])
            ckvT = sbo("ckvT", [KV_RANK, 1, TOK])
            krT = sbo("krT", [QKW, 2, TOK])
            Z = sbo("pool_z", [P, 2, ZL])
            rows = sbo("sgu_rows", [P, TT, 2 * GW])
            with scope(nc) as sbx:
                x = norm(c, sbx, SPANS, [mod(0, 4), mod(1, 4)], [mod(0, 3), mod(1, 3)], f"m{l}")
                w = dram["w_in_2"][l]

                def drain_kv(dve, ch, tile, n, ps):
                    a, e = SPANS[n]
                    if tile == 0:
                        return nc.vector.tensor_copy(ckvT[:, 0, a:e], ps)
                    return nc.vector.tensor_copy(krT[QK_NOPE:QKW, tile - 1, a:e], ps[QK_NOPE:QKW])

                project_cols(c, ring, x, w, kv_tiles(dram, l), SPANS, drain_kv, cols_step(ring, w, REST_TILES))

                def drain_rest(dve, ch, tile, n, ps):
                    a, e = spans[n]
                    if tile < 2:
                        return nc.vector.tensor_copy(fT[:, tile, a:e], ps)
                    if tile < 4:
                        return nc.vector.tensor_copy(cqT[:, tile - 2, a:e], ps)
                    return nc.vector.tensor_copy(Z[:, tile - 4, Z_AT[n]:Z_AT[n] + e - a], ps)

                with nc.Block() as block:
                    @block.vector
                    def _(dve):
                        c.dve.on(dve).link(nc.vector.memset(Z[:], 0.0))
                project_cols(c, ring, x, w, REST_TILES, spans, drain_rest, rows_step(ring, w, OFF_G, 2 * GW))
                project_rows(c, ring, x, w, OFF_G, 2 * GW, list(range(n_tt)), rows, cols_step(ring, dram["w_out_2"][l], ALL_TILES))
            attention_mixer(c, l, spans, cqT, ckvT, krT, mixf, dram)
            fourier_mixer_(c, l, spans, fT, mixf, dram)
            pooling_mixer_(c, l, spans, Z, mixf, dram)
            gating_mixer(c, l, n_tt, rows, mixf, dram)
        hi, lo = sbm("mix2_hi", [P, KT, n_out], F32R), sbm("mix2_lo", [P, KT, n_out], F32R)
        rounded = c.tally("m_rounded")
        r0 = rounded.n
        with nc.Block() as block:
            @block.scalar
            def _(act):
                for k in range(KT):
                    nc.scalar.activation(hi[:, k], mixf[:, k], ACT.Copy).then_inc(rounded.sem, 1)

            @block.vector
            def _(dve):
                for k in range(KT):
                    dve.wait_ge(rounded.sem, r0 + k + 1)
                    nc.vector.tensor_tensor(lo[:, k], mixf[:, k], hi[:, k].bitcast(F32), ALU.subtract)
        rounded.n += KT

        def drain(dve, ch, d, n, ps):
            a, e = spans[n]
            return nc.vector.scalar_tensor_tensor(c.hT[:, d, a:e], ps, mod(n, 5)[:, d:d + 1], c.hT[:, d, a:e], ALU.mult, ALU.add)

        project_cols(c, ring, (hi, lo), dram["w_out_2"][l], ALL_TILES, spans, drain, after)


def rank_norm(c, sb, parts, x, n_tiles, spans, rank, gain, issue, tag):
    nc = c.nc
    sq_done, sum_done, root_done, in_done = c.tally("rn_squared"), c.tally("rn_summed"), c.tally("rn_rooted"), c.tally("rn_loaded")
    b = [t.n for t in (sq_done, sum_done, root_done, in_done)]
    n_tok = spans[-1][1]
    with scope(nc) as tmp:
        sq = tmp("rn_sq_" + tag, [parts, n_tiles, n_tok])
        inv = tmp("rn_inv_" + tag, [parts, n_tok])
        with nc.Block() as block:
            @block.sync
            def _(sp):
                issue(sp)
                sp.sem_inc(in_done.sem, 1)

            @block.scalar
            def _(act):
                nc.scalar.activation(sq[:], x[:, :, 0:n_tok], ACT.Square).then_inc(sq_done.sem, 1)
                act.wait_ge(sum_done.sem, b[1] + 1)
                for a, e in spans:
                    nc.scalar.activation(inv[:, a:e], c.PS[0:parts, a // 512, 0:e - a], ACT.Sqrt, bias=c.eps[0:parts],
                                         scale=1.0 / rank).then_inc(root_done.sem, 1)

            @block.tensor
            def _(pe):
                pe.wait_ge(sq_done.sem, b[0] + 1)
                for a, e in spans:
                    for j in range(n_tiles):
                        last = nc.tensor.matmul(c.PS[0:parts, a // 512, 0:e - a], c.ones1[0:parts, 0:parts], sq[:, j, a:e],
                                                start=(j == 0), stop=(j == n_tiles - 1))
                last.then_inc(sum_done.sem, 1)

            @block.vector
            def _(dve):
                ch = c.dve.on(dve)
                dve.wait_ge(root_done.sem, b[2] + len(spans))
                dve.wait_ge(in_done.sem, b[3] + 1)
                ch.link(nc.vector.reciprocal(inv[:], inv[:]))
                for j in range(n_tiles):
                    last = ch.mark(nc.vector.scalar_tensor_tensor(x[:, j, 0:n_tok], x[:, j, 0:n_tok], gain[:, j:j + 1], inv[:],
                                                                  ALU.mult, ALU.mult))
                ch.wait(last)
    for t, d in ((sq_done, 1), (sum_done, 1), (root_done, len(spans)), (in_done, 1)):
        t.n += d


def attention_mixer(c, l, spans, cqT, ckvT, krT, mixf, dram):
    nc = c.nc
    n_out = spans[-1][1]
    with scope(nc) as sb:
        w_uq, w_uqs = sb("w_uq", [96, 2, MH * QKW]), sb("w_uqs", [96, 2, MH * QKW])
        w_ukv = sb("w_ukv", [KV_RANK, MH, 2, 64])
        g_q, g_kv = sb("g_q", [96, 2]), sb("g_kv", [KV_RANK, 1])
        cosT, sinT = sb("rope_cos", [QKW, SEQ]), sb("rope_sin", [QKW, SEQ])
        qT, kT = sb("qT", [QKW, MH, n_out]), sb("kT", [QKW, MH, TOK])
        V = sb("v2", [P, TT, MH * V_HD])
        att = sb("att", [P, n_out // P, MH * V_HD])
        issue = load_all(c, "mla_in", [(w_uq[:], dram["w_uq"][l].rearrange("(j p) n -> p j n", p=96)),
                                       (w_uqs[:], dram["w_uq_swapped"][l].rearrange("(j p) n -> p j n", p=96)),
                                       (w_ukv[:], dram["w_ukv"][l].rearrange("p (h t n) -> p h t n", h=MH, t=2)),
                                       (g_q[:], dram["g_q"][l]), (g_kv[:], dram["g_kv"][l]),
                                       (cosT[:], dram["rope_cos"]), (sinT[:], dram["rope_sin"])])
        rank_norm(c, sb, 96, cqT, 2, spans, Q_RANK, g_q, issue, "q")
        rank_norm(c, sb, KV_RANK, ckvT, 1, SPANS, KV_RANK, g_kv, lambda sp: None, "kv")

        made, taken = c.tally("mla_made"), c.tally("mla_taken")
        m0, t0 = made.n, taken.n
        items = []
        for h in range(MH):
            for n, (a, e) in enumerate(spans):
                items.append(("q", h, n, a, e))
                if n == 0:
                    items.append(("qs", h, n, a, e))
            for n, (a, e) in enumerate(SPANS):
                items.append(("k", h, n, a, e))
        for t in range(TT):
            items.append(("v", 0, t, t * P, (t + 1) * P))
        with scope(nc) as tmp:
            A, B = tmp("mla_a", [QKW, SEQ]), tmp("mla_b", [QKW, SEQ])
            kr = tmp("mla_kr", [QKW, TOK])
            with nc.Block() as block:
                @block.tensor
                def _(pe):
                    for i, (what, h, n, a, e) in enumerate(items):
                        if i >= 6:
                            pe.wait_ge(taken.sem, t0 + i - 5)
                        bank = c.PS[:, i % 6, :]
                        if what in ("q", "qs"):
                            wt = w_uq if what == "q" else w_uqs
                            for j in range(2):
                                last = nc.tensor.matmul(bank[0:QKW, 0:e - a], wt[:, j, h * QKW:(h + 1) * QKW], cqT[:, j, a:e],
                                                        start=(j == 0), stop=(j == 1))
                        elif what == "k":
                            last = nc.tensor.matmul(bank[0:QK_NOPE, 0:e - a], w_ukv[:, h, 0, :], ckvT[:, 0, a:e], start=True, stop=True)
                        else:
                            last = nc.tensor.matmul(bank[:, 0:MH * V_HD], ckvT[:, 0, a:e], w_ukv[:, :, 1, :], start=True, stop=True)
                        last.then_inc(made.sem, 1)

                @block.vector
                def _(dve):
                    ch = c.dve.on(dve)
                    rope = slice(QK_NOPE, QKW)
                    ch.mark(nc.vector.tensor_tensor(A[rope], krT[rope, 0, 0:SEQ], cosT[rope], ALU.mult))
                    ch.mark(nc.vector.tensor_copy(kr[rope, SEQ:TOK], krT[rope, 0, SEQ:TOK]))
                    ch.link(nc.vector.tensor_tensor(B[rope], krT[rope, 1, 0:SEQ], sinT[rope], ALU.mult))
                    ch.link(nc.vector.tensor_tensor(kr[rope, 0:SEQ], A[rope], B[rope], ALU.add))
                    for i, (what, h, n, a, e) in enumerate(items):
                        bank = c.PS[:, i % 6, :]
                        dve.wait_ge(made.sem, m0 + i + 1)
                        if what == "q" and n == 0:
                            nc.vector.tensor_tensor(A[:], bank[0:QKW, 0:SEQ], cosT[:], ALU.mult).then_inc(taken.sem, 1)
                            dve.wait_ge(taken.sem, t0 + i + 1)
                        elif what == "qs":
                            nc.vector.tensor_tensor(B[:], bank[0:QKW, 0:SEQ], sinT[:], ALU.mult).then_inc(taken.sem, 1)
                            dve.wait_ge(taken.sem, t0 + i + 1)
                            ch.link(nc.vector.tensor_tensor(qT[:, h, 0:SEQ], A[:], B[:], ALU.add))
                        elif what == "q":
                            nc.vector.tensor_copy(qT[:, h, a:e], bank[0:QKW, 0:e - a]).then_inc(taken.sem, 1)
                        elif what == "k":
                            nc.vector.tensor_copy(kT[0:QK_NOPE, h, a:e], bank[0:QK_NOPE, 0:e - a]).then_inc(taken.sem, 1)
                            nc.vector.tensor_copy(kT[rope, h, a:e], kr[rope, a:e])
                        else:
                            nc.vector.tensor_copy(V[:, n, :], bank[:, 0:MH * V_HD]).then_inc(taken.sem, 1)
        made.n += len(items)
        taken.n += len(items)

        units, groups = [], []
        for t in range(n_out // P):
            kt = list(range(TT)) if t < QT else list(range(QT, TT))
            for h in range(MH):
                units.append(Unit(qT[:, h, t * P:(t + 1) * P], lambda lo, hi, h=h, k0=kt[0] * P: kT[:, h, k0 + lo:k0 + hi],
                                  [V[:, x, h * V_HD:min(h + 2, MH) * V_HD] for x in kt], None, len(groups), h * V_HD, QKW ** -0.5))
            groups.append(t)
        co = sb("mla_co", [P, MH])

        def finish(ch, g, rs, drained):
            ch.link(nc.vector.reciprocal(co[:], rs[:, MH * g:MH * (g + 1)]))
            nc.vector.tensor_tensor(att[:, g, :].rearrange("p (h d) -> p h d", h=MH),
                                    c.PS[:, 7, 0:MH * V_HD].rearrange("p (h d) -> p h d", h=MH),
                                    co[:, :, None].to_broadcast([P, MH, V_HD]), ALU.mult).then_inc(drained.sem, 1)

        attend(c, sb, f"m{l}", units, [0, 2], [4, 5, 6], [7], finish)
        turn_rows(c, [lambda t, j=j: att[:, t, j * P:(j + 1) * P] for j in range(2)], n_out // P,
                  lambda j, a, e: (mixf[:, 2 + j, a:e],), f"att{l}")


def fourier_mixer_(c, l, spans, fT, mixf, dram):
    nc = c.nc
    n_tt = spans[-1][1] // P
    loaded = c.tally("ft_loaded")
    head, taken, seq, out, fin = (c.tally("ft_" + x) for x in ("head", "taken", "seq", "seq_taken", "out"))
    b = {t: t.n for t in (loaded, head, taken, seq, out, fin)}
    with scope(nc) as sb:
        CS = sb("dft_head", [P, 2 * P])
        CL, SL = sb("dft_cos", [P, QT, SEQ]), sb("dft_nsin", [P, QT, SEQ])
        wf = sb("w_fnet", [P, 2, P])
        AB = sb("dft_ab", [P, n_tt, 2, 2 * P])
        F = sb("dft_f", [P, 2, spans[-1][1]])
        issue = load_all(c, "ft_in", [(CS[:], dram["dft_head"]), (CL[:], dram["dft_cos"]), (SL[:], dram["dft_nsin"]),
                                      (wf[:], dram["w_fnet"][l])])
        head_items = [(t, j) for t in range(n_tt) for j in range(2)]
        seq_items = [(j, n) for j in range(2) for n in range(len(spans))]
        with nc.Block() as block:
            @block.sync
            def _(sp):
                issue(sp)
                sp.sem_inc(loaded.sem, 1)

            @block.tensor
            def _(pe):
                pe.wait_ge(loaded.sem, b[loaded] + 1)
                for i, (t, j) in enumerate(head_items):
                    if i >= 4:
                        pe.wait_ge(taken.sem, b[taken] + i - 3)
                    nc.tensor.matmul(c.PS[:, i % 4, 0:2 * P], fT[:, j, t * P:(t + 1) * P], CS[:], start=True, stop=True
                                     ).then_inc(head.sem, 1)
                pe.wait_ge(taken.sem, b[taken] + len(head_items))
                for i, (j, n) in enumerate(seq_items):
                    a, e = spans[n]
                    step = SEQ // (e - a)
                    k0, k1 = a // P, e // P
                    for t in range(k0, k1):
                        for s, M in enumerate((CL, SL)):
                            last = nc.tensor.matmul(c.PS[:, 4 + i, 0:e - a], AB[:, t, j, s * P:(s + 1) * P],
                                                    M[:, t - k0, 0:SEQ:step], start=(t == k0 and s == 0), stop=(t == k1 - 1 and s == 1))
                    last.then_inc(seq.sem, 1)
                for i, (j, n) in enumerate(seq_items):
                    a, e = spans[n]
                    pe.wait_ge(out.sem, b[out] + i + 1)
                    nc.tensor.matmul(c.PS[:, i, 0:e - a], wf[:, j, :], F[:, j, a:e], start=True, stop=True).then_inc(fin.sem, 1)

            @block.scalar
            def _(act):
                for i, (j, n) in enumerate(seq_items):
                    a, e = spans[n]
                    act.wait_ge(seq.sem, b[seq] + i + 1)
                    nc.scalar.activation(F[:, j, a:e], c.PS[:, 4 + i, 0:e - a], ACT.Copy, scale=((e - a) * 64) ** -0.5
                                         ).then_inc(out.sem, 1)

            @block.vector
            def _(dve):
                for i, (t, j) in enumerate(head_items):
                    dve.wait_ge(head.sem, b[head] + i + 1)
                    nc.vector.tensor_copy(AB[:, t, j, :], c.PS[:, i % 4, 0:2 * P]).then_inc(taken.sem, 1)
                for i, (j, n) in enumerate(seq_items):
                    a, e = spans[n]
                    dve.wait_ge(fin.sem, b[fin] + i + 1)
                    nc.vector.tensor_copy(mixf[:, j, a:e], c.PS[:, i, 0:e - a])
    for t, d in ((loaded, 1), (head, len(head_items)), (taken, len(head_items)), (seq, len(seq_items)), (out, len(seq_items)),
                 (fin, len(seq_items))):
        t.n += d


def pooling_mixer_(c, l, spans, Z, mixf, dram):
    nc = c.nc
    loaded, pooled, fin = c.tally("pl_loaded"), c.tally("pl_pooled"), c.tally("pl_out")
    b = {t: t.n for t in (loaded, pooled, fin)}
    items = [(j, n) for j in range(2) for n in range(len(spans))]
    with scope(nc) as sb:
        inv = sb("pool_inv", [P, 2, ZL])
        wp, sp_col = sb("w_pool", [P, 2, P]), sb("s_pool", [P, 2])
        S2, S4, S8, S16 = (sb("pool_s%d" % w, [P, 2, ZL]) for w in (2, 4, 8, 16))
        R = sb("pool_r", [P, 2, ZL])
        issue = load_all(c, "pl_in", [(inv[:], dram["pool_inv"]), (wp[:], dram["w_pool"][l]), (sp_col[:], dram["s_pool"][l])])
        with nc.Block() as block:
            @block.sync
            def _(sp):
                issue(sp)
                sp.sem_inc(loaded.sem, 1)

            @block.vector
            def _(dve):
                ch = c.dve.on(dve)
                for t in (S2, S4, S8, S16):
                    n = ch.mark(nc.vector.memset(t[:], 0.0))
                ch.wait(n)
                ch.link(nc.vector.tensor_tensor(S2[:, :, 1:ZL], Z[:, :, 0:ZL - 1], Z[:, :, 1:ZL], ALU.add))
                for w, A, B in ((2, S2, S4), (4, S4, S8), (8, S8, S16)):
                    h = w // 2
                    ch.link(nc.vector.tensor_tensor(B[:, :, h:ZL - h], A[:, :, 0:ZL - 2 * h], A[:, :, 2 * h:ZL], ALU.add))
                dve.wait_ge(loaded.sem, b[loaded] + 1)
                for j, tiles in enumerate(((S2, S4), (S8, S16))):
                    for half, S in enumerate(tiles):
                        r = slice(64 * half, 64 * half + 64)
                        n = ch.mark(nc.vector.tensor_tensor(R[r, j], S[r, j], inv[r, j], ALU.mult))
                ch.wait(n)
                nc.vector.tensor_tensor(R[:], R[:], Z[:], ALU.subtract).then_inc(pooled.sem, 1)
                for i, (j, n) in enumerate(items):
                    a, e = spans[n]
                    dve.wait_ge(fin.sem, b[fin] + i + 1)
                    nc.vector.tensor_scalar(mixf[:, 6 + j, a:e], c.PS[:, i, 0:e - a], sp_col[:, j:j + 1], None, ALU.mult)

            @block.tensor
            def _(pe):
                pe.wait_ge(loaded.sem, b[loaded] + 1)
                pe.wait_ge(pooled.sem, b[pooled] + 1)
                for i, (j, n) in enumerate(items):
                    a, e = spans[n]
                    nc.tensor.matmul(c.PS[:, i, 0:e - a], wp[:, j, :], R[:, j, Z_AT[n]:Z_AT[n] + e - a], start=True, stop=True
                                     ).then_inc(fin.sem, 1)
    loaded.n += 1
    pooled.n += 1
    fin.n += len(items)


def gating_mixer(c, l, n_tt, rows, mixf, dram):
    nc = c.nc
    loaded, gelu, squared, rooted, mixed = (c.tally("sg_" + x) for x in ("loaded", "gelu", "squared", "rooted", "mixed"))
    summed, ready = c.tally("sg_summed"), c.tally("sg_ready")
    b = {t: t.n for t in (loaded, gelu, squared, rooted, mixed, summed, ready)}
    with scope(nc) as sb:
        gain = sb("sgu_gain", [P, MH, 64])
        wsT, bs = sb("w_sgu", [P, MH, P]), sb("b_sgu", [P, MH])
        G, V = sb("sgu_g", [P, TT, 2 * GW]), sb("sgu_v", [P, TT, GW])
        sq = sb("sgu_sq", [P, TT, GW])
        ss = sb("sgu_ss", [P, TT * MH])
        out = sb("sgu_out", [P, TT, GW])
        issue = load_all(c, "sg_in", [(gain[:], dram["g_sgu_rows"][l]), (wsT[:], dram["w_sgu_t"][l]), (bs[:], dram["b_sgu_t"][l])])
        heads = lambda x: x.rearrange("p t (h d) -> p (t h) d", h=MH)
        with nc.Block() as block:
            @block.sync
            def _(sp):
                issue(sp)
                sp.sem_inc(loaded.sem, 1)

            @block.scalar
            def _(act):
                nc.scalar.activation(G[:, 0:n_tt], rows[:, 0:n_tt], ACT.Gelu_apprx_tanh).then_inc(gelu.sem, 1)
                act.wait_ge(gelu.sem, b[gelu] + 1)
                nc.scalar.activation(sq[:, 0:n_tt], G[:, 0:n_tt, GW:2 * GW], ACT.Square).then_inc(squared.sem, 1)
                act.wait_ge(summed.sem, b[summed] + 1)
                nc.scalar.activation(ss[:, 0:n_tt * MH], ss[:, 0:n_tt * MH], ACT.Sqrt, bias=c.eps[:], scale=1.0 / 64).then_inc(rooted.sem, 1)

            @block.vector
            def _(dve):
                ch = c.dve.on(dve)
                dve.wait_ge(squared.sem, b[squared] + 1)
                n = n_tt * MH
                nc.vector.reduce_sum(ss[:, 0:n], heads(sq[:, 0:n_tt]), AX_X).then_inc(summed.sem, 1)
                dve.wait_ge(rooted.sem, b[rooted] + 1)
                dve.wait_ge(loaded.sem, b[loaded] + 1)
                ch.link(nc.vector.reciprocal(ss[:, 0:n], ss[:, 0:n]))
                v = V[:, 0:n_tt].rearrange("p t (h d) -> p (t h) d", h=MH)
                for t in range(n_tt):
                    m = ch.mark(nc.vector.tensor_tensor(V[:, t].rearrange("p (h d) -> p h d", h=MH),
                                                        G[:, t, GW:2 * GW].rearrange("p (h d) -> p h d", h=MH),
                                                        ss[:, t * MH:(t + 1) * MH, None].to_broadcast([P, MH, 64]), ALU.mult))
                ch.wait(m)
                for t in range(n_tt):
                    last = nc.vector.tensor_tensor(V[:, t], V[:, t], gain[:].rearrange("p h d -> p (h d)"), ALU.mult)
                last.then_inc(ready.sem, 1)
                for t in range(n_tt):
                    dve.wait_ge(mixed.sem, b[mixed] + t + 1)
                    for h in range(MH):
                        cols = slice(h * 64, (h + 1) * 64)
                        m = nc.vector.scalar_tensor_tensor(out[:, t, cols], c.PS[:, t, cols], bs[:, h:h + 1], G[:, t, cols],
                                                           ALU.add, ALU.mult)
                ch.link(m)

            @block.tensor
            def _(pe):
                pe.wait_ge(loaded.sem, b[loaded] + 1)
                pe.wait_ge(ready.sem, b[ready] + 1)
                for t in range(n_tt):
                    for h in range(MH):
                        cols = slice(h * 64, (h + 1) * 64)
                        last = nc.tensor.matmul(c.PS[:, t, cols], wsT[:, h, :], V[:, t, cols], start=True, stop=True)
                    last.then_inc(mixed.sem, 1)
        turn_rows(c, [lambda t, j=j: out[:, t, j * P:(j + 1) * P] for j in range(2)], n_tt,
                  lambda j, a, e: (mixf[:, 4 + j, a:e],), f"sgu{l}")
    for t, d in ((loaded, 1), (gelu, 1), (squared, 1), (rooted, 1), (mixed, n_tt), (summed, 1), (ready, 1)):
        t.n += d


def finish_output(c, dram, out):
    nc = c.nc
    g_in, stored = c.tally("final_gain_in"), c.tally("stored")
    with scope(nc) as sb:
        gain, zero = sb("g_final", [P, KT]), None
        with nc.Block() as block:
            @block.sync
            def _(sp):
                sp.dma_start(gain[:], dram["g_final"]).then_inc(g_in.sem, 16)
                sp.wait_ge(g_in.sem, 16)
        squared, summed, rooted, scaled, turned, moved = (c.tally("o_" + x) for x in
                                                          ("squared", "summed", "rooted", "scaled", "turned", "moved"))
        sq = sb("o_sq", [P, 2, SEQ])
        inv = sb("o_inv", [P, SEQ])
        rows = sb("o_rows", [P, QT, D])
        with nc.Block() as block:
            @block.scalar
            def _(act):
                for k in range(KT):
                    if k >= 2:
                        act.wait_ge(summed.sem, k - 1)
                    nc.scalar.activation(sq[:, k % 2], c.hT[:, k, 0:SEQ], ACT.Square).then_inc(squared.sem, 1)
                act.wait_ge(summed.sem, KT)
                nc.scalar.activation(inv[:], c.PS[:, 0, :], ACT.Sqrt, bias=c.eps[:]).then_inc(rooted.sem, 1)

            @block.tensor
            def _(pe):
                for k in range(KT):
                    pe.wait_ge(squared.sem, k + 1)
                    nc.tensor.matmul(c.PS[:, 0, :], c.ones[:], sq[:, k % 2], start=(k == 0), stop=(k == KT - 1)).then_inc(summed.sem, 1)
                pe.wait_ge(scaled.sem, KT)
                for n in range(2 * QT):
                    t, half = n // 2, n % 2
                    if n >= 4:
                        pe.wait_ge(moved.sem, n - 3)
                    for j in range(4):
                        last = nc.tensor.transpose(c.PS[:, 1 + n % 4, j * P:(j + 1) * P], c.hT[:, 4 * half + j, t * P:(t + 1) * P], c.ident[:])
                    last.then_inc(turned.sem, 1)

            @block.vector
            def _(dve):
                ch = c.dve.on(dve)
                dve.wait_ge(rooted.sem, 1)
                ch.link(nc.vector.reciprocal(inv[:], inv[:]))
                for k in range(KT):
                    nc.vector.scalar_tensor_tensor(c.hT[:, k, 0:SEQ], c.hT[:, k, 0:SEQ], gain[:, k:k + 1], inv[:], ALU.mult,
                                                   ALU.mult).then_inc(scaled.sem, 1)
                for n in range(2 * QT):
                    dve.wait_ge(turned.sem, n + 1)
                    nc.vector.tensor_copy(rows[:, n // 2, (n % 2) * 512:(n % 2) * 512 + 512], c.PS[:, 1 + n % 4, :]).then_inc(moved.sem, 1)

            @block.sync
            def _(sp):
                for t in range(QT):
                    sp.wait_ge(moved.sem, 2 * t + 2)
                    sp.dma_start(out[t * P:(t + 1) * P, :], rows[:, t, :]).then_inc(stored.sem, 16)
                sp.wait_ge(stored.sem, 16 * QT)


def second_block(c, dram, out):
    nc = c.nc
    load_rows(c, dram["ctx"], CTX, SEQ, "ctx")
    with scope(nc) as sbr:
        ring = Ring(c, sbr)
        for l in range(LAYERS):
            mod = lambda v, m: c.mod[:, l, v, m * KT:(m + 1) * KT]
            for half in range(2):
                spans = SPANS[:1] if (half and l == LAYERS - 1) else SPANS
                m = 6 * half
                vs = range(len(spans))
                with scope(nc) as sb:
                    x = norm(c, sb, spans, [mod(v, m + 1) for v in vs], [mod(v, m) for v in vs], f"f{l}{half}")
                    if not half:
                        after = cols_step(ring, dram["w_in_2"][l], kv_tiles(dram, l))
                    else:
                        after = ffn_step(ring, dram["w13_ffn1"][l + 1]) if l + 1 < LAYERS else None
                    ffn(c, sb, ring, x, dram[f"w13_ffn{half + 1}"][l], dram[f"w2_ffn{half + 1}"][l],
                        [mod(v, m + 2) for v in vs], spans, f"f{l}{half}", after)
                if not half:
                    mix_layer(c, ring, l, dram, ffn_step(ring, dram["w13_ffn2"][l]))
    finish_output(c, dram, out)


def build(nc, dram, out):
    with ExitStack() as st:
        c = Core(nc, st)
        start(c, dram)
        first_block(c, dram)
        second_block(c, dram, out)



def shape_tables():
    import numpy as np
    f = np.float32

    def half_angles(pos):
        inv = (f(10000.0) ** (-np.arange(HD // 2, dtype=f) / f(HD // 2))).astype(f)
        ang = (pos[:, None] * inv[None, :]).astype(f)
        co, si = np.cos(ang), np.sin(ang)
        return np.concatenate([co, co], 1), np.concatenate([-si, si], 1)

    def tiles(a):
        return a.reshape(-1, P, a.shape[-1]).transpose(1, 0, 2)

    co, si = half_angles(np.arange(SEQ, dtype=f))
    starts = np.arange(N_CMP) * CMP_STRIDE + CMP_BLOCK - 1
    c_co, c_si = half_angles(np.append(starts, 0).astype(f))
    seen = np.append(starts, 10 ** 9)[None, :] <= np.arange(SEQ)[:, None]
    tri = np.zeros((P, SEQ), f)
    tri[:, SEQ - P:] = np.where(np.arange(P)[None, :] <= np.arange(P)[:, None], 0, NEG)

    axis = QK_ROPE // 2
    inv2 = np.power(f(10000.0), -np.arange(0, axis, 2, dtype=f) / f(axis)).astype(f)
    t = np.arange(SEQ)
    cos2, sin2 = np.ones((QKW, SEQ), f), np.zeros((QKW, SEQ), f)
    for i, p in enumerate(((t // 64).astype(f), (t % 64).astype(f))):
        ang = (p[:, None] * inv2).astype(f).T
        r = QK_NOPE + axis * i
        cos2[r:r + 8], cos2[r + 8:r + 16] = np.cos(ang), np.cos(ang)
        sin2[r:r + 8], sin2[r + 8:r + 16] = -np.sin(ang), np.sin(ang)

    k = np.arange(64)
    ang = 2 * np.pi * (np.outer(k, k) % 64) / 64
    head = np.zeros((P, 2 * P))
    for h in range(2):
        head[h * 64:h * 64 + 64, h * 64:h * 64 + 64] = np.cos(ang)
        head[h * 64:h * 64 + 64, P + h * 64:P + h * 64 + 64] = np.sin(ang)
    n = np.arange(SEQ)
    ang = 2 * np.pi * (np.outer(n, n) % SEQ) / SEQ
    pool_inv = np.zeros((P, 2, ZL), f)
    for g, w in enumerate((2, 4, 8, 16)):
        for at, length in zip(Z_AT, (SEQ, CTX)):
            p = np.arange(length)
            lo, hi = np.clip(p - w // 2, 0, length), np.clip(p - w // 2 + w, 0, length)
            pool_inv[(g % 2) * 64:(g % 2) * 64 + 64, g // 2, at:at + length] = (f(1.0) / (hi - lo).astype(f))[None]
    return dict(identity=np.eye(P), cos=tiles(co), sin=tiles(si), cmp_cos=c_co, cmp_sin=c_si,
                cmp_neg=tiles(np.where(seen, 0.0, NEG)), cmp_one=tiles(seen.astype(f)), tri=tri,
                rope_cos=cos2, rope_sin=sin2, dft_head=head, dft_cos=tiles(np.cos(ang)), dft_nsin=tiles(-np.sin(ang)),
                pool_inv=pool_inv)


def laid_out(i):
    import numpy as np

    def cols(a):
        a = a.reshape(a.shape[:-1] + (-1, P))
        return np.moveaxis(a, -1, 0)

    def repeated(a, n=P):
        return np.broadcast_to(a, (n,) + a.shape)

    def diagonal(a):
        out = np.zeros((LAYERS, P, 2, P), a.dtype)
        for h in range(4):
            r = (h % 2) * 64
            out[:, r:r + 64, h // 2, r:r + 64] = a[:, h]
        return out

    swap = np.arange(QK_ROPE).reshape(2, 2, QK_ROPE // 4)[:, ::-1].reshape(-1)
    head_swap = np.concatenate([np.arange(QK_NOPE), QK_NOPE + swap])
    gains = [np.tile(i[n][0], r) for n, r in (("nsa_q_gain", 8), ("dsa_q_gain", 8), ("nsa_ks_gain", 2), ("nsa_kw_gain", 2),
                                              ("dsa_k_gain", 2))]
    out = dict(
        x=i["x"][0], norm_gain=cols(i["norm_gain"][0]), w_in=i["w_in"][0], w_out=i["w_out"][0],
        gain_rows=repeated(np.concatenate(gains).reshape(N_NORMED, HD)), kc_gain=repeated(i["nsa_kc_gain"][0], CMP_PAD),
        conditions=cols(np.stack([i["c_2"][0], i["c_ctx_2"]])).transpose(0, 2, 1), ctx=i["ctx_2"][0],
        w_ada=i["w_ada_2"], b_ada=cols(i["b_ada_2"]),
        layer_gains=cols(np.stack([i["g_ffn1_2"], i["g_mix_2"], i["g_ffn2_2"]], 1)),
        w13_ffn1=i["w13_ffn1_2"], w2_ffn1=i["w2_ffn1_2"], w13_ffn2=i["w13_ffn2_2"], w2_ffn2=i["w2_ffn2_2"],
        w_in_2=i["w_in_2"], w_kr_swapped=i["w_in_2"][:, :, OFF_KR - QK_NOPE + head_swap], w_out_2=i["w_out_2"],
        w_uq=i["w_uq_2"], w_uq_swapped=i["w_uq_2"].reshape(LAYERS, Q_RANK, MH, QKW)[..., head_swap].reshape(i["w_uq_2"].shape),
        w_ukv=i["w_ukv_2"], g_q=i["g_q_2"].reshape(LAYERS, 2, 96).transpose(0, 2, 1), g_kv=i["g_kv_2"][:, :, None],
        w_fnet=diagonal(i["w_fnet_2"]), w_pool=diagonal(i["w_pool_2"]), s_pool=i["s_pool_2"].reshape(LAYERS, 2, P).transpose(0, 2, 1),
        g_sgu_rows=np.stack([repeated(i["g_sgu_2"][l]) for l in range(LAYERS)]), w_sgu_t=i["w_sgu_2"].transpose(0, 3, 1, 2),
        b_sgu_t=i["b_sgu_2"].transpose(0, 2, 1), g_final=cols(i["g_final_2"]),
    )
    for x in "kv":
        out[f"cmp_{x}_w1"] = i[f"cmp_{x}_w1"][0]
        out[f"cmp_{x}_w2"] = i[f"cmp_{x}_w2"][0]
        out[f"cmp_{x}_b1"] = cols(i[f"cmp_{x}_b1"][0])
        out[f"cmp_pe_{x}"] = i[f"cmp_pe_{x}"][0].reshape(CMP_BLOCK // 2, P).T
    return out


def kernel(**inputs):
    import numpy as np
    import concourse.bacc as bacc
    from concourse.bass_utils import run_bass_kernel_spmd as run

    nc = bacc.Bacc("TRN2", target_bir_lowering=False, num_devices=1)
    arrays = {f"in_{n}_dram": np.ascontiguousarray(a, dtype=np.float32) for n, a in shape_tables().items()}
    for n, a in laid_out({n: np.asarray(a) for n, a in inputs.items()}).items():
        arrays[f"in_{n}_dram"] = np.ascontiguousarray(a)
    dram = {n[3:-5]: nc.dram_tensor(n, a.shape, F32, kind="ExternalInput").ap() for n, a in arrays.items()}
    out = nc.dram_tensor("out_0_dram", (SEQ, D), F32, kind="ExternalOutput").ap()
    build(nc, dram, out)
    r = run(nc, [arrays], core_ids=[0])
    return r.results[0]["out_0_dram"].reshape(1, SEQ, D)
```

```python
from contextlib import ExitStack, contextmanager
from itertools import count

import concourse.bass as bass
from concourse import mybir

P = 128
SERIAL = count()
F32 = mybir.dt.float32
F32R = mybir.dt.float32r
ALU = mybir.AluOpType
ACT = mybir.ActivationFunctionType
AX_X = mybir.AxisListType.X

D = 1024
KT = D // P
SEQ = 512
QT = SEQ // P
HD = 64
HEADS = 8
GROUPS = 2
PER_GROUP = HEADS // GROUPS
IDX_HEADS = 4
CMP_BLOCK, CMP_STRIDE, CMP_HIDDEN = 32, 16, 256
N_CMP = (SEQ - CMP_BLOCK) // CMP_STRIDE + 1
CMP_PAD = 32
TOPK = min(256, SEQ // 4)
WIDTHS = dict(q_n=512, kc=128, vc=128, ks=128, vs=128, kw=128, vw=128, gate=3 * HEADS, z_n=512,
              q_d=512, k_d=128, v_d=128, qi=IDX_HEADS * HD, ki=HD, wi=IDX_HEADS, z_d=512)
OFF, _at = {}, 0
for _name, _w in WIDTHS.items():
    OFF[_name] = _at
    _at += _w
IN_COLS = _at
ROTATED = [("q_n", 8), ("q_d", 8), ("ks", 2), ("kw", 2), ("k_d", 2), ("qi", 4), ("ki", 1)]
HEAD_AT, _at = {}, 0
for _name, _n in ROTATED:
    HEAD_AT[_name] = _at
    _at += _n
N_ROT = _at
N_NORMED = HEAD_AT["qi"]
SCALE = HD ** -0.5
EPS = 1e-6
NEG = -1e30
TAKEN = -3e38
TAKEN_LIMIT = -2e38

CTX = 256
TOK = SEQ + CTX
TT = TOK // P
N_MOD = 9
LAYERS = 2
FF = 2816
FT = FF // P
GW = 256
MH = 4
QK_NOPE, QK_ROPE, V_HD = 64, 32, 64
QKW = QK_NOPE + QK_ROPE
Q_RANK, KV_RANK = 192, 128
OFF_F = 0
OFF_Q = OFF_F + GW
OFF_KV = OFF_Q + Q_RANK
OFF_KR = OFF_KV + KV_RANK
OFF_G = OFF_KR + QK_ROPE
OFF_P = OFF_G + 2 * GW
IN_W = OFF_P + GW
SPANS = [(0, SEQ), (SEQ, TOK)]


RING_W = 2048


class Tally:

    def __init__(self, sem, n=0):
        self.sem, self.n = sem, n


class Chain:

    def __init__(self, tally):
        self.t = tally
        self.eng = None

    def on(self, eng):
        self.eng = eng
        return self

    def mark(self, ins):
        ins.then_inc(self.t.sem, 1)
        self.t.n += 1
        return self.t.n

    def wait(self, n):
        self.eng.wait_ge(self.t.sem, n)

    def link(self, ins):
        self.wait(self.mark(ins))


class Core:

    def __init__(self, nc, ctx):
        self.nc, self.ctx = nc, ctx
        self.sems = {}

    def sb(self, name, shape, dt=F32):
        return self.ctx.enter_context(self.nc.sbuf_tensor(name, shape, dt))

    def tally(self, name):
        if name not in self.sems:
            self.sems[name] = Tally(self.ctx.enter_context(self.nc.semaphore(name)))
        return self.sems[name]


@contextmanager
def scope(nc):
    with ExitStack() as st:
        yield lambda name, shape, dt=F32: st.enter_context(nc.sbuf_tensor(f"{name}_{next(SERIAL)}", shape, dt))



class Ring:

    def __init__(self, c, sb):
        self.nc = c.nc
        self.raw = sb("w_raw", [P, 2, RING_W])
        self.hi = sb("w_hi", [P, 2, RING_W], F32R)
        self.lo = sb("w_lo", [P, 2, RING_W], F32R)
        self.loaded = [c.tally("w_loaded0").sem, c.tally("w_loaded1").sem]
        self.rounded = c.tally("w_rounded").sem
        self.split = c.tally("w_split").sem
        self.used = c.tally("w_used").sem
        self.drained = c.tally("psum_drained").sem
        self.c = c
        self.ahead = False

    def load_ahead(self, sp, s, after):
        for i in range(2):
            self.load(sp, s + i, (s + i) // 2, (s + i) % 2, after(s + i, i))

    def load(self, sp, s, half, slot, parts):
        sp.wait_ge(self.split, s + 1)
        for dst, src in parts:
            sp.dma_start(dst, src).then_inc(self.loaded[slot], 16)

    def round(self, act, s, half, slot, n):
        act.wait_ge(self.loaded[slot], half * 32 + 32)
        act.wait_ge(self.used, s + 1)
        self.nc.scalar.activation(self.hi[:, slot, 0:n], self.raw[:, slot, 0:n], ACT.Copy).then_inc(self.rounded, 1)

    def rest(self, dve, s, half, slot, n):
        dve.wait_ge(self.rounded, s + 1)
        self.nc.vector.tensor_tensor(self.lo[:, slot, 0:n], self.raw[:, slot, 0:n],
                                     self.hi[:, slot, 0:n].bitcast(F32), ALU.subtract).then_inc(self.split, 1)

    def round_second(self, act, s0):
        return lambda: self.round(act, s0 + 1, (s0 + 1) // 2, (s0 + 1) % 2, RING_W)

    def rest_second(self, dve, s0):
        return lambda: self.rest(dve, s0 + 1, (s0 + 1) // 2, (s0 + 1) % 2, RING_W)

    def view(self, slot, pattern, n=RING_W, **kw):
        return tuple(t[:, slot, 0:n].rearrange(pattern, **kw) for t in (self.raw, self.hi, self.lo))



def start(c, dram):
    nc = c.nc
    c.hT = c.sb("hT", [P, KT, TOK])
    c.ident = c.sb("ident", [P, P])
    c.ones = c.sb("ones", [P, P])
    c.ones1 = c.sb("ones1", [P, P])
    c.eps = c.sb("eps", [P, 1])
    c.mod = c.sb("mod", [P, LAYERS, 2, N_MOD * KT])
    c.PS = c.ctx.enter_context(nc.psum_tensor("PS", [P, 8, 512], F32))
    c.dve = Chain(c.tally("dve_step"))
    c.act = Chain(c.tally("act_step"))
    c.step = 0
    const_in = c.tally("const_in")
    with nc.Block() as block:
        @block.sync
        def _(sp):
            sp.dma_start(c.ident[:], dram["identity"]).then_inc(const_in.sem, 16)
            sp.wait_ge(const_in.sem, 16)

        @block.vector
        def _(dve):
            nc.vector.memset(c.ones[:], 1.0 / D).then_inc(c.tally("w_split").sem, 2)
            nc.vector.memset(c.ones1[:], 1.0).then_inc(c.tally("w_used").sem, 2)
            nc.vector.memset(c.eps[:], EPS).then_inc(c.tally("psum_drained").sem, 2)


def load_rows(c, src, n_tok, at, tag, ring, after):
    nc = c.nc
    nt = n_tok // P
    rows_in, turned, moved = [c.tally(f"rows_in{i}") for i in range(2)], c.tally("rows_turned"), c.tally("rows_moved")
    t0, m0 = turned.n, moved.n
    r0 = [r.n for r in rows_in]
    with scope(nc) as sb:
        rows = sb("rows_" + tag, [P, 2, D])
        with nc.Block() as block:
            @block.sync
            def _(sp):
                for t in range(nt):
                    if t >= 2:
                        sp.wait_ge(turned.sem, t0 + 2 * (t - 1))
                    sp.dma_start(rows[:, t % 2, :], src[t * P:(t + 1) * P, :]).then_inc(rows_in[t % 2].sem, 16)
                ring.load_ahead(sp, c.step, after)

            @block.scalar
            def _(act):
                ring.round(act, c.step, c.step // 2, c.step % 2, RING_W)

            @block.tensor
            def _(pe):
                for t in range(nt):
                    pe.wait_ge(rows_in[t % 2].sem, r0[t % 2] + 16 * (t // 2 + 1))
                    for half in range(2):
                        n = 2 * t + half
                        if n >= 2:
                            pe.wait_ge(moved.sem, m0 + n - 1)
                        for j in range(4):
                            last = nc.tensor.transpose(c.PS[:, n % 2, j * P:(j + 1) * P],
                                                       rows[:, t % 2, (4 * half + j) * P:(4 * half + j + 1) * P], c.ident[:])
                        last.then_inc(turned.sem, 1)

            @block.vector
            def _(dve):
                for n in range(2 * nt):
                    t, half = n // 2, n % 2
                    dve.wait_ge(turned.sem, t0 + n + 1)
                    nc.vector.tensor_copy(c.hT[:, 4 * half:4 * half + 4, at + t * P:at + (t + 1) * P],
                                          c.PS[:, n % 2, :].rearrange("p (j t) -> p j t", j=4)).then_inc(moved.sem, 1)
                ring.rest(dve, c.step, 0, c.step % 2, RING_W)
    ring.ahead = True
    turned.n += 2 * nt
    moved.n += 2 * nt
    for t in range(nt):
        rows_in[t % 2].n += 16


class Operand:

    def __init__(self, c, sb, n, tag, made=False):
        self.c, self.n = c, n
        self.hi, self.lo = sb(f"x_hi_{tag}", [P, KT, n], F32R), sb(f"x_lo_{tag}", [P, KT, n], F32R)
        self.ready = c.tally("x_ready")
        self.r0 = self.ready.n
        self.made = made
        if not made:
            self.ready.n += KT

    def first_use(self):
        first, self.made = not self.made, True
        return first

    def wait(self, pe, k):
        pe.wait_ge(self.ready.sem, self.r0 + k + 1)

    def tensor(self, pe):
        pass


class Normed(Operand):

    def __init__(self, c, sb, spans, gains, shifts, tag):
        super().__init__(c, sb, spans[-1][1], tag)
        n = self.n
        self.spans, self.gains, self.shifts = spans, gains, shifts
        self.sq = sb("sq_" + tag, [P, 4, n])
        self.inv = sb("inv_" + tag, [P, n])
        self.normed = self.sq
        self.squared, self.paired, self.summed = c.tally("n_squared"), c.tally("n_paired"), c.tally("n_summed")
        self.rooted, self.scaled, self.shifted = c.tally("n_rooted"), c.tally("n_scaled"), c.tally("n_shifted")
        counts = ((self.squared, KT), (self.paired, KT // 2), (self.summed, KT // 2), (self.rooted, len(spans)),
                  (self.scaled, KT), (self.shifted, KT))
        self.b = {t: t.n for t, _ in counts}
        for t, d in counts:
            t.n += d

    def scalar(self, act, meanwhile):
        nc, b = self.c.nc, self.b
        for k in range(KT):
            if k >= 4:
                act.wait_ge(self.summed.sem, b[self.summed] + k // 2 - 1)
            nc.scalar.activation(self.sq[:, k % 4, :], self.c.hT[:, k, 0:self.n], ACT.Square).then_inc(self.squared.sem, 1)
        meanwhile()
        act.wait_ge(self.summed.sem, b[self.summed] + KT // 2)
        for a, e in self.spans:
            nc.scalar.activation(self.inv[:, a:e], self.c.PS[:, a // 512, 0:e - a], ACT.Sqrt, bias=self.c.eps[:]
                                 ).then_inc(self.rooted.sem, 1)
        for k in range(KT):
            act.wait_ge(self.scaled.sem, b[self.scaled] + k + 1)
            for (a, e), s in zip(self.spans, self.shifts):
                last = nc.scalar.activation(self.hi[:, k, a:e], self.normed[:, k % 4, a:e], ACT.Identity,
                                            bias=0.0 if s is None else s[:, k:k + 1])
            last.then_inc(self.shifted.sem, 1)

    def tensor(self, pe):
        nc, b = self.c.nc, self.b
        for j in range(KT // 2):
            pe.wait_ge(self.paired.sem, b[self.paired] + j + 1)
            for a, e in self.spans:
                last = nc.tensor.matmul(self.c.PS[:, a // 512, 0:e - a], self.c.ones[:], self.sq[:, 2 * j % 4, a:e],
                                        start=(j == 0), stop=(j == KT // 2 - 1))
            last.then_inc(self.summed.sem, 1)

    def vector(self, dve, ch, meanwhile):
        nc, b = self.c.nc, self.b
        for j in range(KT // 2):
            dve.wait_ge(self.squared.sem, b[self.squared] + 2 * j + 2)
            q = 2 * j % 4
            nc.vector.tensor_tensor(self.sq[:, q, :], self.sq[:, q, :], self.sq[:, q + 1, :], ALU.add).then_inc(self.paired.sem, 1)
        meanwhile()
        dve.wait_ge(self.rooted.sem, b[self.rooted] + len(self.spans))
        ch.link(nc.vector.reciprocal(self.inv[:], self.inv[:]))

        def scale(k):
            for (a, e), g in zip(self.spans, self.gains):
                last = nc.vector.scalar_tensor_tensor(self.normed[:, k % 4, a:e], self.c.hT[:, k, a:e], g[:, k:k + 1],
                                                      self.inv[:, a:e], ALU.mult, ALU.mult)
            last.then_inc(self.scaled.sem, 1)

        scale(0)
        for k in range(KT):
            if k + 1 < KT:
                if k >= 3:
                    self.wait(dve, k - 3)
                scale(k + 1)
            dve.wait_ge(self.shifted.sem, b[self.shifted] + k + 1)
            for (a, e), s in zip(self.spans, self.shifts):
                hi = self.hi[:, k, a:e].bitcast(F32)
                if s is None:
                    last = nc.vector.tensor_tensor(self.lo[:, k, a:e], self.normed[:, k % 4, a:e], hi, ALU.subtract)
                else:
                    last = nc.vector.scalar_tensor_tensor(self.lo[:, k, a:e], self.normed[:, k % 4, a:e], s[:, k:k + 1], hi,
                                                          ALU.add, ALU.subtract)
            last.then_inc(self.ready.sem, 1)


class Split(Operand):

    def __init__(self, c, sb, x, n, tag):
        super().__init__(c, sb, n, tag)
        self.x = x
        self.rounded = c.tally("x_rounded")
        self.b0 = self.rounded.n
        self.rounded.n += KT

    def scalar(self, act, meanwhile):
        for k in range(KT):
            self.c.nc.scalar.activation(self.hi[:, k], self.x[:, k], ACT.Copy).then_inc(self.rounded.sem, 1)
            if k == 1:
                meanwhile()

    def vector(self, dve, ch, meanwhile):
        for k in range(KT):
            dve.wait_ge(self.rounded.sem, self.b0 + k + 1)
            self.c.nc.vector.tensor_tensor(self.lo[:, k], self.x[:, k], self.hi[:, k].bitcast(F32), ALU.subtract
                                           ).then_inc(self.ready.sem, 1)
            if k == 1:
                meanwhile()


def opening(x, pe, products_of, finish):
    for k in range(KT // 2):
        x.wait(pe, k)
        for i in range(2):
            products_of(i, k)
    for i in range(2):
        for k in range(KT // 2, KT):
            if i == 0:
                x.wait(pe, k)
            last = products_of(i, k)
        finish(i, last)


def rows_step(ring, w, col0, n_cols):
    def parts(s, i):
        a = 256 * (i % -(-n_cols // 256))
        m = min(256, n_cols - a)
        raw = ring.view(s % 2, "p (k n) -> p k n", k=KT)[0]
        src = w.rearrange("(k p) n -> p k n", p=P)
        return [(raw[:, k:k + 4, 0:m], src[:, k:k + 4, col0 + a:col0 + a + m]) for k in (0, 4)]
    return parts


def cols_step(ring, w, tiles):
    steps = [tiles[i:i + 2] for i in range(0, len(tiles), 2)]

    def parts(s, i):
        raw = ring.raw[:, s % 2, :].rearrange("p (j k n) -> p j k n", j=2, k=KT)
        out = []
        for j in range(2):
            half = slice(None) if len(steps[i]) == 2 else slice(4 * j, 4 * j + 4)
            t = steps[i][j % len(steps[i])]
            src = (t[2] if len(t) > 2 else w).rearrange("(k p) n -> p k n", p=P)
            out.append((raw[:, j % len(steps[i]), half, 0:t[1]], src[:, half, t[0]:t[0] + t[1]]))
        return out
    return parts


def project_rows(c, ring, x, w, col0, n_cols, tiles, out, after=None, beside=None):
    nc = c.nc
    hi, lo = x.hi, x.lo
    first_use = x.first_use()
    parts = rows_step(ring, w, col0, n_cols)
    done = 2 if ring.ahead else 0
    chunks = [(a, min(256, n_cols - a)) for a in range(0, n_cols, 256)]
    steps = []
    for t0 in range(0, len(tiles), 4):
        for a, m in chunks:
            steps.append((tiles[t0:t0 + 4], t0, a, m))
    s0 = c.step

    def bank(s, j):
        if first_use:
            return c.PS[:, 4 * (s % 2) + j, 0:256]
        return c.PS[:, 4 * (s % 2) + j // 2, (j % 2) * 256:(j % 2) * 256 + 256]

    with nc.Block() as block:
        @block.sync
        def _(sp):
            for i in range(done, len(steps)):
                ring.load(sp, s0 + i, (s0 + i) // 2, (s0 + i) % 2, parts(s0 + i, i))
            if beside:
                beside.loads.issue(sp)
            if after:
                ring.load_ahead(sp, s0 + len(steps), after)

        @block.scalar
        def _(act):
            if first_use:
                x.scalar(act, ring.round_second(act, s0))
            if beside:
                beside.squares(act)
            for i in range(2 if first_use else done // 2, len(steps)):
                s = s0 + i
                m = steps[i][3]
                act.wait_ge(ring.loaded[s % 2], (s // 2) * 32 + 32)
                act.wait_ge(ring.used, s + 1)
                raw, hi_, lo_ = ring.view(s % 2, "p (k n) -> p k n", k=KT)
                nc.scalar.activation(hi_[:, :, 0:m], raw[:, :, 0:m], ACT.Copy).then_inc(ring.rounded, 1)
                if beside and i == done // 2:
                    beside.roots(act)
            if after:
                s = s0 + len(steps)
                ring.round(act, s, s // 2, s % 2, RING_W)

        @block.vector
        def _(dve):
            ch = c.dve.on(dve)

            def evac(i):
                ts, t0, a, m = steps[i]
                s = s0 + i
                dve.wait_ge(ring.used, s + 3)
                for j in range(len(ts)):
                    last = nc.vector.tensor_copy(out[:, t0 + j, a:a + m], bank(s, j)[:, 0:m])
                last.then_inc(ring.drained, 1)

            if first_use:
                x.vector(dve, ch, ring.rest_second(dve, s0))
            for i in range(len(steps)):
                s = s0 + i
                m = steps[i][3]
                raw, hi_, lo_ = ring.view(s % 2, "p (k n) -> p k n", k=KT)
                if i >= (2 if first_use else done // 2):
                    dve.wait_ge(ring.rounded, s + 1)
                    nc.vector.tensor_tensor(lo_[:, :, 0:m], raw[:, :, 0:m], hi_[:, :, 0:m].bitcast(F32),
                                            ALU.subtract).then_inc(ring.split, 1)
                if i >= 1:
                    evac(i - 1)
                if beside:
                    beside.vector(dve, ch, i, len(steps))
            if after:
                s = s0 + len(steps)
                ring.rest(dve, s, s // 2, s % 2, RING_W)
            evac(len(steps) - 1)

        @block.tensor
        def _(pe):
            def products_of(i, k, js):
                ts, t0, a, m = steps[i]
                s = s0 + i
                _, whi, wlo = ring.view(s % 2, "p (k n) -> p k n", k=KT)
                for j in js:
                    tok = slice(ts[j] * P, (ts[j] + 1) * P)
                    for xt, wt, start in ((hi, whi, k == 0), (hi, wlo, False), (lo, whi, False)):
                        last = nc.tensor.matmul(bank(s, j)[:, 0:m], xt[:, k, tok], wt[:, k, 0:m], start=start,
                                                stop=(k == KT - 1 and xt is lo))
                return last

            def opening_products(i, k):
                pe.wait_ge(ring.split, s0 + i + 3)
                return products_of(i, k, range(len(steps[i][0])))

            if first_use:
                x.tensor(pe)
                opening(x, pe, opening_products, lambda i, last: last.then_inc(ring.used, 1))
            for i in range(2 if first_use else 0, len(steps)):
                pe.wait_ge(ring.split, s0 + i + 3)
                pe.wait_ge(ring.drained, s0 + i + 1)
                for j in range(len(steps[i][0])):
                    for k in range(KT):
                        last = products_of(i, k, [j])
                last.then_inc(ring.used, 1)
                if beside:
                    beside.tensor(pe, i)
    c.step += len(steps)
    ring.ahead = after is not None


def rotate(c, P1, QKT, dram):
    nc = c.nc
    tab_in = c.tally("tables_in")
    sq_done, rooted, raw_copied = c.tally("r_squared"), c.tally("r_rooted"), c.tally("r_raw_copied")
    summed, normed, crossed, rotated = c.tally("r_summed"), c.tally("r_normed"), c.tally("r_crossed"), c.tally("r_rotated")
    turned, moved = c.tally("r_turned"), c.tally("r_moved")
    all_t = [tab_in, sq_done, rooted, raw_copied, summed, normed, crossed, rotated, turned, moved]
    b = {t: t.n for t in all_t}
    n_bank = (N_ROT + 3) // 4
    segs = [(OFF[name], HEAD_AT[name], n) for name, n in ROTATED if name not in ("qi", "ki")]
    with scope(nc) as sb:
        gain = sb("rot_gain", [P, N_NORMED, HD])
        cos, sin = sb("rot_cos", [P, QT, HD]), sb("rot_sin", [P, QT, HD])
        sq = sb("rot_sq", [P, N_NORMED, HD])
        X = sb("rot_x", [P, 2, N_ROT, HD])
        A, B = sb("rot_a", [P, N_ROT, HD]), sb("rot_b", [P, N_ROT, HD])
        R = sb("rot_r", [P, 2, N_ROT, HD])
        ss, rt, inv = (sb("rot_" + x, [P, N_NORMED]) for x in ("ss", "rt", "inv"))
        with nc.Block() as block:
            @block.sync
            def _(sp):
                sp.dma_start(gain[:], dram["gain_rows"]).then_inc(tab_in.sem, 16)
                sp.dma_start(cos[:], dram["cos"]).then_inc(tab_in.sem, 16)
                sp.dma_start(sin[:], dram["sin"]).then_inc(tab_in.sem, 16)

            @block.scalar
            def _(act):
                def evac(n):
                    t, j = n // n_bank, n % n_bank
                    m = min(4, N_ROT - 4 * j)
                    act.wait_ge(turned.sem, b[turned] + n + 1)
                    nc.scalar.activation(QKT[:, 4 * j:4 * j + m, t * P:(t + 1) * P],
                                         c.PS[0:HD, n % 4, 0:m * P].rearrange("p (h t) -> p h t", h=m),
                                         ACT.Copy).then_inc(moved.sem, 1)

                def first(t):
                    if t >= 1:
                        act.wait_ge(summed.sem, b[summed] + t)
                    for col, h, n in segs:
                        last = nc.scalar.activation(sq[:, h:h + n, :],
                                                    P1[:, t, col:col + n * HD].rearrange("p (h d) -> p h d", h=n), ACT.Square)
                    last.then_inc(sq_done.sem, 1)
                    if t >= 2:
                        act.wait_ge(rotated.sem, b[rotated] + t - 1)
                    nc.scalar.activation(X[:, t % 2, N_NORMED:N_ROT, :],
                                         P1[:, t, OFF["qi"]:OFF["qi"] + 5 * HD].rearrange("p (h d) -> p h d", h=5),
                                         ACT.Copy).then_inc(raw_copied.sem, 1)
                    act.wait_ge(summed.sem, b[summed] + t + 1)
                    nc.scalar.activation(rt[:], ss[:], ACT.Sqrt, bias=c.eps[:], scale=1.0 / HD).then_inc(rooted.sem, 1)

                first(0)
                first(1)
                for t in range(QT):
                    if t + 2 < QT:
                        first(t + 2)
                    for j in range(n_bank):
                        evac(t * n_bank + j)

            @block.gpsimd
            def _(pool):
                pool.wait_ge(tab_in.sem, b[tab_in] + 48)
                for t in range(QT):
                    pool.wait_ge(normed.sem, b[normed] + t + 1)
                    pool.wait_ge(raw_copied.sem, b[raw_copied] + t + 1)
                    if t >= 1:
                        pool.wait_ge(rotated.sem, b[rotated] + t)
                    x = X[:, t % 2].rearrange("p h (a d) -> p h a d", a=2)
                    s = sin[:, t, :].rearrange("p (a d) -> p a d", a=2)
                    bb = B[:].rearrange("p h (a d) -> p h a d", a=2)
                    for a in range(2):
                        last = nc.gpsimd.tensor_tensor(bb[:, :, a, :], x[:, :, 1 - a, :],
                                                       s[:, None, a, :].to_broadcast([P, N_ROT, HD // 2]), ALU.mult)
                    last.then_inc(crossed.sem, 1)

            @block.vector
            def _(dve):
                ch = c.dve.on(dve)
                dve.wait_ge(tab_in.sem, b[tab_in] + 48)

                def normalise(t):
                    dve.wait_ge(sq_done.sem, b[sq_done] + t + 1)
                    if t >= 1:
                        dve.wait_ge(rooted.sem, b[rooted] + t)
                    nc.vector.reduce_sum(ss[:], sq[:], AX_X).then_inc(summed.sem, 1)
                    dve.wait_ge(rooted.sem, b[rooted] + t + 1)
                    ch.link(nc.vector.reciprocal(inv[:], rt[:]))
                    if t >= 2:
                        dve.wait_ge(rotated.sem, b[rotated] + t - 1)
                    for col, h, n in segs:
                        last = nc.vector.tensor_tensor(X[:, t % 2, h:h + n, :],
                                                       P1[:, t, col:col + n * HD].rearrange("p (h d) -> p h d", h=n),
                                                       inv[:, h:h + n, None].to_broadcast([P, n, HD]), ALU.mult)
                    ch.link(last)
                    nc.vector.tensor_tensor(X[:, t % 2, 0:N_NORMED, :], X[:, t % 2, 0:N_NORMED, :], gain[:],
                                            ALU.mult).then_inc(normed.sem, 1)

                def turn(t):
                    dve.wait_ge(normed.sem, b[normed] + t + 1)
                    dve.wait_ge(raw_copied.sem, b[raw_copied] + t + 1)
                    if t >= 1:
                        dve.wait_ge(rotated.sem, b[rotated] + t)
                    ch.link(nc.vector.tensor_tensor(A[:], X[:, t % 2], cos[:, t, None, :].to_broadcast([P, N_ROT, HD]), ALU.mult))
                    dve.wait_ge(crossed.sem, b[crossed] + t + 1)
                    if t >= 2:
                        dve.wait_ge(turned.sem, b[turned] + (t - 1) * n_bank)
                    nc.vector.tensor_tensor(R[:, t % 2], A[:], B[:], ALU.add).then_inc(rotated.sem, 1)

                normalise(0)
                for t in range(QT):
                    if t + 1 < QT:
                        normalise(t + 1)
                    turn(t)

            @block.tensor
            def _(pe):
                for t in range(QT):
                    pe.wait_ge(rotated.sem, b[rotated] + t + 1)
                    for j in range(n_bank):
                        n = t * n_bank + j
                        if n >= 4:
                            pe.wait_ge(moved.sem, b[moved] + n - 3)
                        for h in range(4 * j, min(4 * j + 4, N_ROT)):
                            last = nc.tensor.transpose(c.PS[0:HD, n % 4, (h % 4) * P:(h % 4 + 1) * P], R[:, t % 2, h, :], c.ident[:])
                        last.then_inc(turned.sem, 1)
    for t, d in ((tab_in, 48), (sq_done, QT), (rooted, QT), (raw_copied, QT), (summed, QT), (normed, QT), (crossed, QT),
                 (rotated, QT), (turned, QT * n_bank), (moved, QT * n_bank)):
        t.n += d


def compress(c, P1, kcmpT, vbd, dram):
    nc = c.nc
    w_in, small_in = c.tally("cmp_w_in"), c.tally("cmp_small_in")
    turned, moved, shifted, added = c.tally("cmp_turned"), c.tally("cmp_moved"), c.tally("cmp_shifted"), c.tally("cmp_added")
    hid_done, silu_done, rep_done, out_done = c.tally("cmp_hid"), c.tally("cmp_silu"), c.tally("cmp_repeated"), c.tally("cmp_out")
    rooted, summed, normed, kturned, kmoved = (c.tally("cmp_" + x) for x in ("rooted", "summed", "normed", "kturned", "kmoved"))
    NJ = CMP_BLOCK // 2
    HT = CMP_HIDDEN // P
    with scope(nc) as sb:
        w1 = sb("cmp_w1", [P, 2, NJ, CMP_HIDDEN])
        w2 = sb("cmp_w2", [P, 2, HT, HD])
        b1 = sb("cmp_b1", [P, 2, HT])
        pe_t = sb("cmp_pe", [P, 2, NJ])
        gain = sb("cmp_gain", [CMP_PAD, HD])
        cos, sin = sb("cmp_cos", [CMP_PAD, HD]), sb("cmp_sin", [CMP_PAD, HD])
        T = sb("cmp_t", [P, 2, SEQ])
        S = sb("cmp_s", [P, 2, GROUPS, SEQ])
        G = sb("cmp_g", [P, 2, NJ, GROUPS, CMP_PAD])
        hid = sb("cmp_hid_sb", [P, 2, HT, GROUPS, CMP_PAD])
        rep = sb("cmp_rep", [P, HT, GROUPS, PER_GROUP, CMP_PAD])
        kraw, sq, A, B, R = (sb("cmp_" + x, [CMP_PAD, GROUPS, HD]) for x in ("kraw", "sq", "a", "b", "r"))
        ss, rt, inv = (sb("cmp_" + x, [CMP_PAD, GROUPS]) for x in ("ss", "rt", "inv"))
        with nc.Block() as block:
            @block.sync
            def _(sp):
                for i, x in enumerate("kv"):
                    sp.dma_start(w1[:, i], dram[f"cmp_{x}_w1"].rearrange("(j p) n -> p j n", p=P)).then_inc(w_in.sem, 16)
                    sp.dma_start(w2[:, i], dram[f"cmp_{x}_w2"].rearrange("(j p) n -> p j n", p=P)).then_inc(w_in.sem, 16)
                    sp.dma_start(b1[:, i], dram[f"cmp_{x}_b1"]).then_inc(small_in.sem, 16)
                    sp.dma_start(pe_t[:, i], dram[f"cmp_pe_{x}"]).then_inc(small_in.sem, 16)
                sp.dma_start(gain[:], dram["kc_gain"]).then_inc(small_in.sem, 16)
                sp.dma_start(cos[:], dram["cmp_cos"]).then_inc(small_in.sem, 16)
                sp.dma_start(sin[:], dram["cmp_sin"]).then_inc(small_in.sem, 16)
                sp.wait_ge(moved.sem, 2)
                for i in range(2):
                    for g in range(GROUPS):
                        for par in range(2):
                            sp.dma_start(S[par * HD:(par + 1) * HD, i, g, 0:SEQ - par],
                                         T[g * HD:(g + 1) * HD, i, par:SEQ]).then_inc(shifted.sem, 16)

            @block.tensor
            def _(pe):
                for i, x in enumerate(("kc", "vc")):
                    for t in range(QT):
                        last = nc.tensor.transpose(c.PS[:, i, t * P:(t + 1) * P], P1[:, t, OFF[x]:OFF[x] + P], c.ident[:])
                    last.then_inc(turned.sem, 1)
                pe.wait_ge(added.sem, 5)
                pe.wait_ge(w_in.sem, 64)
                for i in range(2):
                    for ht in range(HT):
                        for j in range(NJ):
                            last = nc.tensor.matmul(c.PS[:, 2 + i, ht * 64:ht * 64 + 64], w1[:, i, j, ht * P:(ht + 1) * P],
                                                    G[:, i, j].rearrange("p g c -> p (g c)"), start=(j == 0), stop=(j == NJ - 1))
                    last.then_inc(hid_done.sem, 1)
                pe.wait_ge(silu_done.sem, 4)
                for g in range(GROUPS):
                    for ht in range(HT):
                        last = nc.tensor.matmul(c.PS[0:CMP_PAD, 4, g * HD:(g + 1) * HD], hid[:, 0, ht, g, :], w2[:, 0, ht, :],
                                                start=(ht == 0), stop=(ht == HT - 1))
                last.then_inc(out_done.sem, 1)
                pe.wait_ge(rep_done.sem, 1)
                for g in range(GROUPS):
                    for ht in range(HT):
                        last = nc.tensor.matmul(c.PS[:, 5, g * HD:(g + 1) * HD], rep[:, ht, g].rearrange("p r c -> p (r c)"),
                                                w2[:, 1, ht, :], start=(ht == 0), stop=(ht == HT - 1))
                last.then_inc(out_done.sem, 1)
                pe.wait_ge(normed.sem, 1)
                for g in range(GROUPS):
                    last = nc.tensor.transpose(c.PS[0:HD, 6, g * CMP_PAD:(g + 1) * CMP_PAD], R[:, g, :], c.ident[0:CMP_PAD, 0:CMP_PAD])
                last.then_inc(kturned.sem, 1)

            @block.scalar
            def _(act):
                ch = c.act.on(act)
                act.wait_ge(small_in.sem, 16 * 7)
                for i in range(2):
                    act.wait_ge(hid_done.sem, i + 1)
                    for ht in range(HT):
                        nc.scalar.activation(hid[:, i, ht].rearrange("p g c -> p (g c)"), c.PS[:, 2 + i, ht * 64:ht * 64 + 64],
                                             ACT.Silu, bias=b1[:, i, ht:ht + 1]).then_inc(silu_done.sem, 1)
                act.wait_ge(out_done.sem, 1)
                ch.link(nc.scalar.activation(sq[:].rearrange("p g d -> p (g d)"), c.PS[0:CMP_PAD, 4, 0:GROUPS * HD], ACT.Square))
                nc.scalar.activation(kraw[:].rearrange("p g d -> p (g d)"), c.PS[0:CMP_PAD, 4, 0:GROUPS * HD],
                                     ACT.Copy).then_inc(silu_done.sem, 1)
                act.wait_ge(summed.sem, 1)
                nc.scalar.activation(rt[:], ss[:], ACT.Sqrt, bias=c.eps[0:CMP_PAD], scale=1.0 / HD).then_inc(rooted.sem, 1)

            @block.vector
            def _(dve):
                ch = c.dve.on(dve)
                nc.vector.memset(G[:], 0.0).then_inc(added.sem, 1)
                ch.link(nc.vector.memset(vbd[:], 0.0))
                for i in range(2):
                    dve.wait_ge(turned.sem, i + 1)
                    nc.vector.tensor_copy(T[:, i, :], c.PS[:, i, :]).then_inc(moved.sem, 1)
                dve.wait_ge(added.sem, 1)
                dve.wait_ge(small_in.sem, 16 * 7)
                dve.wait_ge(shifted.sem, 16 * 8)
                for i in range(2):
                    for g in range(GROUPS):
                        for part in range(2):
                            src = S[:, i, g, part * CMP_STRIDE:part * CMP_STRIDE + N_CMP * CMP_STRIDE].rearrange(
                                "p (c j two) -> p j c two", c=N_CMP, two=2)[:, :, :, 0]
                            js = slice(part * 8, part * 8 + 8)
                            last = nc.vector.tensor_tensor(G[:, i, js, g, 0:N_CMP], src,
                                                           pe_t[:, i, js, None].to_broadcast([P, 8, N_CMP]), ALU.add)
                        last.then_inc(added.sem, 1)
                dve.wait_ge(silu_done.sem, 4)
                for ht in range(HT):
                    last = nc.vector.tensor_copy(rep[:, ht], hid[:, 1, ht, :, None, :].to_broadcast([P, GROUPS, PER_GROUP, CMP_PAD]))
                last.then_inc(rep_done.sem, 1)
                dve.wait_ge(silu_done.sem, 5)
                nc.vector.reduce_sum(ss[:], sq[:], AX_X).then_inc(summed.sem, 1)
                dve.wait_ge(rooted.sem, 1)
                ch.link(nc.vector.reciprocal(inv[:], rt[:]))
                ch.link(nc.vector.tensor_tensor(kraw[:], kraw[:], inv[:, :, None].to_broadcast([CMP_PAD, GROUPS, HD]), ALU.mult))
                ch.link(nc.vector.tensor_tensor(kraw[:], kraw[:], gain[:, None, :].to_broadcast([CMP_PAD, GROUPS, HD]), ALU.mult))
                nc.vector.tensor_tensor(A[:], kraw[:], cos[:, None, :].to_broadcast([CMP_PAD, GROUPS, HD]), ALU.mult)
                for a in range(2):
                    lo, hi = a * 32, a * 32 + 32
                    last = nc.vector.tensor_tensor(B[:, :, lo:hi], kraw[:, :, 32 - lo:64 - lo],
                                                   sin[:, None, lo:hi].to_broadcast([CMP_PAD, GROUPS, 32]), ALU.mult)
                ch.link(last)
                nc.vector.tensor_tensor(R[:], A[:], B[:], ALU.add).then_inc(normed.sem, 1)
                dve.wait_ge(out_done.sem, 2)
                for g in range(GROUPS):
                    for h in range(PER_GROUP):
                        rows = slice(h * CMP_PAD, (h + 1) * CMP_PAD)
                        nc.vector.tensor_copy(vbd[rows, g, h * HD:(h + 1) * HD], c.PS[rows, 5, g * HD:(g + 1) * HD])
                dve.wait_ge(kturned.sem, 1)
                ch.link(nc.vector.tensor_copy(kcmpT[:].rearrange("p g c -> p (g c)"), c.PS[0:HD, 6, 0:GROUPS * CMP_PAD]))


def gate_and_compressed(c, P1, QKT, kcmpT, vbd, gates, dram):
    nc = c.nc
    mask_in, sig, scored, masked, shifted, expd = (c.tally("cb_" + x) for x in ("mask_in", "sig", "scored", "masked", "shifted", "expd"))
    weighed, turned, moved, out = (c.tally("cb_" + x) for x in ("weighed", "turned", "moved", "out"))
    score_banks, turn_banks, out_banks = (0, 1, 2, 3), (4, 5), (6, 7, 0, 1)
    with scope(nc) as sb:
        neg = sb("cb_neg", [P, QT, CMP_PAD])
        one = sb("cb_one", [P, QT, CMP_PAD])
        S = sb("cb_s", [P, QT * HEADS, CMP_PAD])
        E = sb("cb_e", [P, QT * HEADS, CMP_PAD])
        PT = sb("cb_pt", [P, QT, GROUPS * P])
        mx, co = (sb("cb_" + x, [P, QT * HEADS]) for x in ("mx", "co"))
        heads = lambda x, t: x[:, t * HEADS:(t + 1) * HEADS]
        with nc.Block() as block:
            @block.sync
            def _(sp):
                sp.dma_start(neg[:], dram["cmp_neg"]).then_inc(mask_in.sem, 16)
                sp.dma_start(one[:], dram["cmp_one"]).then_inc(mask_in.sem, 16)

            @block.tensor
            def _(pe):
                for t in range(QT):
                    for h in range(HEADS):
                        last = nc.tensor.matmul(c.PS[:, score_banks[t], h * CMP_PAD:(h + 1) * CMP_PAD],
                                                QKT[:, HEAD_AT["q_n"] + h, t * P:(t + 1) * P], kcmpT[:, h // PER_GROUP, :],
                                                start=True, stop=True)
                    last.then_inc(scored.sem, 1)
                for t in range(QT):
                    pe.wait_ge(weighed.sem, t + 1)
                    for g in range(GROUPS):
                        last = nc.tensor.transpose(c.PS[:, turn_banks[t // 2], (t % 2) * 256 + g * P:(t % 2) * 256 + (g + 1) * P],
                                                   heads(E, t)[:, 4 * g:4 * g + 4, :].rearrange("p h c -> p (h c)"), c.ident[:])
                    last.then_inc(turned.sem, 1)
                for t in range(QT):
                    pe.wait_ge(moved.sem, t // 2 + 1)
                    for g in range(GROUPS):
                        last = nc.tensor.matmul(c.PS[:, out_banks[t], g * 256:(g + 1) * 256], PT[:, t, g * P:(g + 1) * P], vbd[:, g, :],
                                                start=True, stop=True)
                    last.then_inc(out.sem, 1)

            @block.scalar
            def _(act):
                nc.scalar.activation(gates[:], P1[:, :, OFF["gate"]:OFF["gate"] + 3 * HEADS], ACT.Sigmoid).then_inc(sig.sem, 1)
                act.wait_ge(shifted.sem, 1)
                nc.scalar.activation(E[:], S[:], ACT.Exp, scale=SCALE).then_inc(expd.sem, 1)
                for z in ("z_n", "z_d"):
                    nc.scalar.activation(P1[:, :, OFF[z]:OFF[z] + 512], P1[:, :, OFF[z]:OFF[z] + 512], ACT.Silu)

            @block.vector
            def _(dve):
                ch = c.dve.on(dve)
                dve.wait_ge(mask_in.sem, 32)
                for t in range(QT):
                    dve.wait_ge(scored.sem, t + 1)
                    nc.vector.tensor_tensor(heads(S, t), c.PS[:, score_banks[t], 0:HEADS * CMP_PAD].rearrange("p (h c) -> p h c", h=HEADS),
                                            neg[:, t, None, :].to_broadcast([P, HEADS, CMP_PAD]), ALU.add).then_inc(masked.sem, 1)
                dve.wait_ge(masked.sem, QT)
                ch.link(nc.vector.reduce_max(mx[:], S[:], AX_X))
                nc.vector.tensor_tensor(S[:], S[:], mx[:, :, None].to_broadcast([P, QT * HEADS, CMP_PAD]),
                                        ALU.subtract).then_inc(shifted.sem, 1)
                dve.wait_ge(expd.sem, 1)
                ch.link(nc.vector.reduce_sum(co[:], E[:], AX_X))
                for t in range(QT):
                    nc.vector.tensor_tensor(heads(E, t), heads(E, t), one[:, t, None, :].to_broadcast([P, HEADS, CMP_PAD]),
                                            ALU.mult).then_inc(weighed.sem, 1)
                ch.link(nc.vector.reciprocal(co[:], co[:]))
                dve.wait_ge(sig.sem, 1)
                co_t = co[:].rearrange("p (t h) -> p t h", t=QT)
                ch.link(nc.vector.tensor_tensor(co_t, co_t, gates[:].rearrange("p t (h b) -> p t h b", b=3)[:, :, :, 0], ALU.mult))
                for i in range(QT // 2):
                    dve.wait_ge(turned.sem, 2 * i + 2)
                    nc.vector.tensor_copy(PT[:, 2 * i:2 * i + 2].rearrange("p t q -> p (t q)"), c.PS[:, turn_banks[i], :]).then_inc(moved.sem, 1)
                for t in range(QT):
                    dve.wait_ge(out.sem, t + 1)
                    nc.vector.tensor_tensor(P1[:, t, OFF["q_n"]:OFF["q_n"] + 512].rearrange("p (h d) -> p h d", h=HEADS),
                                            c.PS[:, out_banks[t], :].rearrange("p (h d) -> p h d", h=HEADS),
                                            co_t[:, t, :, None].to_broadcast([P, HEADS, HD]), ALU.mult)


def index_scores(c, P1, QKT, scores, tri, sc_at, dram):
    nc = c.nc
    tri_in, scored, relu, added = (c.tally("ix_" + x) for x in ("tri_in", "scored", "relu", "added"))
    items = [(t, h) for t in range(1, QT) for h in range(IDX_HEADS)]
    with scope(nc) as sb:
        R = sb("ix_r", [P, 2, SEQ])
        wi = sb("ix_w", [P, QT, IDX_HEADS])
        with nc.Block() as block:
            @block.sync
            def _(sp):
                sp.dma_start(tri[:], dram["tri"]).then_inc(tri_in.sem, 16)

            @block.tensor
            def _(pe):
                for n, (t, h) in enumerate(items):
                    if n >= 4:
                        pe.wait_ge(relu.sem, n - 3)
                    keys = (t + 1) * P
                    nc.tensor.matmul(c.PS[:, n % 4, 0:keys], QKT[:, HEAD_AT["qi"] + h, t * P:(t + 1) * P],
                                     QKT[:, HEAD_AT["ki"], 0:keys], start=True, stop=True).then_inc(scored.sem, 1)

            @block.scalar
            def _(act):
                for n, (t, h) in enumerate(items):
                    act.wait_ge(scored.sem, n + 1)
                    if n >= 2:
                        act.wait_ge(added.sem, n - 1)
                    keys = (t + 1) * P
                    nc.scalar.activation(R[:, n % 2, 0:keys], c.PS[:, n % 4, 0:keys], ACT.Relu, scale=HD ** -0.5).then_inc(relu.sem, 1)

            @block.vector
            def _(dve):
                ch = c.dve.on(dve)
                ch.link(nc.vector.tensor_scalar(wi[:], P1[:, :, OFF["wi"]:OFF["wi"] + IDX_HEADS], IDX_HEADS ** -0.5, None, ALU.mult))
                dve.wait_ge(tri_in.sem, 16)
                for n, (t, h) in enumerate(items):
                    keys = (t + 1) * P
                    dst = scores[:, sc_at[t]:sc_at[t] + keys]
                    prev = tri[:, SEQ - keys:SEQ] if h == 0 else dst
                    dve.wait_ge(relu.sem, n + 1)
                    if h > 0:
                        dve.wait_ge(added.sem, n)
                    nc.vector.scalar_tensor_tensor(dst, R[:, n % 2, 0:keys], wi[:, t, h:h + 1], prev, ALU.mult,
                                                   ALU.add).then_inc(added.sem, 1)


class Unit:

    def __init__(self, q, k, v, mask, group, at, scale, needs=0):
        self.q, self.k, self.v, self.mask, self.group, self.at, self.scale = q, k, v, mask, group, at, scale
        self.needs = needs
        self.keys = P * len(v)
        self.pieces = [(a, min(4, len(v) - a)) for a in range(0, len(v), 4)]


def attend(c, sb, tag, units, s_banks, pt_banks, out_banks, finish, between=None, chosen=None, extra=None):
    nc = c.nc
    names = ["scored", "masked", "expd", "turned", "weighed", "drained"]
    scored, masked, expd, turned, weighed, drained = (c.tally("at_" + x) for x in names)
    b = {t: t.n for t in (scored, masked, expd, turned, weighed, drained)}
    moved = [c.tally("at_moved_even"), c.tally("at_moved_odd")]
    bm = [t.n for t in moved]
    most = max(u.keys for u in units)
    S = sb("at_s_" + tag, [P, 2, most])
    E = sb("at_e_" + tag, [P, 3, most])
    NPT = len(pt_banks)
    PT = sb("at_pt_" + tag, [P, NPT, 512])
    mx, rs = sb("at_mx_" + tag, [P, len(units)]), sb("at_rs_" + tag, [P, len(units)])
    first = [0]
    for u in units:
        first.append(first[-1] + len(u.pieces))
    pieces = [(i, a, n) for i, u in enumerate(units) for a, n in u.pieces]
    ends = {u.group: i for i, u in enumerate(units)}

    def s_ps(i, lo, hi):
        return c.PS[:].rearrange("p b n -> p (b n)")[:, s_banks[i % 2] * 512 + lo:s_banks[i % 2] * 512 + hi]

    with nc.Block() as block:
        @block.sync
        def _(sp):
            if extra:
                extra.load(sp)

        @block.gpsimd
        def _(pool):
            if extra:
                extra.gpsimd(pool)

        @block.tensor
        def _(pe):
            def score(i):
                u = units[i]
                if i >= 2:
                    pe.wait_ge(masked.sem, b[masked] + i - 1)
                for lo in range(0, u.keys, 512):
                    hi = min(u.keys, lo + 512)
                    last = nc.tensor.matmul(s_ps(i, lo, hi), u.q, u.k(lo, hi), start=True, stop=True)
                last.then_inc(scored.sem, 1)

            def turn(p):
                i, a, n = pieces[p]
                pe.wait_ge(expd.sem, b[expd] + i + 1)
                if p >= NPT:
                    pe.wait_ge(moved[(p - NPT) % 2].sem, bm[(p - NPT) % 2] + (p - NPT) // 2 + 1)
                for j in range(n):
                    last = nc.tensor.transpose(c.PS[:, pt_banks[p % NPT], j * P:(j + 1) * P], E[:, i % 3, (a + j) * P:(a + j + 1) * P],
                                               c.ident[:])
                last.then_inc(turned.sem, 1)

            def weigh(p):
                i, a, n = pieces[p]
                u = units[i]
                pe.wait_ge(moved[p % 2].sem, bm[p % 2] + p // 2 + 1)
                n_out = len(out_banks)
                if u.group >= n_out and (i == 0 or units[i - 1].group != u.group) and a == 0:
                    pe.wait_ge(drained.sem, b[drained] + u.group - n_out + 1)
                bank = out_banks[u.group % n_out]
                width = u.v[a].shape[1]
                for j in range(n):
                    last = nc.tensor.matmul(c.PS[:, bank, u.at:u.at + width], PT[:, p % NPT, j * P:(j + 1) * P], u.v[a + j],
                                            start=(a + j == 0), stop=(a + j == len(u.v) - 1))
                last.then_inc(weighed.sem, 1)

            score(0)
            score(1)
            for i in range(len(units)):
                if i + 2 < len(units):
                    score(i + 2)
                for p in range(first[i], first[i + 1]):
                    turn(p)
                    if p >= 2:
                        weigh(p - 2)
                if extra:
                    extra.tensor(pe, i)
            weigh(len(pieces) - 2)
            weigh(len(pieces) - 1)
            if extra:
                extra.tensor(pe, len(units))

        @block.scalar
        def _(act):
            def exp(i):
                u = units[i]
                act.wait_ge(masked.sem, b[masked] + i + 1)
                if i >= 3:
                    act.wait_ge(turned.sem, b[turned] + first[i - 2])
                nc.scalar.activation(E[:, i % 3, 0:u.keys], S[:, i % 2, 0:u.keys], ACT.Exp, bias=mx[:, i:i + 1], scale=-1.0,
                                     accum_out=rs[:, i:i + 1]).then_inc(expd.sem, 1)

            def move(p):
                i, a, n = pieces[p]
                act.wait_ge(turned.sem, b[turned] + p + 1)
                if p >= NPT:
                    act.wait_ge(weighed.sem, b[weighed] + p - NPT + 1)
                nc.scalar.activation(PT[:, p % NPT, 0:n * P], c.PS[:, pt_banks[p % NPT], 0:n * P], ACT.Copy
                                     ).then_inc(moved[p % 2].sem, 1)

            exp(0)
            exp(1)
            for i in range(len(units)):
                for p in range(first[i], first[i + 1]):
                    if p % 2 == 0:
                        move(p)
                if extra:
                    extra.scalar(act, i)
                if i + 2 < len(units):
                    exp(i + 2)

        @block.vector
        def _(dve):
            ch = c.dve.on(dve)

            def mask(i):
                u = units[i]
                dve.wait_ge(scored.sem, b[scored] + i + 1)
                if i >= 2:
                    dve.wait_ge(expd.sem, b[expd] + i - 1)
                if u.mask is None:
                    nc.vector.tensor_scalar(S[:, i % 2, 0:u.keys], s_ps(i, 0, u.keys), -u.scale, None, ALU.mult, ALU.min,
                                            accum_out=mx[:, i:i + 1]).then_inc(masked.sem, 1)
                else:
                    if u.needs:
                        ch.wait(chosen[u.needs])
                    nc.vector.tensor_tensor_reduce(S[:, i % 2, 0:u.keys], s_ps(i, 0, u.keys), u.mask, -u.scale, 3e38,
                                                   ALU.add, ALU.min, mx[:, i:i + 1]).then_inc(masked.sem, 1)

            def move(p):
                i, a, n = pieces[p]
                dve.wait_ge(turned.sem, b[turned] + p + 1)
                if p >= NPT:
                    dve.wait_ge(weighed.sem, b[weighed] + p - NPT + 1)
                nc.vector.tensor_copy(PT[:, p % NPT, 0:n * P], c.PS[:, pt_banks[p % NPT], 0:n * P]).then_inc(moved[p % 2].sem, 1)

            mask(0)
            mask(1)
            for i in range(len(units)):
                for p in range(first[i], first[i + 1]):
                    if p % 2 == 1:
                        move(p)
                needed = i + 2 < len(units) and units[i + 2].needs
                if between and needed:
                    between(ch, i)
                if i + 2 < len(units):
                    mask(i + 2)
                if between and not needed:
                    between(ch, i)
                g = units[i - 1].group
                if i >= 1 and units[i - 1].group != units[i].group:
                    dve.wait_ge(weighed.sem, b[weighed] + first[ends[g] + 1])
                    finish(ch, g, rs, drained)
                if extra:
                    extra.vector(dve, i)
            g = units[-1].group
            dve.wait_ge(weighed.sem, b[weighed] + len(pieces))
            finish(ch, g, rs, drained)
            if extra:
                extra.copy_out(dve, LAYERS - 1)
    n_groups = units[-1].group + 1
    for t, d in ((scored, len(units)), (masked, len(units)), (expd, len(units)), (turned, len(pieces)),
                 (moved[0], (len(pieces) + 1) // 2), (moved[1], len(pieces) // 2), (weighed, len(pieces)), (drained, n_groups)):
        t.n += d


def project_cols(c, ring, x, w, tiles, spans, drain, after=None, wide=None):
    nc = c.nc
    hi, lo = x.hi, x.lo
    first_use = x.first_use()
    parts = cols_step(ring, w, tiles)
    done = 2 if ring.ahead else 0
    steps = [tiles[i:i + 2] for i in range(0, len(tiles), 2)]
    s0 = c.step
    wide = len(tiles) if wide is None else wide

    def spans_of(i, j):
        return spans if 2 * i + j < wide else spans[:1]

    def ps(s, j, n, width):
        a, e = spans[n]
        return c.PS[0:width, 4 * (s % 2) + 2 * j + n, 0:e - a]

    def views(s, j):
        return tuple(t[:, s % 2, :].rearrange("p (j k n) -> p j k n", j=2, k=KT)[:, j] for t in (ring.raw, ring.hi, ring.lo))

    with nc.Block() as block:
        @block.sync
        def _(sp):
            for i in range(done, len(steps)):
                ring.load(sp, s0 + i, (s0 + i) // 2, (s0 + i) % 2, parts(s0 + i, i))
            if after:
                ring.load_ahead(sp, s0 + len(steps), after)

        @block.scalar
        def _(act):
            if first_use:
                x.scalar(act, ring.round_second(act, s0))
            for i, step in list(enumerate(steps))[2 if first_use else done // 2:]:
                s = s0 + i
                act.wait_ge(ring.loaded[s % 2], (s // 2) * 32 + 32)
                act.wait_ge(ring.used, s + 1)
                for j, (_, width, *_) in enumerate(step):
                    raw, whi, _ = views(s, j)
                    last = nc.scalar.activation(whi[:, :, 0:width], raw[:, :, 0:width], ACT.Copy)
                last.then_inc(ring.rounded, 1)
            if after:
                s = s0 + len(steps)
                ring.round(act, s, s // 2, s % 2, RING_W)

        @block.vector
        def _(dve):
            ch = c.dve.on(dve)

            def evac(i):
                dve.wait_ge(ring.used, s0 + i + 3)
                for j, tile in enumerate(steps[i]):
                    for n in range(len(spans_of(i, j))):
                        last = drain(dve, ch, 2 * i + j, n, ps(s0 + i, j, n, tile[1]))
                last.then_inc(ring.drained, 1)

            if first_use:
                x.vector(dve, ch, ring.rest_second(dve, s0))
            for i, step in enumerate(steps):
                s = s0 + i
                if i >= (2 if first_use else done // 2):
                    dve.wait_ge(ring.rounded, s + 1)
                    for j, (_, width, *_) in enumerate(step):
                        raw, whi, wlo = views(s, j)
                        last = nc.vector.tensor_tensor(wlo[:, :, 0:width], raw[:, :, 0:width], whi[:, :, 0:width].bitcast(F32),
                                                       ALU.subtract)
                    last.then_inc(ring.split, 1)
                if i >= 1:
                    evac(i - 1)
            if after:
                s = s0 + len(steps)
                ring.rest(dve, s, s // 2, s % 2, RING_W)
            evac(len(steps) - 1)

        @block.tensor
        def _(pe):
            def products_of(i, k):
                s = s0 + i
                pe.wait_ge(ring.split, s + 3)
                for j, (_, width, *_) in enumerate(steps[i]):
                    _, whi, wlo = views(s, j)
                    for wt, xt, first, end in ((whi, hi, k == 0, False), (whi, lo, False, False), (wlo, hi, False, k == KT - 1)):
                        for n, (a, e) in enumerate(spans_of(i, j)):
                            last = nc.tensor.matmul(ps(s, j, n, width), wt[:, k, 0:width], xt[:, k, a:e], start=first, stop=end)
                return last

            if first_use:
                x.tensor(pe)
                opening(x, pe, products_of, lambda i, last: last.then_inc(ring.used, 1))
            for i in range(2 if first_use else 0, len(steps)):
                pe.wait_ge(ring.drained, s0 + i + 1)
                for k in range(KT):
                    last = products_of(i, k)
                last.then_inc(ring.used, 1)
    c.step += len(steps)
    ring.ahead = after is not None


def attend_first(c, P1, QKT, scores, sc_at, tri, gates, sb, extra=None):
    nc = c.nc
    units, groups = [], []
    for t in range(QT):
        for kname, vname, gate in (("ks", "vs", 1), ("kw", "vw", 2)):
            for h in range(HEADS):
                g = h // PER_GROUP
                units.append(Unit(QKT[:, HEAD_AT["q_n"] + h, t * P:(t + 1) * P],
                                  lambda lo, hi, kh=HEAD_AT[kname] + g: QKT[:, kh, lo:hi],
                                  [P1[:, kt, OFF[vname] + g * HD:OFF[vname] + g * HD + (HD if h == HEADS - 1 else 2 * HD)] for kt in range(t + 1)],
                                  tri[:, SEQ - (t + 1) * P:SEQ], len(groups), h * HD, SCALE))
            groups.append((t, gate))
    n_before = len(units)
    for t in range(QT):
        mask = tri[:, SEQ - P:SEQ] if t == 0 else scores[:, sc_at[t]:sc_at[t] + (t + 1) * P]
        for h in range(HEADS):
            g = h // PER_GROUP
            units.append(Unit(QKT[:, HEAD_AT["q_d"] + h, t * P:(t + 1) * P],
                              lambda lo, hi, kh=HEAD_AT["k_d"] + g: QKT[:, kh, lo:hi],
                              [P1[:, kt, OFF["v_d"] + g * HD:OFF["v_d"] + g * HD + (HD if h == HEADS - 1 else 2 * HD)] for kt in range(t + 1)],
                              mask, len(groups), h * HD, SCALE, needs=t))
        groups.append((t, 0))
    top = sb("top", [P, 8])
    co = sb("co", [P, HEADS])
    tmp = sb("o_tmp", [P, HEADS, HD])
    chosen = {}
    rounds = [(t, r) for t in range(1, QT) for r in range(TOPK // 8)]

    def between(ch, i):
        if i >= len(rounds):
            return
        t, r = rounds[i]
        s = scores[:, sc_at[t]:sc_at[t] + (t + 1) * P]
        ch.link(nc.vector.max(top[:], s))
        ch.link(nc.vector.match_replace(s, top[:], s, TAKEN))
        if r == TOPK // 8 - 1:
            chosen[t] = ch.mark(nc.vector.tensor_scalar(s, s, TAKEN_LIMIT, NEG, ALU.is_ge, ALU.mult))

    def finish(ch, g, rs, drained):
        t, gate = groups[g]
        ps = c.PS[:, 6 + g % 2, :].rearrange("p (h d) -> p h d", h=HEADS)
        at, z_at = (OFF["q_n"], OFF["z_n"]) if gate else (OFF["q_d"], OFF["z_d"])
        dst = P1[:, t, at:at + 512].rearrange("p (h d) -> p h d", h=HEADS)
        z = P1[:, t, z_at:z_at + 512].rearrange("p (h d) -> p h d", h=HEADS)
        ch.link(nc.vector.reciprocal(co[:], rs[:, 8 * g:8 * g + 8]))
        if gate:
            ch.link(nc.vector.tensor_tensor(co[:], co[:], gates[:, t].rearrange("p (h b) -> p h b", b=3)[:, :, gate], ALU.mult))
        n = drained.n + g + 1
        nc.vector.tensor_tensor(tmp[:], ps, co[:, :, None].to_broadcast([P, HEADS, HD]), ALU.mult).then_inc(drained.sem, 1)
        ch.eng.wait_ge(drained.sem, n)
        if gate:
            ch.link(nc.vector.tensor_tensor(dst, dst, tmp[:], ALU.add))
            if gate == 2:
                ch.link(nc.vector.tensor_tensor(dst, dst, z, ALU.mult))
        else:
            ch.link(nc.vector.tensor_tensor(dst, tmp[:], z, ALU.mult))

    if len(rounds) > n_before - 2:
        raise ValueError("the rounds of the top-k end before the indexed units")
    attend(c, sb, "1", units, [0, 1], [2, 4, 5], [6, 7], finish, between, chosen, extra)


def turn_rows(c, tiles, n_tok_tiles, out, ring=None, after=None):
    nc = c.nc
    turned, rounded, split = c.tally("tr_turned"), c.tally("tr_rounded"), c.tally("tr_split")
    b = {t: t.n for t in (turned, rounded, split)}
    items = [(j, a, min(a + 4, n_tok_tiles)) for j in range(len(tiles)) for a in range(0, n_tok_tiles, 4)]
    with nc.Block() as block:
        @block.sync
        def _(sp):
            if after:
                ring.load_ahead(sp, c.step, after)

        @block.tensor
        def _(pe):
            for n, (j, a, e) in enumerate(items):
                if n >= 4:
                    pe.wait_ge(split.sem, b[split] + n - 3)
                for t in range(a, e):
                    last = nc.tensor.transpose(c.PS[:, n % 4, (t - a) * P:(t - a + 1) * P], tiles[j](t), c.ident[:])
                last.then_inc(turned.sem, 1)

        @block.scalar
        def _(act):
            for n, (j, a, e) in enumerate(items):
                dst = out(j, a * P, e * P)
                if len(dst) == 2:
                    act.wait_ge(turned.sem, b[turned] + n + 1)
                    nc.scalar.activation(dst[0], c.PS[:, n % 4, 0:(e - a) * P], ACT.Copy).then_inc(rounded.sem, 1)
            if after:
                ring.round(act, c.step, c.step // 2, c.step % 2, RING_W)

        @block.vector
        def _(dve):
            for n, (j, a, e) in enumerate(items):
                dst = out(j, a * P, e * P)
                if len(dst) == 2:
                    dve.wait_ge(rounded.sem, b[rounded] + n + 1)
                    nc.vector.tensor_tensor(dst[1], c.PS[:, n % 4, 0:(e - a) * P], dst[0].bitcast(F32),
                                            ALU.subtract).then_inc(split.sem, 1)
                else:
                    dve.wait_ge(turned.sem, b[turned] + n + 1)
                    nc.vector.tensor_copy(dst[0], c.PS[:, n % 4, 0:(e - a) * P]).then_inc(split.sem, 1)
            if after:
                ring.rest(dve, c.step, 0, c.step % 2, RING_W)
                ring.ahead = True
    turned.n += len(items)
    split.n += len(items)
    if len(out(0, 0, P)) == 2:
        rounded.n += len(items)


class Adaptive:
    SLOTS = 3
    RAW_SLOTS = 5
    POOL_EVERY = 3
    KTS = 2
    PARTS = KT // KTS
    GROUPS = N_MOD * D // 512
    ROWS = 4 * GROUPS

    def __init__(self, c, sb, w_ada, s_c, bank, results):
        self.nc, self.c, self.s_c, self.bank, self.results = c.nc, c, s_c, bank, results
        self.w = w_ada.rearrange("l (h k p) (g m n) -> l g h p k m n", p=P, k=self.KTS, m=2, n=CTX)
        own = sb("ada_raw", [P, self.RAW_SLOTS - 2, self.KTS, 2, CTX])
        self.raw = [own[:, i] for i in range(self.RAW_SLOTS - 2)] + [
            c.hT[:, 4 * i:4 * i + 4, SEQ:TOK].rearrange("p (k m) n -> p k m n", m=2) for i in range(2)]
        self.hi, self.lo = (sb("ada_" + x, [P, self.SLOTS, self.KTS, 512], F32R) for x in ("hi", "lo"))
        self.loaded = [c.tally(f"ada_loaded{i}").sem for i in range(self.RAW_SLOTS)]
        self.rounded, self.used = (c.tally("ada_" + x).sem for x in ("rounded", "used"))
        self.split = [c.tally(f"ada_split{i}").sem for i in range(self.SLOTS)]
        self.copied = c.tally("ada_copied").sem
        self.per_layer = self.PARTS * self.GROUPS
        self.n = LAYERS * self.per_layer
        self.units = 1

    def steps(self, u):
        return range(self.n * u // self.units, self.n * (u + 1) // self.units) if u >= 0 else range(0)

    def half_columns(self, x, n):
        return x[:, n % self.SLOTS].rearrange("p k (m n) -> p k m n", m=2)

    def load(self, sp):
        for n in range(self.n):
            q = n % self.RAW_SLOTS
            if n >= self.RAW_SLOTS:
                was = n - self.RAW_SLOTS
                sp.wait_ge(self.split[was % self.SLOTS], was // self.SLOTS + 1)
            src = self.w[n // self.per_layer, n // self.PARTS % self.GROUPS, n % self.PARTS]
            for k in range(self.KTS):
                sp.dma_start(self.raw[q][:, k], src[:, k]).then_inc(self.loaded[q], 16)

    def scalar(self, act, u):
        for n in self.steps(u):
            q = n % self.RAW_SLOTS
            act.wait_ge(self.loaded[q], 16 * self.KTS * (n // self.RAW_SLOTS + 1))
            if n >= self.SLOTS:
                act.wait_ge(self.used, n - self.SLOTS + 1)
            self.nc.scalar.activation(self.half_columns(self.hi, n), self.raw[q], ACT.Copy).then_inc(self.rounded, 1)

    def by_pool(self, n):
        return n % self.POOL_EVERY == self.POOL_EVERY - 1

    def split_step(self, eng, ops, n):
        eng.wait_ge(self.rounded, n + 1)
        ops.tensor_tensor(self.half_columns(self.lo, n), self.raw[n % self.RAW_SLOTS], self.half_columns(self.hi, n).bitcast(F32),
                          ALU.subtract).then_inc(self.split[n % self.SLOTS], 1)

    def vector(self, dve, u):
        for n in self.steps(u):
            if not self.by_pool(n):
                self.split_step(dve, self.nc.vector, n)
            if n % self.per_layer == 0 and n > 0:
                self.copy_out(dve, n // self.per_layer - 1)

    def gpsimd(self, pool):
        for n in range(self.n):
            if self.by_pool(n):
                self.split_step(pool, self.nc.gpsimd, n)

    def copy_out(self, dve, l):
        dve.wait_ge(self.used, self.per_layer * (l + 1))
        self.nc.vector.tensor_copy(self.results[0:self.ROWS, l], self.c.PS[0:self.ROWS, self.bank, :]).then_inc(self.copied, 1)

    def tensor(self, pe, u):
        for n in self.steps(u - 1):
            l, m = n // self.per_layer, n % self.per_layer
            g, h = m // self.PARTS, m % self.PARTS
            pe.wait_ge(self.split[n % self.SLOTS], n // self.SLOTS + 1)
            if m == 0 and l > 0:
                pe.wait_ge(self.copied, l)
            first = self.ROWS - 4 - 4 * g
            for k in range(self.KTS):
                st = self.s_c[:, h * self.KTS + k, first:first + self.ROWS]
                for w in (self.hi, self.lo):
                    last = self.nc.tensor.matmul(self.c.PS[0:self.ROWS, self.bank, :], st, w[:, n % self.SLOTS, k], start=(m == 0 and k == 0 and w is self.hi),
                                                 stop=(m == self.per_layer - 1 and k == self.KTS - 1 and w is self.lo))
            last.then_inc(self.used, 1)


S_C_COLS = 2 * Adaptive.ROWS - 4


def silu_conditions(c, s_c, dram):
    nc = c.nc
    c_in, cleared, rounded = c.tally("cond_in"), c.tally("cond_cleared"), c.tally("cond_rounded")
    with scope(nc) as tmp:
        raw, zero = tmp("cond_raw", [P, KT, 2]), tmp("cond_zero", [P, KT, S_C_COLS])
        parts = s_c[:, :, Adaptive.ROWS - 4:Adaptive.ROWS].rearrange("p k (v part) -> p k v part", part=2)
        with nc.Block() as block:
            @block.sync
            def _(sp):
                sp.dma_start(raw[:], dram["conditions"]).then_inc(c_in.sem, 16)

            @block.vector
            def _(dve):
                ch = c.dve.on(dve)
                ch.link(nc.vector.memset(zero[:], 0.0))
                nc.vector.tensor_copy(s_c[:], zero[:]).then_inc(cleared.sem, 1)
                dve.wait_ge(rounded.sem, 2)
                nc.vector.tensor_tensor(parts[:, :, :, 1], raw[:], parts[:, :, :, 0].bitcast(F32), ALU.subtract)

            @block.scalar
            def _(act):
                act.wait_ge(c_in.sem, 16)
                nc.scalar.activation(raw[:], raw[:], ACT.Silu).then_inc(rounded.sem, 1)
                act.wait_ge(rounded.sem, 1)
                act.wait_ge(cleared.sem, 1)
                nc.scalar.activation(parts[:, :, :, 0], raw[:], ACT.Copy).then_inc(rounded.sem, 1)


def finish_adaptive(c, results, dram):
    nc = c.nc
    small, turned = c.tally("ada_small_in"), c.tally("ada_turned")
    rows = Adaptive.ROWS
    with scope(nc) as sb:
        bias = sb("b_ada", [P, LAYERS, N_MOD * KT])
        gains = sb("layer_gains", [P, LAYERS, 3, KT])
        with nc.Block() as block:
            @block.sync
            def _(sp):
                sp.dma_start(bias[:], dram["b_ada"]).then_inc(small.sem, 16)
                sp.dma_start(gains[:], dram["layer_gains"]).then_inc(small.sem, 16)

            @block.tensor
            def _(pe):
                for l in range(LAYERS):
                    for q in range(4):
                        last = nc.tensor.transpose(c.PS[:, l, q * rows:(q + 1) * rows], results[0:rows, l, q * P:(q + 1) * P],
                                                   c.ident[0:rows, 0:rows])
                    last.then_inc(turned.sem, 1)

            @block.vector
            def _(dve):
                ch = c.dve.on(dve)
                dve.wait_ge(small.sem, 32)
                for part in range(2):
                    for l in range(LAYERS):
                        dve.wait_ge(turned.sem, l + 1)
                        for v in range(2):
                            src = c.PS[:, l, 0:4 * rows].rearrange("p (q g v part) -> p q g v part", q=4, v=2, part=2)[:, :, :, v, part]
                            dst, old = (x.rearrange("p (g q) -> p q g", q=4) for x in (c.mod[:, l, v, :], bias[:, l, :] if part == 0 else c.mod[:, l, v, :]))
                            last = ch.mark(nc.vector.tensor_tensor(dst, src, old, ALU.add))
                    ch.wait(last)
                for l in range(LAYERS):
                    for v in range(2):
                        for i, m in enumerate((1, 4, 7)):
                            x = c.mod[:, l, v, m * KT:(m + 1) * KT]
                            ch.mark(nc.vector.scalar_tensor_tensor(x, x, 1.0, gains[:, l, i], ALU.add, ALU.mult))
                        for m in (2, 8):
                            x = c.mod[:, l, v, m * KT:(m + 1) * KT]
                            last = ch.mark(nc.vector.tensor_scalar(x, x, 0.5, None, ALU.mult))
                ch.wait(last)


def first_block(c, dram):
    nc = c.nc
    g_in = c.tally("gain_in")
    with scope(nc) as sb1:
        P1 = sb1("P1", [P, QT, IN_COLS])
        with scope(nc) as sb:
            gain = sb("norm_gain_cols", [P, KT])
            with nc.Block() as block:
                @block.sync
                def _(sp):
                    sp.dma_start(gain[:], dram["norm_gain"]).then_inc(g_in.sem, 16)
                    sp.wait_ge(g_in.sem, 16)
            ring = Ring(c, sb)
            load_rows(c, dram["x"], SEQ, 0, "x", ring, rows_step(ring, dram["w_in"], 0, IN_COLS))
            x = Normed(c, sb, [(0, SEQ)], [gain], [None], "b1")
            project_rows(c, ring, x, dram["w_in"], 0, IN_COLS, list(range(QT)), P1)
        with scope(nc) as sb2:
            QKT = sb2("QKT", [HD, N_ROT, SEQ])
            kcmpT = sb2("kcmpT", [HD, GROUPS, CMP_PAD])
            vbd = sb2("vbd", [P, GROUPS, PER_GROUP * HD])
            gates = sb2("gates", [P, QT, 3 * HEADS])
            tri = sb2("tri_mask", [P, SEQ])
            sc_at = {1: 0, 2: 2 * P, 3: 5 * P}
            scores = sb2("scores", [P, 9 * P])
            rotate(c, P1, QKT, dram)
            compress(c, P1, kcmpT, vbd, dram)
            gate_and_compressed(c, P1, QKT, kcmpT, vbd, gates, dram)
            index_scores(c, P1, QKT, scores, tri, sc_at, dram)
            s_c = sb2("s_c", [P, KT, S_C_COLS], F32R)
            ada_results = sb2("ada_results", [P, LAYERS, 512])
            silu_conditions(c, s_c, dram)
            with scope(nc) as sb:
                ada = Adaptive(c, sb, dram["w_ada"], s_c, 3, ada_results)
                ada.units = 3 * HEADS * QT
                attend_first(c, P1, QKT, scores, sc_at, tri, gates, sb, ada)
            finish_adaptive(c, ada_results, dram)
        with scope(nc) as sb:
            ring = Ring(c, sb)
            x = Operand(c, sb, SEQ, "mixT", made=True)
            hi, lo = x.hi, x.lo
            cols = [OFF[n] + j * P for n in ("q_n", "q_d") for j in range(4)]
            turn_rows(c, [lambda t, a=a: P1[:, t, a:a + P] for a in cols], QT,
                      lambda j, a, e: (hi[:, j, a:e], lo[:, j, a:e]), ring, cols_step(ring, dram["w_out"], ALL_TILES))

            def drain(dve, ch, d, n, ps):
                return nc.vector.tensor_tensor(c.hT[:, d, 0:SEQ], ps, c.hT[:, d, 0:SEQ], ALU.add)

            project_cols(c, ring, x, dram["w_out"], ALL_TILES, [(0, SEQ)], drain)



def ffn_step(ring, w13):
    src = w13.rearrange("(k p) (f n) -> p k f n", p=P, n=P)

    def parts(s, i):
        raw = ring.raw[:, s % 2].rearrange("p (w k n) -> p w k n", w=2, k=KT)
        return [(raw[:, w], src[:, :, w * FT + i, :]) for w in range(2)]
    return parts


def ffn(c, sb, ring, x, w13, w2, gates, spans, tag, after=None):
    nc = c.nc
    hi, lo = x.hi, x.lo
    x.first_use()
    n_tok = spans[-1][1]
    G = 8
    groups = [(f, min(G, FT - f)) for f in range(0, FT, G)]
    hid_hi, hid_lo = sb("hid_hi_" + tag, [P, G, n_tok], F32R), sb("hid_lo_" + tag, [P, G, n_tok], F32R)
    sa, hf = sb("silu_a_" + tag, [P, 2, n_tok]), sb("hid_f_" + tag, [P, 2, n_tok])
    silu_done, h_rounded, h_split = c.tally("f_silu"), c.tally("f_h_rounded"), c.tally("f_h_split")
    u0, hr0, hs0 = silu_done.n, h_rounded.n, h_split.n
    w13_v = w13.rearrange("(k p) (f n) -> p k f n", p=P, n=P)
    w2_v = w2.rearrange("(f p) (q n) -> p f q n", p=P, n=2 * P)
    s0 = c.step
    n_steps = FT + len(groups) * KT // 2
    flat = c.PS[:].rearrange("p b n -> p (b n)")
    raw_up = [ring.raw[:, q].rearrange("p (w k n) -> p w k n", w=2, k=KT) for q in range(2)]
    up = [[t[:, q].rearrange("p (w k n) -> p w k n", w=2, k=KT) for q in range(2)] for t in (ring.hi, ring.lo)]
    raw_dn = [ring.raw[:, q].rearrange("p (f n) -> p f n", f=G) for q in range(2)]
    dn = [[t[:, q].rearrange("p (f n) -> p f n", f=G) for q in range(2)] for t in (ring.hi, ring.lo)]

    def phases():
        s = s0
        for f, nf in groups:
            yield s, nf, f, nf, True
            s += nf
            yield s, KT // 2, f, nf, False
            s += KT // 2

    def two(s, i):
        return [(2 * i + (s + k), i + (s + k) // 2, (s + k) % 2, k) for k in range(2)]

    with nc.Block() as block:
        @block.sync
        def _(sp):
            for s1, n, f0, nf, is_up in phases():
                with sp.Fori(1 if s1 == s0 else 0, n // 2) as i:
                    for s, half, q, k in two(s1, i):
                        sp.wait_ge(ring.split, s + 1)
                        if is_up:
                            for w in range(2):
                                sp.dma_start(raw_up[q][:, w], w13_v[:, :, 2 * i + (w * FT + f0 + k), :]).then_inc(ring.loaded[q], 16)
                        else:
                            for h in range(2):
                                fs = slice(h * nf // 2, (h + 1) * nf // 2)
                                sp.dma_start(raw_dn[q][:, fs], w2_v[:, f0 + h * nf // 2:f0 + (h + 1) * nf // 2, 2 * i + k, :]
                                             ).then_inc(ring.loaded[q], 16)
            if after:
                ring.load_ahead(sp, s0 + n_steps, after)

        @block.tensor
        def _(pe):
            def products_of(i, k):
                q = (s0 + i) % 2
                pe.wait_ge(ring.split, s0 + i + 3)
                for w in range(2):
                    whi, wlo = up[0][q][:, w, k, :], up[1][q][:, w, k, :]
                    for wt, xt, first, end in ((whi, hi, k == 0, False), (whi, lo, False, False), (wlo, hi, False, k == KT - 1)):
                        for m, (a, e) in enumerate(spans):
                            last = nc.tensor.matmul(c.PS[:, 4 * q + 2 * w + m, 0:e - a], wt, xt[:, k, a:e], start=first, stop=end)
                return last

            x.tensor(pe)
            opening(x, pe, products_of, lambda i, last: last.then_inc(ring.used, 1))
            for s1, n, f0, nf, is_up in phases():
                if not is_up:
                    pe.wait_ge(h_split.sem, hs0 + f0 + nf - 1)
                with pe.Fori(1 if s1 == s0 else 0, n // 2) as i:
                    for s, half, q, k in two(s1, i):
                        pe.wait_ge(ring.split, s + 3)
                        pe.wait_ge(ring.drained, s + 1)
                        for w in range(2):
                            n_k = KT if is_up else nf
                            for kk in range(n_k):
                                if not is_up and k == 0 and w == 0 and kk == nf - 1:
                                    pe.wait_ge(h_split.sem, hs0 + f0 + nf)
                                if is_up:
                                    whi, wlo = up[0][q][:, w, kk, :], up[1][q][:, w, kk, :]
                                    xhi, xlo = hi[:, kk], lo[:, kk]
                                else:
                                    whi, wlo = dn[0][q][:, kk, w * P:(w + 1) * P], dn[1][q][:, kk, w * P:(w + 1) * P]
                                    xhi, xlo = hid_hi[:, kk], hid_lo[:, kk]
                                for wt, xt, first, end in ((whi, xhi, kk == 0, False), (whi, xlo, False, False),
                                                           (wlo, xhi, False, kk == n_k - 1)):
                                    for m, (a, e) in enumerate(spans):
                                        last = nc.tensor.matmul(c.PS[:, 4 * q + 2 * w + m, 0:e - a], wt, xt[:, a:e],
                                                                start=first, stop=end)
                        last.then_inc(ring.used, 1)

        def res(q, w):
            return flat[:, (4 * q + 2 * w) * 512:(4 * q + 2 * w) * 512 + n_tok]

        def round_next(act, s, half, q):
            act.wait_ge(ring.loaded[q], half * 32 + 32)
            act.wait_ge(ring.used, s + 1)
            nc.scalar.activation(ring.hi[:, q, :], ring.raw[:, q, :], ACT.Copy).then_inc(ring.rounded, 1)

        @block.scalar
        def _(act):
            def body(s1, f0, is_up, i, more, opened=False):
                for s, half, q, k in two(s1, i):
                    if (k == 0 and not opened) or (k == 1 and more):
                        round_next(act, s + 1, i + (s1 + k + 1) // 2, 1 - q)
                    if is_up:
                        act.wait_ge(ring.used, s + 3)
                        act.wait_ge(ring.drained, s + 1)
                        nc.scalar.activation(sa[:, q, :], res(q, 0), ACT.Silu).then_inc(silu_done.sem, 1)
                        act.wait_ge(ring.drained, s + 3)
                        nc.scalar.activation(hid_hi[:, 2 * i + k, :], hf[:, q, :], ACT.Copy).then_inc(h_rounded.sem, 1)

            x.scalar(act, ring.round_second(act, s0))
            body(s0, 0, True, 0, True, True)
            for s1, n, f0, nf, is_up in phases():
                if after or s1 + n < s0 + n_steps:
                    with act.Fori(1 if s1 == s0 else 0, n // 2) as i:
                        body(s1, f0, is_up, i, True)
                else:
                    for i in range(n // 2):
                        body(s1, f0, is_up, i, i < n // 2 - 1)

        @block.vector
        def _(dve):
            def rest_next(s, half, q):
                dve.wait_ge(ring.rounded, s + 1)
                nc.vector.tensor_tensor(ring.lo[:, q, :], ring.raw[:, q, :], ring.hi[:, q, :].bitcast(F32),
                                        ALU.subtract).then_inc(ring.split, 1)

            def body(s1, f0, is_up, i, more, opened=False):
                for s, half, q, k in two(s1, i):
                    if (k == 0 and not opened) or (k == 1 and more):
                        rest_next(s + 1, 0, 1 - q)
                    if is_up:
                        u = 2 * i + (f0 + k)
                        dve.wait_ge(silu_done.sem, u + (u0 + 1))
                        nc.vector.tensor_tensor(hf[:, q, :], res(q, 1), sa[:, q, :], ALU.mult).then_inc(ring.drained, 1)
                        dve.wait_ge(h_rounded.sem, u + (hr0 + 1))
                        nc.vector.tensor_tensor(hid_lo[:, 2 * i + k, :], hf[:, q, :], hid_hi[:, 2 * i + k, :].bitcast(F32),
                                                ALU.subtract).then_inc(h_split.sem, 1)
                    else:
                        dve.wait_ge(ring.used, s + 3)
                        for w in range(2):
                            for (a, e), gate in zip(spans, gates):
                                d = 4 * i + (2 * k + w)
                                last = nc.vector.scalar_tensor_tensor(c.hT[:, d, a:e], res(q, w)[:, a:e], gate[:, bass.ds(d, 1)],
                                                                      c.hT[:, d, a:e], ALU.mult, ALU.add)
                        last.then_inc(ring.drained, 1)

            x.vector(dve, c.dve.on(dve), ring.rest_second(dve, s0))
            body(s0, 0, True, 0, True, True)
            for s1, n, f0, nf, is_up in phases():
                if after or s1 + n < s0 + n_steps:
                    with dve.Fori(1 if s1 == s0 else 0, n // 2) as i:
                        body(s1, f0, is_up, i, True)
                else:
                    for i in range(n // 2):
                        body(s1, f0, is_up, i, i < n // 2 - 1)
    c.step += n_steps
    ring.ahead = after is not None
    for t in (silu_done, h_rounded, h_split):
        t.n += FT


PAD = 8
ZL = PAD + SEQ + 2 * PAD + CTX + PAD
Z_AT = [PAD, PAD + SEQ + 2 * PAD]


class Loads:

    def __init__(self, c, name, pairs):
        self.t, self.pairs = c.tally(name), pairs
        self.t.n += 16 * len(pairs)
        self.n = self.t.n

    def issue(self, sp):
        for dst, src in self.pairs:
            sp.dma_start(dst, src).then_inc(self.t.sem, 16)

    def wait(self, eng):
        eng.wait_ge(self.t.sem, self.n)


KR_AT = OFF_KR - QK_NOPE


def kv_tiles(dram, l):
    return [(OFF_KV, P), (KR_AT, QKW), (0, QKW, dram["w_kr_swapped"][l])]


REST_TILES = [(OFF_Q, 96), (OFF_Q + 96, 96), (OFF_F, P), (OFF_F + P, P), (OFF_P, P), (OFF_P + P, P)]
ALL_TILES = [(d * P, P) for d in range(KT)]


def mix_layer(c, ring, l, dram, after):
    nc = c.nc
    last = l == LAYERS - 1
    spans = SPANS[:1] if last else SPANS
    n_out = spans[-1][1]
    n_tt = n_out // P
    mod = lambda v, m: c.mod[:, l, v, m * KT:(m + 1) * KT]
    with scope(nc) as sbm:
        mixf = sbm("mixf", [P, KT, n_out])
        with scope(nc) as sbo:
            fT = sbo("fT", [P, 2, n_out])
            cqT = sbo("cqT", [96, 2, n_out])
            ckvT = sbo("ckvT", [KV_RANK, 1, TOK])
            krT = sbo("krT", [QKW, 2, TOK])
            Z = sbo("pool_z", [P, 2, ZL])
            rows = sbo("sgu_rows", [P, TT, 2 * GW])
            with scope(nc) as sbx:
                x = Normed(c, sbx, SPANS, [mod(0, 4), mod(1, 4)], [mod(0, 3), mod(1, 3)], f"m{l}")
                w = dram["w_in_2"][l]

                kv = kv_tiles(dram, l)

                def drain_in(dve, ch, tile, n, ps):
                    a, e = SPANS[n]
                    if tile == 0:
                        if n == 0:
                            ch.link(nc.vector.memset(Z[:], 0.0))
                        return nc.vector.tensor_copy(ckvT[:, 0, a:e], ps)
                    if tile < len(kv):
                        return nc.vector.tensor_copy(krT[QK_NOPE:QKW, tile - 1, a:e], ps[QK_NOPE:QKW])
                    tile -= len(kv)
                    if tile < 2:
                        return nc.vector.tensor_copy(cqT[:, tile, a:e], ps)
                    if tile < 4:
                        return nc.vector.tensor_copy(fT[:, tile - 2, a:e], ps)
                    return nc.vector.tensor_copy(Z[:, tile - 4, Z_AT[n]:Z_AT[n] + e - a], ps)

                project_cols(c, ring, x, w, kv + REST_TILES, SPANS, drain_in, rows_step(ring, w, OFF_G, 2 * GW),
                             len(kv) if last else None)
                project_rows(c, ring, x, w, OFF_G, 2 * GW, list(range(n_tt)), rows, cols_step(ring, dram["w_out_2"][l], ALL_TILES),
                             RankNorms(c, sbx, x, cqT, ckvT, spans, dram["g_q"][l], dram["g_kv"][l]))
            gt = Gating(c, n_tt, rows, mixf)
            attention_mixer(c, l, spans, cqT, ckvT, krT, mixf, dram, gt)
            gt.mixing_room(sbo, dram["w_sgu_t"][l], dram["b_sgu_t"][l])
            with scope(nc) as sb:
                ft, pl = Fourier(c, sb, l, spans, fT, mixf, dram), Pooling(c, sb, l, spans, Z, mixf, dram)
                fourier_and_pooling(c, ft, pl, gt.loads)
            gt.finish()
        x = Split(c, sbm, mixf, n_out, f"mix{l}")

        def drain(dve, ch, d, n, ps):
            a, e = spans[n]
            return nc.vector.scalar_tensor_tensor(c.hT[:, d, a:e], ps, mod(n, 5)[:, d:d + 1], c.hT[:, d, a:e], ALU.mult, ALU.add)

        project_cols(c, ring, x, dram["w_out_2"][l], ALL_TILES, spans, drain, after)


class RankNorms:

    def __init__(self, c, sb, x, cqT, ckvT, spans, g_q, g_kv):
        self.c = c
        gains = sb("g_q", [96, 2]), sb("g_kv", [KV_RANK, 1])
        self.loads = Loads(c, "rn_in", [(gains[0][:], g_q), (gains[1][:], g_kv)])
        self.jobs = [(96, cqT, spans, Q_RANK, gains[0], x.sq[0:96, 0:2], x.sq[0:96, 3], (2, 3)),
                     (KV_RANK, ckvT, SPANS, KV_RANK, gains[1], x.sq[0:KV_RANK, 2:3], x.inv[0:KV_RANK], (6, 7))]
        self.squared, self.summed, self.rooted = c.tally("rn_squared"), c.tally("rn_summed"), c.tally("rn_rooted")
        self.b = {t: t.n for t in (self.squared, self.summed, self.rooted)}
        for t in self.b:
            t.n += 2

    def squares(self, act):
        for rows, y, spans, rank, gain, sq, inv, banks in self.jobs:
            n = spans[-1][1]
            self.c.nc.scalar.activation(sq[:, :, 0:n], y[:, :, 0:n], ACT.Square).then_inc(self.squared.sem, 1)

    def roots(self, act):
        act.wait_ge(self.summed.sem, self.b[self.summed] + 2)
        for rows, y, spans, rank, gain, sq, inv, banks in self.jobs:
            for (a, e), bank in zip(spans, banks):
                last = self.c.nc.scalar.activation(inv[:, a:e], self.c.PS[0:rows, bank, 0:e - a], ACT.Sqrt, bias=self.c.eps[0:rows],
                                                   scale=1.0 / rank)
            last.then_inc(self.rooted.sem, 1)

    def tensor(self, pe, i):
        if i > 0:
            return
        for m, (rows, y, spans, rank, gain, sq, inv, banks) in enumerate(self.jobs):
            pe.wait_ge(self.squared.sem, self.b[self.squared] + m + 1)
            for (a, e), bank in zip(spans, banks):
                for j in range(sq.shape[1]):
                    last = self.c.nc.tensor.matmul(self.c.PS[0:rows, bank, 0:e - a], self.c.ones1[0:rows, 0:rows], sq[:, j, a:e],
                                                   start=(j == 0), stop=(j == sq.shape[1] - 1))
            last.then_inc(self.summed.sem, 1)

    def vector(self, dve, ch, i, n_steps):
        for m, (rows, y, spans, rank, gain, sq, inv, banks) in enumerate(self.jobs):
            if i != max(1, n_steps - 2 + m):
                continue
            n = spans[-1][1]
            self.loads.wait(dve)
            dve.wait_ge(self.rooted.sem, self.b[self.rooted] + m + 1)
            ch.link(self.c.nc.vector.reciprocal(inv[:, 0:n], inv[:, 0:n]))
            for j in range(y.shape[1]):
                last = ch.mark(self.c.nc.vector.scalar_tensor_tensor(y[:, j, 0:n], y[:, j, 0:n], gain[:, j:j + 1], inv[:, 0:n],
                                                                     ALU.mult, ALU.mult))
            ch.wait(last)


def attention_mixer(c, l, spans, cqT, ckvT, krT, mixf, dram, gt):
    nc = c.nc
    n_out = spans[-1][1]
    with scope(nc) as sb:
        qT, kT = sb("qT", [QKW, MH, n_out]), sb("kT", [QKW, MH, TOK])
        V = sb("v2", [P, TT, MH * V_HD])
        att = sb("att", [P, n_out // P, MH * V_HD])
        made, taken = c.tally("mla_made"), c.tally("mla_taken")
        m0, t0 = made.n, taken.n
        items = []
        for h in range(MH):
            for n, (a, e) in enumerate(spans):
                items.append(("q", h, n, a, e))
                if n == 0:
                    items.append(("qs", h, n, a, e))
            for n, (a, e) in enumerate(SPANS):
                items.append(("k", h, n, a, e))
        for t in range(TT):
            items.append(("v", 0, t, t * P, (t + 1) * P))
        gt_at = [len(items) // 2, len(items) - 1]
        with scope(nc) as tmp:
            w_uq, w_uqs = tmp("w_uq", [96, 2, MH * QKW]), tmp("w_uqs", [96, 2, MH * QKW])
            w_ukv = tmp("w_ukv", [KV_RANK, MH, 2, 64])
            cosT, sinT = tmp("rope_cos", [QKW, SEQ]), tmp("rope_sin", [QKW, SEQ])
            gt.norm_room(tmp, dram["g_sgu_rows"][l])
            loads = Loads(c, "mla_in", [(w_uq[:], dram["w_uq"][l].rearrange("(j p) n -> p j n", p=96)),
                                        (w_uqs[:], dram["w_uq_swapped"][l].rearrange("(j p) n -> p j n", p=96)),
                                        (w_ukv[:], dram["w_ukv"][l].rearrange("p (h t n) -> p h t n", h=MH, t=2)),
                                        (cosT[:], dram["rope_cos"]), (sinT[:], dram["rope_sin"])])
            A, B = tmp("mla_a", [QKW, SEQ]), tmp("mla_b", [QKW, SEQ])
            kr = tmp("mla_kr", [QKW, TOK])
            with nc.Block() as block:
                @block.sync
                def _(sp):
                    loads.issue(sp)
                    gt.gain_in.issue(sp)

                @block.tensor
                def _(pe):
                    loads.wait(pe)
                    for i, (what, h, n, a, e) in enumerate(items):
                        if i >= 6:
                            pe.wait_ge(taken.sem, t0 + i - 5)
                        bank = c.PS[:, i % 6, :]
                        if what in ("q", "qs"):
                            wt = w_uq if what == "q" else w_uqs
                            for j in range(2):
                                last = nc.tensor.matmul(bank[0:QKW, 0:e - a], wt[:, j, h * QKW:(h + 1) * QKW], cqT[:, j, a:e],
                                                        start=(j == 0), stop=(j == 1))
                        elif what == "k":
                            last = nc.tensor.matmul(bank[0:QK_NOPE, 0:e - a], w_ukv[:, h, 0, :], ckvT[:, 0, a:e], start=True, stop=True)
                        else:
                            last = nc.tensor.matmul(bank[:, 0:MH * V_HD], ckvT[:, 0, a:e], w_ukv[:, :, 1, :], start=True, stop=True)
                        last.then_inc(made.sem, 1)

                @block.scalar
                def _(act):
                    gt.scalar(act)

                @block.vector
                def _(dve):
                    ch = c.dve.on(dve)
                    rope = slice(QK_NOPE, QKW)
                    loads.wait(dve)
                    ch.mark(nc.vector.tensor_tensor(A[rope], krT[rope, 0, 0:SEQ], cosT[rope], ALU.mult))
                    ch.mark(nc.vector.tensor_copy(kr[rope, SEQ:TOK], krT[rope, 0, SEQ:TOK]))
                    ch.link(nc.vector.tensor_tensor(B[rope], krT[rope, 1, 0:SEQ], sinT[rope], ALU.mult))
                    ch.link(nc.vector.tensor_tensor(kr[rope, 0:SEQ], A[rope], B[rope], ALU.add))
                    for i, (what, h, n, a, e) in enumerate(items):
                        bank = c.PS[:, i % 6, :]
                        dve.wait_ge(made.sem, m0 + i + 1)
                        if what == "q" and n == 0:
                            nc.vector.tensor_tensor(A[:], bank[0:QKW, 0:SEQ], cosT[:], ALU.mult).then_inc(taken.sem, 1)
                            dve.wait_ge(taken.sem, t0 + i + 1)
                        elif what == "qs":
                            nc.vector.tensor_tensor(B[:], bank[0:QKW, 0:SEQ], sinT[:], ALU.mult).then_inc(taken.sem, 1)
                            dve.wait_ge(taken.sem, t0 + i + 1)
                            ch.link(nc.vector.tensor_tensor(qT[:, h, 0:SEQ], A[:], B[:], ALU.add))
                        elif what == "q":
                            nc.vector.tensor_copy(qT[:, h, a:e], bank[0:QKW, 0:e - a]).then_inc(taken.sem, 1)
                        elif what == "k":
                            nc.vector.tensor_copy(kT[0:QK_NOPE, h, a:e], bank[0:QK_NOPE, 0:e - a]).then_inc(taken.sem, 1)
                            nc.vector.tensor_copy(kT[rope, h, a:e], kr[rope, a:e])
                        else:
                            nc.vector.tensor_copy(V[:, n, :], bank[:, 0:MH * V_HD]).then_inc(taken.sem, 1)
                        if i in gt_at:
                            gt.vector(dve, ch, gt_at.index(i))
        made.n += len(items)
        taken.n += len(items)

        units, groups = [], []
        for t in range(n_out // P):
            kt = list(range(TT)) if t < QT else list(range(QT, TT))
            for h in range(MH):
                units.append(Unit(qT[:, h, t * P:(t + 1) * P], lambda lo, hi, h=h, k0=kt[0] * P: kT[:, h, k0 + lo:k0 + hi],
                                  [V[:, x, h * V_HD:min(h + 2, MH) * V_HD] for x in kt], None, len(groups), h * V_HD, QKW ** -0.5))
            groups.append(t)
        co = sb("mla_co", [P, MH])

        def finish(ch, g, rs, drained):
            ch.link(nc.vector.reciprocal(co[:], rs[:, MH * g:MH * (g + 1)]))
            nc.vector.tensor_tensor(att[:, g, :].rearrange("p (h d) -> p h d", h=MH),
                                    c.PS[:, 7, 0:MH * V_HD].rearrange("p (h d) -> p h d", h=MH),
                                    co[:, :, None].to_broadcast([P, MH, V_HD]), ALU.mult).then_inc(drained.sem, 1)

        attend(c, sb, f"m{l}", units, [0, 2], [4, 5, 6], [7], finish)
        turn_rows(c, [lambda t, j=j: att[:, t, j * P:(j + 1) * P] for j in range(2)], n_out // P,
                  lambda j, a, e: (mixf[:, 2 + j, a:e],))


class Fourier:

    def __init__(self, c, sb, l, spans, fT, mixf, dram):
        self.c, self.spans, self.fT, self.mixf = c, spans, fT, mixf
        self.head, self.taken, self.seq, self.out, self.fin = (c.tally("ft_" + x) for x in ("head", "taken", "seq", "seq_taken", "out"))
        self.CS = sb("dft_head", [P, 2 * P])
        self.CL, self.SL = sb("dft_cos", [P, QT, SEQ]), sb("dft_nsin", [P, QT, SEQ])
        self.wf = sb("w_fnet", [P, 2, P])
        self.AB = sb("dft_ab", [P, spans[-1][1] // P, 2, 2 * P])
        self.F = sb("dft_f", [P, 2, spans[-1][1]])
        self.head_in = Loads(c, "ft_head_in", [(self.CS[:], dram["dft_head"])])
        self.seq_in = Loads(c, "ft_seq_in", [(self.CL[:], dram["dft_cos"]), (self.SL[:], dram["dft_nsin"]), (self.wf[:], dram["w_fnet"][l])])
        self.head_items = [(t, j) for t in range(spans[-1][1] // P) for j in range(2)]
        self.seq_items = [(j, n) for j in range(2) for n in range(len(spans))]
        counts = ((self.head, len(self.head_items)), (self.taken, len(self.head_items)), (self.seq, len(self.seq_items)),
                  (self.out, len(self.seq_items)), (self.fin, len(self.seq_items)))
        self.b = {t: t.n for t, _ in counts}
        for t, d in counts:
            t.n += d

    def tensor(self, pe):
        nc, c, b = self.c.nc, self.c, self.b
        self.head_in.wait(pe)
        for i, (t, j) in enumerate(self.head_items):
            if i >= 4:
                pe.wait_ge(self.taken.sem, b[self.taken] + i - 3)
            nc.tensor.matmul(c.PS[:, i % 4, 0:2 * P], self.fT[:, j, t * P:(t + 1) * P], self.CS[:], start=True, stop=True
                             ).then_inc(self.head.sem, 1)
        pe.wait_ge(self.taken.sem, b[self.taken] + len(self.head_items))
        self.seq_in.wait(pe)
        for i, (j, n) in enumerate(self.seq_items):
            a, e = self.spans[n]
            step = SEQ // (e - a)
            k0, k1 = a // P, e // P
            for t in range(k0, k1):
                for s, M in enumerate((self.CL, self.SL)):
                    last = nc.tensor.matmul(c.PS[:, 4 + i, 0:e - a], self.AB[:, t, j, s * P:(s + 1) * P],
                                            M[:, t - k0, 0:SEQ:step], start=(t == k0 and s == 0), stop=(t == k1 - 1 and s == 1))
            last.then_inc(self.seq.sem, 1)
        for i, (j, n) in enumerate(self.seq_items):
            a, e = self.spans[n]
            pe.wait_ge(self.out.sem, b[self.out] + i + 1)
            nc.tensor.matmul(c.PS[:, i, 0:e - a], self.wf[:, j, :], self.F[:, j, a:e], start=True, stop=True).then_inc(self.fin.sem, 1)

    def scalar(self, act):
        for i, (j, n) in enumerate(self.seq_items):
            a, e = self.spans[n]
            act.wait_ge(self.seq.sem, self.b[self.seq] + i + 1)
            self.c.nc.scalar.activation(self.F[:, j, a:e], self.c.PS[:, 4 + i, 0:e - a], ACT.Copy, scale=((e - a) * 64) ** -0.5
                                        ).then_inc(self.out.sem, 1)

    def vector_heads(self, dve):
        for i, (t, j) in enumerate(self.head_items):
            dve.wait_ge(self.head.sem, self.b[self.head] + i + 1)
            self.c.nc.vector.tensor_copy(self.AB[:, t, j, :], self.c.PS[:, i % 4, 0:2 * P]).then_inc(self.taken.sem, 1)

    def vector_out(self, dve):
        for i, (j, n) in enumerate(self.seq_items):
            a, e = self.spans[n]
            dve.wait_ge(self.fin.sem, self.b[self.fin] + i + 1)
            self.c.nc.vector.tensor_copy(self.mixf[:, j, a:e], self.c.PS[:, i, 0:e - a])


class Pooling:

    def __init__(self, c, sb, l, spans, Z, mixf, dram):
        self.c, self.spans, self.Z, self.mixf = c, spans, Z, mixf
        self.pooled, self.fin = c.tally("pl_pooled"), c.tally("pl_out")
        self.items = [(j, n) for j in range(2) for n in range(len(spans))]
        self.inv = sb("pool_inv", [P, 2, ZL])
        self.wp, self.sp_col = sb("w_pool", [P, 2, P]), sb("s_pool", [P, 2])
        self.S = [sb("pool_s%d" % w, [P, 2 if w < 8 else 1, ZL]) for w in (2, 4, 8, 16)]
        self.loads = Loads(c, "pl_in", [(self.inv[:], dram["pool_inv"]), (self.wp[:], dram["w_pool"][l]), (self.sp_col[:], dram["s_pool"][l])])
        self.b = {t: t.n for t in (self.pooled, self.fin)}
        self.pooled.n += 1
        self.fin.n += len(self.items)

    def vector_sums(self, dve, ch):
        nc = self.c.nc
        Z, R = self.Z, self.S[0]
        for t in self.S:
            n = ch.mark(nc.vector.memset(t[:], 0.0))
        ch.wait(n)
        ch.link(nc.vector.tensor_tensor(self.S[0][:, :, 1:ZL], Z[:, :, 0:ZL - 1], Z[:, :, 1:ZL], ALU.add))
        for i, h in enumerate((1, 2, 4)):
            A, B = self.S[i], self.S[i + 1]
            js = A.shape[1] - B.shape[1]
            ch.link(nc.vector.tensor_tensor(B[:, :, h:ZL - h], A[:, js:, 0:ZL - 2 * h], A[:, js:, 2 * h:ZL], ALU.add))
        self.loads.wait(dve)
        for i, S in enumerate(self.S):
            r, j = slice(64 * (i % 2), 64 * (i % 2) + 64), i // 2
            n = ch.mark(nc.vector.tensor_tensor(R[r, j], S[r, j % S.shape[1]], self.inv[r, j], ALU.mult))
        ch.wait(n)
        nc.vector.tensor_tensor(R[:], R[:], Z[:], ALU.subtract).then_inc(self.pooled.sem, 1)

    def vector_out(self, dve):
        for i, (j, n) in enumerate(self.items):
            a, e = self.spans[n]
            dve.wait_ge(self.fin.sem, self.b[self.fin] + i + 1)
            self.c.nc.vector.tensor_scalar(self.mixf[:, 6 + j, a:e], self.c.PS[:, 4 + i, 0:e - a], self.sp_col[:, j:j + 1], None, ALU.mult)

    def tensor(self, pe):
        self.loads.wait(pe)
        pe.wait_ge(self.pooled.sem, self.b[self.pooled] + 1)
        for i, (j, n) in enumerate(self.items):
            a, e = self.spans[n]
            self.c.nc.tensor.matmul(self.c.PS[:, 4 + i, 0:e - a], self.wp[:, j, :], self.S[0][:, j, Z_AT[n]:Z_AT[n] + e - a],
                                    start=True, stop=True).then_inc(self.fin.sem, 1)


def fourier_and_pooling(c, ft, pl, later):
    with c.nc.Block() as block:
        @block.sync
        def _(sp):
            for loads in (ft.head_in, pl.loads, ft.seq_in, later):
                loads.issue(sp)

        @block.tensor
        def _(pe):
            ft.tensor(pe)
            pl.tensor(pe)

        @block.scalar
        def _(act):
            ft.scalar(act)

        @block.vector
        def _(dve):
            ft.vector_heads(dve)
            pl.vector_sums(dve, c.dve.on(dve))
            ft.vector_out(dve)
            pl.vector_out(dve)


class Gating:

    def __init__(self, c, n_tt, rows, mixf):
        self.c, self.n_tt, self.rows, self.mixf = c, n_tt, rows, mixf
        names = ("gelu", "squared", "rooted", "mixed", "summed", "ready")
        self.gelu, self.squared, self.rooted, self.mixed, self.summed, self.ready = (c.tally("sg_" + x) for x in names)
        counts = ((self.gelu, 1), (self.squared, 1), (self.rooted, 1), (self.mixed, n_tt), (self.summed, 1), (self.ready, 1))
        self.b = {t: t.n for t, _ in counts}
        for t, d in counts:
            t.n += d

    def norm_room(self, sb, g):
        self.gain = sb("sgu_gain", [P, MH, 64])
        self.sq = sb("sgu_sq", [P, self.n_tt, GW])
        self.ss = sb("sgu_ss", [P, self.n_tt * MH])
        self.gain_in = Loads(self.c, "sg_gain_in", [(self.gain[:], g)])

    def mixing_room(self, sb, w_t, b_t):
        self.wsT, self.bs = sb("w_sgu", [P, MH, P]), sb("b_sgu", [P, MH])
        self.loads = Loads(self.c, "sg_in", [(self.wsT[:], w_t), (self.bs[:], b_t)])

    def scalar(self, act):
        nc, b = self.c.nc, self.b
        G = self.rows[:, 0:self.n_tt]
        nc.scalar.activation(G, G, ACT.Gelu_apprx_tanh).then_inc(self.gelu.sem, 1)
        act.wait_ge(self.gelu.sem, b[self.gelu] + 1)
        nc.scalar.activation(self.sq[:], G[:, :, GW:2 * GW], ACT.Square).then_inc(self.squared.sem, 1)
        act.wait_ge(self.summed.sem, b[self.summed] + 1)
        nc.scalar.activation(self.ss[:], self.ss[:], ACT.Sqrt, bias=self.c.eps[:], scale=1.0 / 64).then_inc(self.rooted.sem, 1)

    def vector(self, dve, ch, part):
        nc, b = self.c.nc, self.b
        if part == 0:
            dve.wait_ge(self.squared.sem, b[self.squared] + 1)
            nc.vector.reduce_sum(self.ss[:], self.sq[:].rearrange("p t (h d) -> p (t h) d", h=MH), AX_X).then_inc(self.summed.sem, 1)
            return
        dve.wait_ge(self.rooted.sem, b[self.rooted] + 1)
        self.gain_in.wait(dve)
        ch.link(nc.vector.reciprocal(self.ss[:], self.ss[:]))
        for t in range(self.n_tt):
            v = self.rows[:, t, GW:2 * GW].rearrange("p (h d) -> p h d", h=MH)
            m = ch.mark(nc.vector.tensor_tensor(v, v, self.ss[:, t * MH:(t + 1) * MH, None].to_broadcast([P, MH, 64]), ALU.mult))
        ch.wait(m)
        for t in range(self.n_tt):
            v = self.rows[:, t, GW:2 * GW]
            last = nc.vector.tensor_tensor(v, v, self.gain[:].rearrange("p h d -> p (h d)"), ALU.mult)
        last.then_inc(self.ready.sem, 1)

    def finish(self):
        c, nc, b = self.c, self.c.nc, self.b
        with scope(nc) as sb:
            out = sb("sgu_out", [P, self.n_tt, GW])
            with nc.Block() as block:
                @block.tensor
                def _(pe):
                    self.loads.wait(pe)
                    pe.wait_ge(self.ready.sem, b[self.ready] + 1)
                    for t in range(self.n_tt):
                        for h in range(MH):
                            cols = slice(h * 64, (h + 1) * 64)
                            last = nc.tensor.matmul(c.PS[:, t, cols], self.wsT[:, h, :], self.rows[:, t, GW + h * 64:GW + (h + 1) * 64], start=True, stop=True)
                        last.then_inc(self.mixed.sem, 1)

                @block.vector
                def _(dve):
                    ch = c.dve.on(dve)
                    for t in range(self.n_tt):
                        dve.wait_ge(self.mixed.sem, b[self.mixed] + t + 1)
                        for h in range(MH):
                            cols = slice(h * 64, (h + 1) * 64)
                            m = nc.vector.scalar_tensor_tensor(out[:, t, cols], c.PS[:, t, cols], self.bs[:, h:h + 1],
                                                               self.rows[:, t, cols], ALU.add, ALU.mult)
                    ch.link(m)
            turn_rows(c, [lambda t, j=j: out[:, t, j * P:(j + 1) * P] for j in range(2)], self.n_tt,
                      lambda j, a, e: (self.mixf[:, 4 + j, a:e],))


def finish_output(c, dram, out):
    nc = c.nc
    g_in, stored = c.tally("final_gain_in"), c.tally("stored")
    squared, paired, summed, rooted, scaled, turned = (c.tally("o_" + x) for x in ("squared", "paired", "summed", "rooted", "scaled", "turned"))
    moved = [c.tally("o_moved_even"), c.tally("o_moved_odd")]
    items = [(half, t) for half in range(2) for t in range(QT)]
    with scope(nc) as sb:
        gain = sb("g_final", [P, KT])
        sq = sb("o_sq", [P, 4, SEQ])
        inv = sb("o_inv", [P, SEQ])
        rows = sb("o_rows", [P, QT, D])
        with nc.Block() as block:
            @block.scalar
            def _(act):
                for k in range(KT):
                    if k >= 4:
                        act.wait_ge(summed.sem, k // 2 - 1)
                    nc.scalar.activation(sq[:, k % 4], c.hT[:, k, 0:SEQ], ACT.Square).then_inc(squared.sem, 1)
                act.wait_ge(summed.sem, KT // 2)
                nc.scalar.activation(inv[:], c.PS[:, 0, :], ACT.Sqrt, bias=c.eps[:]).then_inc(rooted.sem, 1)
                for n, (half, t) in enumerate(items):
                    if n % 2 == 0:
                        act.wait_ge(turned.sem, n + 1)
                        nc.scalar.activation(rows[:, t, half * 512:half * 512 + 512], c.PS[:, 1 + n % 4, :], ACT.Copy
                                             ).then_inc(moved[0].sem, 1)

            @block.tensor
            def _(pe):
                for j in range(KT // 2):
                    pe.wait_ge(paired.sem, j + 1)
                    nc.tensor.matmul(c.PS[:, 0, :], c.ones[:], sq[:, 2 * j % 4], start=(j == 0), stop=(j == KT // 2 - 1)
                                     ).then_inc(summed.sem, 1)
                for n, (half, t) in enumerate(items):
                    if n >= 4:
                        pe.wait_ge(moved[n % 2].sem, n // 2 - 1)
                    for j in range(4):
                        pe.wait_ge(scaled.sem, 4 * half + j + 1)
                        last = nc.tensor.transpose(c.PS[:, 1 + n % 4, j * P:(j + 1) * P], c.hT[:, 4 * half + j, t * P:(t + 1) * P], c.ident[:])
                    last.then_inc(turned.sem, 1)

            @block.vector
            def _(dve):
                ch = c.dve.on(dve)
                for j in range(KT // 2):
                    dve.wait_ge(squared.sem, 2 * j + 2)
                    q = 2 * j % 4
                    nc.vector.tensor_tensor(sq[:, q], sq[:, q], sq[:, q + 1], ALU.add).then_inc(paired.sem, 1)
                dve.wait_ge(g_in.sem, 16)
                dve.wait_ge(rooted.sem, 1)
                ch.link(nc.vector.reciprocal(inv[:], inv[:]))

                def scale(k):
                    nc.vector.scalar_tensor_tensor(c.hT[:, k, 0:SEQ], c.hT[:, k, 0:SEQ], gain[:, k:k + 1], inv[:], ALU.mult,
                                                   ALU.mult).then_inc(scaled.sem, 1)

                for k in range(4):
                    scale(k)
                for n, (half, t) in enumerate(items):
                    if half == 0:
                        scale(4 + t)
                    if n % 2 == 1:
                        dve.wait_ge(turned.sem, n + 1)
                        nc.vector.tensor_copy(rows[:, t, half * 512:half * 512 + 512], c.PS[:, 1 + n % 4, :]).then_inc(moved[1].sem, 1)

            @block.sync
            def _(sp):
                sp.dma_start(gain[:], dram["g_final"]).then_inc(g_in.sem, 16)
                for n, (half, t) in enumerate(items):
                    sp.wait_ge(moved[n % 2].sem, n // 2 + 1)
                    sp.dma_start(out[t * P:(t + 1) * P, half * 512:half * 512 + 512], rows[:, t, half * 512:half * 512 + 512]
                                 ).then_inc(stored.sem, 16)
                sp.wait_ge(stored.sem, 16 * len(items))


def second_block(c, dram, out):
    nc = c.nc
    with scope(nc) as sbr:
        ring = Ring(c, sbr)
        load_rows(c, dram["ctx"], CTX, SEQ, "ctx", ring, ffn_step(ring, dram["w13_ffn1"][0]))
        for l in range(LAYERS):
            mod = lambda v, m: c.mod[:, l, v, m * KT:(m + 1) * KT]
            for half in range(2):
                spans = SPANS[:1] if (half and l == LAYERS - 1) else SPANS
                m = 6 * half
                vs = range(len(spans))
                with scope(nc) as sb:
                    x = Normed(c, sb, spans, [mod(v, m + 1) for v in vs], [mod(v, m) for v in vs], f"f{l}{half}")
                    if not half:
                        after = cols_step(ring, dram["w_in_2"][l], kv_tiles(dram, l) + REST_TILES)
                    else:
                        after = ffn_step(ring, dram["w13_ffn1"][l + 1]) if l + 1 < LAYERS else None
                    ffn(c, sb, ring, x, dram[f"w13_ffn{half + 1}"][l], dram[f"w2_ffn{half + 1}"][l],
                        [mod(v, m + 2) for v in vs], spans, f"f{l}{half}", after)
                if not half:
                    mix_layer(c, ring, l, dram, ffn_step(ring, dram["w13_ffn2"][l]))
    finish_output(c, dram, out)


def build(nc, dram, out):
    with ExitStack() as st:
        c = Core(nc, st)
        start(c, dram)
        first_block(c, dram)
        second_block(c, dram, out)



def shape_tables():
    import numpy as np
    f = np.float32

    def half_angles(pos):
        inv = (f(10000.0) ** (-np.arange(HD // 2, dtype=f) / f(HD // 2))).astype(f)
        ang = (pos[:, None] * inv[None, :]).astype(f)
        co, si = np.cos(ang), np.sin(ang)
        return np.concatenate([co, co], 1), np.concatenate([-si, si], 1)

    def tiles(a):
        return a.reshape(-1, P, a.shape[-1]).transpose(1, 0, 2)

    co, si = half_angles(np.arange(SEQ, dtype=f))
    starts = np.arange(N_CMP) * CMP_STRIDE + CMP_BLOCK - 1
    c_co, c_si = half_angles(np.append(starts, 0).astype(f))
    seen = np.append(starts, 10 ** 9)[None, :] <= np.arange(SEQ)[:, None]
    tri = np.zeros((P, SEQ), f)
    tri[:, SEQ - P:] = np.where(np.arange(P)[None, :] <= np.arange(P)[:, None], 0, NEG)

    axis = QK_ROPE // 2
    inv2 = np.power(f(10000.0), -np.arange(0, axis, 2, dtype=f) / f(axis)).astype(f)
    t = np.arange(SEQ)
    cos2, sin2 = np.ones((QKW, SEQ), f), np.zeros((QKW, SEQ), f)
    for i, p in enumerate(((t // 64).astype(f), (t % 64).astype(f))):
        ang = (p[:, None] * inv2).astype(f).T
        r = QK_NOPE + axis * i
        cos2[r:r + 8], cos2[r + 8:r + 16] = np.cos(ang), np.cos(ang)
        sin2[r:r + 8], sin2[r + 8:r + 16] = -np.sin(ang), np.sin(ang)

    k = np.arange(64)
    ang = 2 * np.pi * (np.outer(k, k) % 64) / 64
    head = np.zeros((P, 2 * P))
    for h in range(2):
        head[h * 64:h * 64 + 64, h * 64:h * 64 + 64] = np.cos(ang)
        head[h * 64:h * 64 + 64, P + h * 64:P + h * 64 + 64] = np.sin(ang)
    n = np.arange(SEQ)
    ang = 2 * np.pi * (np.outer(n, n) % SEQ) / SEQ
    pool_inv = np.zeros((P, 2, ZL), f)
    for g, w in enumerate((2, 4, 8, 16)):
        for at, length in zip(Z_AT, (SEQ, CTX)):
            p = np.arange(length)
            lo, hi = np.clip(p - w // 2, 0, length), np.clip(p - w // 2 + w, 0, length)
            pool_inv[(g % 2) * 64:(g % 2) * 64 + 64, g // 2, at:at + length] = (f(1.0) / (hi - lo).astype(f))[None]
    return dict(identity=np.eye(P), cos=tiles(co), sin=tiles(si), cmp_cos=c_co, cmp_sin=c_si,
                cmp_neg=tiles(np.where(seen, 0.0, NEG)), cmp_one=tiles(seen.astype(f)), tri=tri,
                rope_cos=cos2, rope_sin=sin2, dft_head=head, dft_cos=tiles(np.cos(ang)), dft_nsin=tiles(-np.sin(ang)),
                pool_inv=pool_inv)


def laid_out(i):
    import numpy as np

    def cols(a):
        a = a.reshape(a.shape[:-1] + (-1, P))
        return np.moveaxis(a, -1, 0)

    def repeated(a, n=P):
        return np.broadcast_to(a, (n,) + a.shape)

    def diagonal(a):
        out = np.zeros((LAYERS, P, 2, P), a.dtype)
        for h in range(4):
            r = (h % 2) * 64
            out[:, r:r + 64, h // 2, r:r + 64] = a[:, h]
        return out

    swap = np.arange(QK_ROPE).reshape(2, 2, QK_ROPE // 4)[:, ::-1].reshape(-1)
    head_swap = np.concatenate([np.arange(QK_NOPE), QK_NOPE + swap])
    gains = [np.tile(i[n][0], r) for n, r in (("nsa_q_gain", 8), ("dsa_q_gain", 8), ("nsa_ks_gain", 2), ("nsa_kw_gain", 2),
                                              ("dsa_k_gain", 2))]
    out = dict(
        x=i["x"][0], norm_gain=cols(i["norm_gain"][0]), w_in=i["w_in"][0], w_out=i["w_out"][0],
        gain_rows=repeated(np.concatenate(gains).reshape(N_NORMED, HD)), kc_gain=repeated(i["nsa_kc_gain"][0], CMP_PAD),
        conditions=cols(np.stack([i["c_2"][0], i["c_ctx_2"]])).transpose(0, 2, 1), ctx=i["ctx_2"][0],
        w_ada=i["w_ada_2"], b_ada=cols(i["b_ada_2"]),
        layer_gains=cols(np.stack([i["g_ffn1_2"], i["g_mix_2"], i["g_ffn2_2"]], 1)),
        w13_ffn1=i["w13_ffn1_2"], w2_ffn1=i["w2_ffn1_2"], w13_ffn2=i["w13_ffn2_2"], w2_ffn2=i["w2_ffn2_2"],
        w_in_2=i["w_in_2"], w_kr_swapped=i["w_in_2"][:, :, OFF_KR - QK_NOPE + head_swap], w_out_2=i["w_out_2"],
        w_uq=i["w_uq_2"], w_uq_swapped=i["w_uq_2"].reshape(LAYERS, Q_RANK, MH, QKW)[..., head_swap].reshape(i["w_uq_2"].shape),
        w_ukv=i["w_ukv_2"], g_q=i["g_q_2"].reshape(LAYERS, 2, 96).transpose(0, 2, 1), g_kv=i["g_kv_2"][:, :, None],
        w_fnet=diagonal(i["w_fnet_2"]), w_pool=diagonal(i["w_pool_2"]), s_pool=i["s_pool_2"].reshape(LAYERS, 2, P).transpose(0, 2, 1),
        g_sgu_rows=np.stack([repeated(i["g_sgu_2"][l]) for l in range(LAYERS)]), w_sgu_t=i["w_sgu_2"].transpose(0, 3, 1, 2),
        b_sgu_t=i["b_sgu_2"].transpose(0, 2, 1), g_final=cols(i["g_final_2"]),
    )
    for x in "kv":
        out[f"cmp_{x}_w1"] = i[f"cmp_{x}_w1"][0]
        out[f"cmp_{x}_w2"] = i[f"cmp_{x}_w2"][0]
        out[f"cmp_{x}_b1"] = cols(i[f"cmp_{x}_b1"][0])
        out[f"cmp_pe_{x}"] = i[f"cmp_pe_{x}"][0].reshape(CMP_BLOCK // 2, P).T
    return out


def kernel(**inputs):
    import numpy as np
    import concourse.bacc as bacc
    from concourse.bass_utils import run_bass_kernel_spmd as run

    nc = bacc.Bacc("TRN2", target_bir_lowering=False, num_devices=1)
    arrays = {f"in_{n}_dram": np.ascontiguousarray(a, dtype=np.float32) for n, a in shape_tables().items()}
    for n, a in laid_out({n: np.asarray(a) for n, a in inputs.items()}).items():
        arrays[f"in_{n}_dram"] = np.ascontiguousarray(a)
    dram = {n[3:-5]: nc.dram_tensor(n, a.shape, F32, kind="ExternalInput").ap() for n, a in arrays.items()}
    out = nc.dram_tensor("out_0_dram", (SEQ, D), F32, kind="ExternalOutput").ap()
    build(nc, dram, out)
    r = run(nc, [arrays], core_ids=[0])
    return r.results[0]["out_0_dram"].reshape(1, SEQ, D)
```
